# Optimizing a Trainium2 kernel written in Bass

```python
import jax, jax.numpy as jnp
from jax import lax
import numpy as np
import math

D_MODEL = 1024
BATCH = 1
SEQ = 256
DEPTH = 1

HEAD_DIM = 64
N_MOBA_HEADS = 6
N_DIL_HEADS = 6
N_MEM_HEADS = 4
N_MEM = 256
MOBA_BLOCK = 256
MOBA_TOPK = 3
MOBA_QCHUNK = 128
DIL_PATTERNS = ((128, 1), (512, 4), (2048, 16))
DIL_BLOCK = 128
D_FF = 2816
CONV_WIDTH = 3
ROPE_THETA = 10000.0
EPS = 1e-6
N_BRANCHES = 3
MOBA_W = N_MOBA_HEADS * HEAD_DIM
DIL_W = N_DIL_HEADS * HEAD_DIM
MEM_W = N_MEM_HEADS * HEAD_DIM
IN_COLS = 3 * MOBA_W + 3 * DIL_W + MEM_W + N_BRANCHES * D_MODEL


def rmsnorm(x, g):
    x32 = x.astype(jnp.float32)
    y = x32 * lax.rsqrt(jnp.mean(x32 * x32, axis=-1, keepdims=True) + EPS)
    return (y * g.astype(jnp.float32)).astype(x.dtype)

def rope(x, positions):
    half = HEAD_DIM // 2
    inv_freq = ROPE_THETA ** (-jnp.arange(half, dtype=jnp.float32) / half)
    ang = positions.astype(jnp.float32)[..., None] * inv_freq
    cos = jnp.cos(ang)[:, :, None, :]
    sin = jnp.sin(ang)[:, :, None, :]
    x1 = x[..., :half].astype(jnp.float32)
    x2 = x[..., half:].astype(jnp.float32)
    out = jnp.concatenate([x1 * cos - x2 * sin, x1 * sin + x2 * cos], axis=-1)
    return out.astype(x.dtype)

def moba_attention(q, k, v):
    B, S, H, Dh = q.shape
    s_pad = -(-S // MOBA_BLOCK) * MOBA_BLOCK
    pad = s_pad - S
    q, k, v = [jnp.pad(t, ((0, 0), (0, pad), (0, 0), (0, 0))).transpose(0, 2, 1, 3) for t in (q, k, v)]
    nb = s_pad // MOBA_BLOCK
    topk = min(MOBA_TOPK, nb)
    kb = k.reshape(B, H, nb, MOBA_BLOCK, Dh)
    vb = v.reshape(B, H, nb, MOBA_BLOCK, Dh)
    k_mean = jnp.mean(kb.astype(jnp.float32), axis=3)
    scale = Dh ** -0.5
    bi = jnp.arange(B)[:, None, None, None]
    hi = jnp.arange(H)[None, :, None, None]
    blk_ids = jnp.arange(nb)

    def one_chunk(c):
        q0 = c * MOBA_QCHUNK
        qc = lax.dynamic_slice_in_dim(q, q0, MOBA_QCHUNK, axis=2)
        qpos = q0 + jnp.arange(MOBA_QCHUNK)
        own = q0 // MOBA_BLOCK
        gate = jnp.einsum('bhqd,bhnd->bhqn', qc.astype(jnp.float32), k_mean)
        gate = jnp.where(blk_ids < own, gate, -jnp.inf)
        gval, sel = lax.top_k(gate, topk)
        sel_ok = jnp.isfinite(gval)
        k_sel = kb[bi, hi, sel]
        v_sel = vb[bi, hi, sel]
        s_sel = jnp.einsum('bhqd,bhqnjd->bhqnj', qc, k_sel).astype(jnp.float32) * scale
        s_sel = jnp.where(sel_ok[..., None], s_sel, -jnp.inf)
        s_sel = s_sel.reshape(B, H, MOBA_QCHUNK, topk * MOBA_BLOCK)
        k_own = lax.dynamic_slice_in_dim(k, own * MOBA_BLOCK, MOBA_BLOCK, axis=2)
        v_own = lax.dynamic_slice_in_dim(v, own * MOBA_BLOCK, MOBA_BLOCK, axis=2)
        kpos = own * MOBA_BLOCK + jnp.arange(MOBA_BLOCK)
        s_own = jnp.einsum('bhqd,bhjd->bhqj', qc, k_own).astype(jnp.float32) * scale
        s_own = jnp.where(kpos[None, :] <= qpos[:, None], s_own, -jnp.inf)
        p = jax.nn.softmax(jnp.concatenate([s_sel, s_own], axis=-1), axis=-1)
        p_sel = p[..., :topk * MOBA_BLOCK].reshape(B, H, MOBA_QCHUNK, topk, MOBA_BLOCK)
        p_own = p[..., topk * MOBA_BLOCK:]
        o = (jnp.einsum('bhqnj,bhqnjd->bhqd', p_sel.astype(v.dtype), v_sel)
             + jnp.einsum('bhqj,bhjd->bhqd', p_own.astype(v.dtype), v_own))
        return o

    outs = lax.map(one_chunk, jnp.arange(s_pad // MOBA_QCHUNK))
    o = outs.transpose(1, 0, 3, 2, 4).reshape(B, s_pad, H, Dh)
    return o[:, :S]

def dilated_attention(q, k, v):
    B, S, H, Dh = q.shape
    max_dil = max(d for _, d in DIL_PATTERNS)
    unit = max_dil * DIL_BLOCK
    s_pad = -(-S // unit) * unit
    pad = s_pad - S
    q, k, v = [jnp.pad(t, ((0, 0), (0, pad), (0, 0), (0, 0))) for t in (q, k, v)]
    scale = Dh ** -0.5
    outs, lses = [], []
    for window, dil in DIL_PATTERNS:
        span = window // dil
        L = s_pad // dil
        nblk = L // DIL_BLOCK

        def to_sub(t):
            return t.reshape(B, L, dil, H, Dh).transpose(0, 2, 1, 3, 4).reshape(B, dil, nblk, DIL_BLOCK, H, Dh)

        def from_sub(t):
            rest = t.shape[4:]
            t = t.reshape((B, dil, L) + rest)
            t = jnp.moveaxis(t, 1, 2)
            return t.reshape((B, s_pad) + rest)

        def with_prev(t):
            prev = jnp.pad(t[:, :, :-1], ((0, 0), (0, 0), (1, 0), (0, 0), (0, 0), (0, 0)))
            return jnp.concatenate([prev, t], axis=3)

        qs = to_sub(q)
        ks = with_prev(to_sub(k))
        vs = with_prev(to_sub(v))
        s = jnp.einsum('brnqhd,brnkhd->brnhqk', qs, ks).astype(jnp.float32) * scale
        qi = jnp.arange(DIL_BLOCK)[:, None] + DIL_BLOCK
        kj = jnp.arange(2 * DIL_BLOCK)[None, :]
        dist = qi - kj
        band = (dist >= 0) & (dist <= span)
        not_before_start = (jnp.arange(nblk) > 0)[:, None, None] | (kj >= DIL_BLOCK)[None]
        mask = band[None] & not_before_start
        s = jnp.where(mask[None, None, :, None], s, -jnp.inf)
        m = jnp.max(s, axis=-1, keepdims=True)
        p = jnp.exp(s - m)
        den = jnp.sum(p, axis=-1)
        o = jnp.einsum('brnhqk,brnkhd->brnqhd', p.astype(v.dtype), vs)
        o = o / den.transpose(0, 1, 2, 4, 3)[..., None]
        lse = (m[..., 0] + jnp.log(den)).transpose(0, 1, 2, 4, 3)
        outs.append(from_sub(o))
        lses.append(from_sub(lse))
    w = jax.nn.softmax(jnp.stack(lses, axis=0), axis=0)
    o = jnp.einsum('pbsh,pbshd->bshd', w, jnp.stack(outs, axis=0).astype(jnp.float32))
    return o[:, :S].astype(q.dtype)

def memory_attention(q, mem_k, mem_v):
    s = jnp.einsum('bshd,bmhd->bhsm', q, mem_k).astype(jnp.float32) * (HEAD_DIM ** -0.5)
    p = jax.nn.softmax(s, axis=-1)
    return jnp.einsum('bhsm,bmhd->bshd', p.astype(mem_v.dtype), mem_v)

def causal_depthwise_conv(u, w, b):
    S = u.shape[1]
    u_pad = jnp.pad(u, ((0, 0), (CONV_WIDTH - 1, 0), (0, 0)))
    y = b
    for j in range(CONV_WIDTH):
        y = y + w[j] * u_pad[:, j:j + S]
    return y

def first_inputs(seed: int = 0) -> dict:
    key = jax.random.key(seed)
    ks = jax.random.split(key, 24)
    f32 = jnp.float32

    def nrm(k, shape, scale):
        return jax.random.normal(k, shape, f32) * scale

    def gain(k, shape):
        return 1.0 + 0.02 * jax.random.normal(k, shape, f32)

    return {
        "x": nrm(ks[0], (BATCH, SEQ, D_MODEL), 1.0),
        "mem": nrm(ks[1], (BATCH, N_MEM, D_MODEL), 1.0),
        "positions": jnp.broadcast_to(jnp.arange(SEQ, dtype=jnp.int32)[None], (BATCH, SEQ)),
        "mix_norm_g": gain(ks[2], (DEPTH, D_MODEL)),
        "mem_norm_g": gain(ks[3], (DEPTH, D_MODEL)),
        "w_in": nrm(ks[4], (DEPTH, D_MODEL, IN_COLS), D_MODEL ** -0.5),
        "moba_q_norm_g": gain(ks[5], (DEPTH, HEAD_DIM)),
        "moba_k_norm_g": gain(ks[6], (DEPTH, HEAD_DIM)),
        "dil_q_norm_g": gain(ks[7], (DEPTH, HEAD_DIM)),
        "dil_k_norm_g": gain(ks[8], (DEPTH, HEAD_DIM)),
        "mem_q_norm_g": gain(ks[9], (DEPTH, HEAD_DIM)),
        "mem_k_norm_g": gain(ks[10], (DEPTH, HEAD_DIM)),
        "w_mem_kv": nrm(ks[11], (DEPTH, D_MODEL, 2 * MEM_W), D_MODEL ** -0.5),
        "w_branch_moba": nrm(ks[12], (DEPTH, MOBA_W, D_MODEL), MOBA_W ** -0.5),
        "w_branch_dil": nrm(ks[13], (DEPTH, DIL_W, D_MODEL), DIL_W ** -0.5),
        "w_branch_mem": nrm(ks[14], (DEPTH, MEM_W, D_MODEL), MEM_W ** -0.5),
        "w_out": nrm(ks[15], (DEPTH, D_MODEL, D_MODEL), D_MODEL ** -0.5),
        "ffn_norm_g": gain(ks[16], (DEPTH, D_MODEL)),
        "w_ffn_up": nrm(ks[17], (DEPTH, D_MODEL, 2 * D_FF), D_MODEL ** -0.5),
        "ffn_conv_w": nrm(ks[18], (DEPTH, CONV_WIDTH, 2 * D_FF), CONV_WIDTH ** -0.5),
        "ffn_conv_b": nrm(ks[19], (DEPTH, 2 * D_FF), 0.01),
        "w_ffn_down": nrm(ks[20], (DEPTH, D_FF, D_MODEL), D_FF ** -0.5),
    }

def first_block(x, mem, positions, mix_norm_g, mem_norm_g, w_in, moba_q_norm_g, moba_k_norm_g,
              dil_q_norm_g, dil_k_norm_g, mem_q_norm_g, mem_k_norm_g, w_mem_kv,
              w_branch_moba, w_branch_dil, w_branch_mem, w_out, ffn_norm_g,
              w_ffn_up, ffn_conv_w, ffn_conv_b, w_ffn_down):
    B, S, _ = x.shape
    split_at = [int(c) for c in np.cumsum([MOBA_W, MOBA_W, MOBA_W, DIL_W, DIL_W, DIL_W, MEM_W])]
    for l in range(DEPTH):
        h = rmsnorm(x, mix_norm_g[l])
        proj = h @ w_in[l]
        qa, ka, va, qd, kd, vd, qm, graw = jnp.split(proj, split_at, axis=-1)
        heads = lambda t, n: t.reshape(B, S, n, HEAD_DIM)
        qa = rope(rmsnorm(heads(qa, N_MOBA_HEADS), moba_q_norm_g[l]), positions)
        ka = rope(rmsnorm(heads(ka, N_MOBA_HEADS), moba_k_norm_g[l]), positions)
        va = heads(va, N_MOBA_HEADS)
        qd = rope(rmsnorm(heads(qd, N_DIL_HEADS), dil_q_norm_g[l]), positions)
        kd = rope(rmsnorm(heads(kd, N_DIL_HEADS), dil_k_norm_g[l]), positions)
        vd = heads(vd, N_DIL_HEADS)
        qm = rmsnorm(heads(qm, N_MEM_HEADS), mem_q_norm_g[l])
        gates = jax.nn.sigmoid(graw.astype(jnp.float32)).astype(x.dtype).reshape(B, S, N_BRANCHES, D_MODEL)

        mem_n = rmsnorm(mem, mem_norm_g[l])
        mkv = (mem_n @ w_mem_kv[l]).reshape(B, N_MEM, 2, N_MEM_HEADS, HEAD_DIM)
        mk = rmsnorm(mkv[:, :, 0], mem_k_norm_g[l])
        mv = mkv[:, :, 1]

        o_a = moba_attention(qa, ka, va).reshape(B, S, MOBA_W) @ w_branch_moba[l]
        o_d = dilated_attention(qd, kd, vd).reshape(B, S, DIL_W) @ w_branch_dil[l]
        o_m = memory_attention(qm, mk, mv).reshape(B, S, MEM_W) @ w_branch_mem[l]
        merged = gates[:, :, 0] * o_a + gates[:, :, 1] * o_d + gates[:, :, 2] * o_m
        x = x + merged @ w_out[l]

        h2 = rmsnorm(x, ffn_norm_g[l])
        u = causal_depthwise_conv(h2 @ w_ffn_up[l], ffn_conv_w[l], ffn_conv_b[l])
        u_gate, u_val = jnp.split(u, 2, axis=-1)
        x = x + (jax.nn.silu(u_gate) * u_val) @ w_ffn_down[l]
    return x


DEPTH_2 = 2

D_MIX = D_MODEL
ATT_HEADS = 8
ATT_HD = 64
D_ATT = ATT_HEADS * ATT_HD
D_CONV = 256
CONV_GROUPS = 4
CONV_K = 31
D_RNN = 256
RNN_BLOCKS = 4
RNN_BD = D_RNN // RNN_BLOCKS
RNN_CONV_K = 4
RG_C = 8.0
Q_BLOCK = 128

Q0, Q1 = 0, D_ATT
K0, K1 = Q1, Q1 + D_ATT
V0, V1 = K1, K1 + D_ATT
F0, F1 = V1, V1 + ATT_HEADS
C0, C1 = F1, F1 + 2 * D_CONV
R0, R1 = C1, C1 + D_RNN
G0, G1 = R1, R1 + D_RNN
N_IN = G1

PEER_HEADS = 8
N_KEYS = 128
N_EXPERTS = N_KEYS * N_KEYS
D_KEY = 256
D_HALF = D_KEY // 2
TOPK = 16
TOK_CHUNK = 128


def rms_norm(x, g):
    xf = x.astype(jnp.float32)
    y = xf * lax.rsqrt(jnp.mean(xf * xf, axis=-1, keepdims=True) + EPS)
    return (y * g.astype(jnp.float32)).astype(x.dtype)

def layer_norm(x, g, b):
    xf = x.astype(jnp.float32)
    mu = jnp.mean(xf, axis=-1, keepdims=True)
    var = jnp.mean(jnp.square(xf - mu), axis=-1, keepdims=True)
    y = (xf - mu) * lax.rsqrt(var + EPS)
    return (y * g.astype(jnp.float32) + b.astype(jnp.float32)).astype(x.dtype)

def causal_dwconv(x, w, b):
    k = w.shape[0]
    y = lax.conv_general_dilated(
        x, w[:, None, :], window_strides=(1,), padding=[(k - 1, 0)],
        dimension_numbers=("NWC", "WIO", "NWC"), feature_group_count=x.shape[-1])
    return y + b

def forgetting_attention(q, k, v, log_f):
    b, s, h, hd = q.shape
    nb = s // Q_BLOCK
    scale = 1.0 / math.sqrt(hd)
    cum = jnp.cumsum(log_f.astype(jnp.float32), axis=1).transpose(0, 2, 1)
    q = q.transpose(0, 2, 1, 3)
    k = k.transpose(0, 2, 1, 3)
    v = v.transpose(0, 2, 1, 3)
    qb = q.reshape(b, h, nb, Q_BLOCK, hd).transpose(2, 0, 1, 3, 4)
    cb = cum.reshape(b, h, nb, Q_BLOCK).transpose(2, 0, 1, 3)
    kpos = jnp.arange(s)

    def one_block(args):
        qi, ci, blk = args
        qpos = blk * Q_BLOCK + jnp.arange(Q_BLOCK)
        logits = jnp.einsum("bhqd,bhkd->bhqk", qi, k).astype(jnp.float32) * scale
        logits = logits + ci[..., :, None] - cum[:, :, None, :]
        logits = jnp.where(kpos[None, :] <= qpos[:, None], logits, -jnp.inf)
        p = jax.nn.softmax(logits, axis=-1)
        return jnp.einsum("bhqk,bhkd->bhqd", p.astype(v.dtype), v)

    o = lax.map(one_block, (qb, cb, jnp.arange(nb)))
    return o.transpose(1, 0, 3, 2, 4).reshape(b, s, h * hd)

def conformer_conv(u, w_dw, b_dw, ln_g, ln_b):
    a, gate = u[..., :D_CONV], u[..., D_CONV:]
    y = a * jax.nn.sigmoid(gate)
    y = causal_dwconv(y, w_dw, b_dw)
    y = layer_norm(y, ln_g, ln_b)
    return jax.nn.silu(y)

def _lin_combine(c1, c2):
    a1, b1 = c1
    a2, b2 = c2
    return a1 * a2, a2 * b1 + b2

def rglru_block(xr, gate_in, conv_w, conv_b, w_r, b_r, w_i, b_i, lam):
    xr = causal_dwconv(xr, conv_w, conv_b)
    b, s, c = xr.shape
    xh = xr.reshape(b, s, RNN_BLOCKS, RNN_BD)
    r = jax.nn.sigmoid(jnp.einsum("bshi,hij->bshj", xh, w_r).reshape(b, s, c) + b_r)
    i = jax.nn.sigmoid(jnp.einsum("bshi,hij->bshj", xh, w_i).reshape(b, s, c) + b_i)
    log_a = -RG_C * r.astype(jnp.float32) * jax.nn.softplus(-lam.astype(jnp.float32))
    a = jnp.exp(log_a)
    mult = jnp.sqrt(-jnp.expm1(2.0 * log_a))
    bterm = mult * (i * xr).astype(jnp.float32)
    _, hs = lax.associative_scan(_lin_combine, (a, bterm), axis=1)
    return hs.astype(xr.dtype) * jax.nn.gelu(gate_in)

def peer(xn, wq, k1, k2, u_tab, v_tab):
    b, s, d = xn.shape
    t = b * s
    xt = xn.reshape(t, d)
    q = (xt @ wq).reshape(t, PEER_HEADS, D_KEY)
    q1, q2 = q[..., :D_HALF], q[..., D_HALF:]
    s1 = jnp.einsum("thd,hnd->thn", q1, k1).astype(jnp.float32)
    s2 = jnp.einsum("thd,hnd->thn", q2, k2).astype(jnp.float32)
    v1, i1 = lax.top_k(s1, TOPK)
    v2, i2 = lax.top_k(s2, TOPK)
    cand = (v1[..., :, None] + v2[..., None, :]).reshape(t, PEER_HEADS, TOPK * TOPK)
    sv, ci = lax.top_k(cand, TOPK)
    e1 = jnp.take_along_axis(i1, ci // TOPK, axis=-1)
    e2 = jnp.take_along_axis(i2, ci % TOPK, axis=-1)
    nc = t // TOK_CHUNK
    experts = (e1 * N_KEYS + e2).reshape(nc, TOK_CHUNK, PEER_HEADS * TOPK)
    gates = jax.nn.softmax(sv, axis=-1).astype(xn.dtype).reshape(nc, TOK_CHUNK, PEER_HEADS * TOPK)
    xc = xt.reshape(nc, TOK_CHUNK, d)

    def chunk(args):
        xi, ei, gi = args
        hid = jax.nn.gelu(jnp.einsum("td,tkd->tk", xi, u_tab[ei]))
        return jnp.einsum("tk,tkd->td", gi * hid, v_tab[ei])

    out = lax.map(chunk, (xc, experts, gates))
    return out.reshape(b, s, d)

def second_inputs(seed: int = 0) -> dict:
    key = jax.random.key(seed)
    ks = jax.random.split(key, 26)
    L, D = DEPTH_2, D_MODEL
    nrm = jax.random.normal
    u_lr = jax.random.uniform(ks[14], (L, D_RNN), minval=0.9, maxval=0.999)
    p_lr = u_lr ** (1.0 / RG_C)
    lam = jnp.log(p_lr) - jnp.log1p(-p_lr)
    return {
        "x": nrm(ks[0], (BATCH, SEQ, D), jnp.float32),
        "norm1_g": 1.0 + 0.01 * nrm(ks[1], (L, D)),
        "w_in": nrm(ks[2], (L, D, N_IN)) * D ** -0.5,
        "b_forget": jax.random.uniform(ks[3], (L, ATT_HEADS), minval=1.0, maxval=5.0),
        "conv_dw_w": nrm(ks[4], (L, CONV_K, D_CONV)) * CONV_K ** -0.5,
        "conv_dw_b": 0.01 * nrm(ks[5], (L, D_CONV)),
        "conv_ln_g": 1.0 + 0.01 * nrm(ks[6], (L, D_CONV)),
        "conv_ln_b": 0.01 * nrm(ks[7], (L, D_CONV)),
        "rg_conv_w": nrm(ks[8], (L, RNN_CONV_K, D_RNN)) * RNN_CONV_K ** -0.5,
        "rg_conv_b": 0.01 * nrm(ks[9], (L, D_RNN)),
        "rg_w_r": nrm(ks[10], (L, RNN_BLOCKS, RNN_BD, RNN_BD)) * RNN_BD ** -0.5,
        "rg_b_r": 0.01 * nrm(ks[11], (L, D_RNN)),
        "rg_w_i": nrm(ks[12], (L, RNN_BLOCKS, RNN_BD, RNN_BD)) * RNN_BD ** -0.5,
        "rg_b_i": 0.01 * nrm(ks[13], (L, D_RNN)),
        "rg_lambda": lam,
        "w_out": nrm(ks[15], (L, D_MIX, D)) * D_MIX ** -0.5,
        "norm2_g": 1.0 + 0.01 * nrm(ks[16], (L, D)),
        "peer_wq": nrm(ks[17], (L, D, PEER_HEADS * D_KEY)) * D ** -0.5,
        "peer_k1": nrm(ks[18], (L, PEER_HEADS, N_KEYS, D_HALF)) * D_HALF ** -0.5,
        "peer_k2": nrm(ks[19], (L, PEER_HEADS, N_KEYS, D_HALF)) * D_HALF ** -0.5,
        "peer_u": nrm(ks[20], (L, N_EXPERTS, D)) * D ** -0.5,
        "peer_v": nrm(ks[21], (L, N_EXPERTS, D)) * 0.5 * PEER_HEADS ** -0.5,
        "final_g": 1.0 + 0.01 * nrm(ks[22], (D,)),
    }

def second_block(x, norm1_g, w_in, b_forget, conv_dw_w, conv_dw_b, conv_ln_g, conv_ln_b,
              rg_conv_w, rg_conv_b, rg_w_r, rg_b_r, rg_w_i, rg_b_i, rg_lambda, w_out,
              norm2_g, peer_wq, peer_k1, peer_k2, peer_u, peer_v, final_g):
    b, s, _ = x.shape
    for l in range(DEPTH_2):
        h = rms_norm(x, norm1_g[l])
        proj = h @ w_in[l]
        q = proj[..., Q0:Q1].reshape(b, s, ATT_HEADS, ATT_HD)
        k = proj[..., K0:K1].reshape(b, s, ATT_HEADS, ATT_HD)
        v = proj[..., V0:V1].reshape(b, s, ATT_HEADS, ATT_HD)
        log_f = jax.nn.log_sigmoid((proj[..., F0:F1] + b_forget[l]).astype(jnp.float32))
        y_att = forgetting_attention(q, k, v, log_f)
        y_conv = conformer_conv(proj[..., C0:C1], conv_dw_w[l], conv_dw_b[l],
                                conv_ln_g[l], conv_ln_b[l])
        y_rnn = rglru_block(proj[..., R0:R1], proj[..., G0:G1], rg_conv_w[l], rg_conv_b[l],
                            rg_w_r[l], rg_b_r[l], rg_w_i[l], rg_b_i[l], rg_lambda[l])
        mixed = jnp.concatenate([y_att, y_conv.astype(x.dtype), y_rnn.astype(x.dtype)], axis=-1)
        x = x + mixed @ w_out[l]
        h2 = rms_norm(x, norm2_g[l])
        x = x + peer(h2, peer_wq[l], peer_k1[l], peer_k2[l], peer_u[l], peer_v[l])
    return rms_norm(x, final_g)


def setup_inputs(seed=0):
    out = dict(first_inputs(seed))
    for name, value in second_inputs(seed + 1).items():
        if name != "x":
            out[name + "_2"] = value
    return out


def reference(
    x, mem, positions, mix_norm_g, mem_norm_g, w_in, moba_q_norm_g, moba_k_norm_g, dil_q_norm_g,
    dil_k_norm_g, mem_q_norm_g, mem_k_norm_g, w_mem_kv, w_branch_moba, w_branch_dil,
    w_branch_mem, w_out, ffn_norm_g, w_ffn_up, ffn_conv_w, ffn_conv_b, w_ffn_down, norm1_g_2,
    w_in_2, b_forget_2, conv_dw_w_2, conv_dw_b_2, conv_ln_g_2, conv_ln_b_2, rg_conv_w_2,
    rg_conv_b_2, rg_w_r_2, rg_b_r_2, rg_w_i_2, rg_b_i_2, rg_lambda_2, w_out_2, norm2_g_2,
    peer_wq_2, peer_k1_2, peer_k2_2, peer_u_2, peer_v_2, final_g_2,
):
    x = first_block(
        x, mem, positions, mix_norm_g, mem_norm_g, w_in, moba_q_norm_g, moba_k_norm_g,
        dil_q_norm_g, dil_k_norm_g, mem_q_norm_g, mem_k_norm_g, w_mem_kv, w_branch_moba,
        w_branch_dil, w_branch_mem, w_out, ffn_norm_g, w_ffn_up, ffn_conv_w, ffn_conv_b,
        w_ffn_down,
    )
    return second_block(
        x, norm1_g_2, w_in_2, b_forget_2, conv_dw_w_2, conv_dw_b_2, conv_ln_g_2, conv_ln_b_2,
        rg_conv_w_2, rg_conv_b_2, rg_w_r_2, rg_b_r_2, rg_w_i_2, rg_b_i_2, rg_lambda_2, w_out_2,
        norm2_g_2, peer_wq_2, peer_k1_2, peer_k2_2, peer_u_2, peer_v_2, final_g_2,
    )


_drawn_inputs = setup_inputs


def setup_inputs(seed=0):
    import zlib

    import numpy as np

    out = dict(_drawn_inputs(seed))
    spreads = {}
    factors = {'mix_norm_g': 4.765,
     'mem_norm_g': 8.0,
     'moba_q_norm_g': 8.0,
     'moba_k_norm_g': 8.0,
     'dil_q_norm_g': 8.0,
     'dil_k_norm_g': 8.0,
     'mem_q_norm_g': 8.0,
     'mem_k_norm_g': 8.0,
     'ffn_norm_g': 2.737,
     'ffn_conv_b': 4.315,
     'norm1_g_2': 5.037,
     'conv_dw_b_2': 32.623,
     'conv_ln_g_2': 53.928,
     'conv_ln_b_2': 58.96,
     'rg_conv_b_2': 3.269,
     'rg_b_r_2': 39.494,
     'rg_b_i_2': 34.232,
     'norm2_g_2': 39.928,
     'final_g_2': 35.173}
    for name, (base, spread) in spreads.items():
        noise = np.random.default_rng([zlib.crc32(name.encode()), seed]).standard_normal(out[name].shape)
        drawn = base * np.exp(spread * noise) if base else spread * noise
        out[name] = __import__('jax').numpy.asarray(drawn.astype(out[name].dtype))
    for name, factor in factors.items():
        out[name] = (out[name] * factor).astype(out[name].dtype)
    return out
```

```python
from contextlib import ExitStack

import numpy as np

import concourse.bass as bass
from concourse import mybir

ALU = mybir.AluOpType
ACT = mybir.ActivationFunctionType
AX = mybir.AxisListType.X
F32 = mybir.dt.float32
I32 = mybir.dt.int32
U32 = mybir.dt.uint32

P = 128
EPS = 1e-6
TWO_PI = 6.283185307179586
C1 = 6.28125
C2 = 0.0019350051879882812
C3 = TWO_PI - C1 - C2
MAGIC = 12582912.0
NEG = -1e30
SLOT = 4096
NSLOT = 4
ROWS = 15
G = 8

K_ID, K_MC, K_MD, K_CD, K_ONE, K_IO, K_IF, K_SEL, K_END = 0, 128, 640, 1152, 1664, 1792, 1808, 1840, 1850
V_MIX, V_MEM, V_FFN, V_N1, V_CW, V_CB, V_L = 0, 8, 16, 24, 40, 172, 216
L_DW, L_DB, L_G, L_B, L_RW, L_RB, L_BR, L_BI, L_LAM, L_BF, L_END = 0, 62, 64, 66, 68, 76, 78, 80, 82, 84, 85
V_END = V_L + 2 * L_END
B_HEAD, B_N2, B_FIN, B_END = 0, 384, 384 + 2048, 384 + 3072


class Ops:

    def activation(self, *a, **k):
        self.call = lambda e: e.activation(*a, **k)

    def dma_start(self, *a, **k):
        self.call = lambda e: e.dma_start(*a, **k)

    def indirect_dma_start(self, *a, **k):
        self.call = lambda e: e.indirect_dma_start(*a, **k)

    def match_replace(self, *a, **k):
        self.call = lambda e: e.match_replace(*a, **k)

    def matmul(self, *a, **k):
        self.call = lambda e: e.matmul(*a, **k)

    def max(self, *a, **k):
        self.call = lambda e: e.max(*a, **k)

    def max_index(self, *a, **k):
        self.call = lambda e: e.max_index(*a, **k)

    def memset(self, *a, **k):
        self.call = lambda e: e.memset(*a, **k)

    def nop(self, *a, **k):
        self.call = lambda e: e.nop(*a, **k)

    def reciprocal(self, *a, **k):
        self.call = lambda e: e.reciprocal(*a, **k)

    def scalar_tensor_tensor(self, *a, **k):
        self.call = lambda e: e.scalar_tensor_tensor(*a, **k)

    def tensor_copy(self, *a, **k):
        self.call = lambda e: e.tensor_copy(*a, **k)

    def tensor_reduce(self, *a, **k):
        self.call = lambda e: e.tensor_reduce(*a, **k)

    def tensor_scalar(self, *a, **k):
        self.call = lambda e: e.tensor_scalar(*a, **k)

    def tensor_tensor(self, *a, **k):
        self.call = lambda e: e.tensor_tensor(*a, **k)

    def tensor_tensor_reduce(self, *a, **k):
        self.call = lambda e: e.tensor_tensor_reduce(*a, **k)

    def tensor_tensor_scan(self, *a, **k):
        self.call = lambda e: e.tensor_tensor_scan(*a, **k)

    def transpose(self, *a, **k):
        self.call = lambda e: e.transpose(*a, **k)


class Step:

    def __init__(self, queue, fn, after):
        self.queue, self.fn, self.after = queue, fn, after
        self.sem = self.value = None
        self.marked = False


def _flat(steps):
    for s in steps:
        if isinstance(s, (list, tuple)):
            yield from _flat(s)
        elif s is not None:
            yield s


class Queue:

    def __init__(self, sem):
        self.sem, self.steps = sem, []

    def __call__(self, fn, *after):
        after = list(_flat(after))
        for a in after:
            a.marked = True
        ops = Ops()
        fn(ops)
        step = Step(self, ops.call, after)
        self.steps.append(step)
        return step

    def dma(self, landed, fn, *after):
        step = self(fn, *after)
        landed[1] += 16
        step.sem, step.value = landed
        return step

    def number(self):
        n = 0
        for s in self.steps:
            if s.sem is None and s.marked:
                n += 1
                s.value = n

    def emit(self, eng):
        seen = {}
        for s in self.steps:
            for a in s.after:
                sem = a.sem or a.queue.sem
                if seen.get(id(sem), 0) < a.value:
                    eng.wait_ge(sem, a.value)
                    seen[id(sem)] = a.value
            ins = s.fn(eng)
            if s.sem is not None:
                ins.then_inc(s.sem, 16)
            elif s.marked:
                ins.then_inc(self.sem, 1)


class Buf:

    def __init__(self, ap):
        self.ap, self.free = ap, []


def program(nc, T, out):
    ctx = ExitStack()
    with ctx:
        def sb(name, cols, dt=F32):
            return ctx.enter_context(nc.sbuf_tensor(name, [P, cols], dt))

        def sem(name):
            return ctx.enter_context(nc.semaphore(name))

        S, A, V, E, M = (Queue(sem(n)) for n in ("q_sp", "q_act", "q_dve", "q_pe", "q_pool"))

        const = sb("const", K_END)
        vecs = sb("vecs", V_END)
        rows = sb("rows", 384)
        rowg = sb("rowg", 1024)
        posi = sb("posi", 2, I32)
        posf = sb("posf", 2)
        x = sb("x", 2048)
        hT = sb("hT", 2048)
        ring = sb("ring", NSLOT * SLOT)
        kk = sb("kk", 2048)
        rgw = sb("rgw", 512)
        wf = sb("wf", 832)
        arena = sb("arena", 15360)
        mkv = sb("mkv", 1024)
        osb = sb("osb", 2048)
        tmp = sb("tmp", 3072)
        junk = sb("junk", 1024)
        cs = sb("cs", 2 * 128)
        sm = sb("sm", 1024)
        smi = sb("smi", 512, U32)
        eidx = sb("eidx", 256, U32)
        hid = sb("hid", 256)
        wexp = sb("wexp", 256)
        diag = sb("diag", 4 * 128)
        diags, ndiag = [Buf(diag[:, 128 * i:128 * i + 128]) for i in range(4)], [0]
        psum = ctx.enter_context(nc.psum_tensor("psum", [P, 4096], F32))
        bank = [Buf(psum[:, 512 * i:512 * i + 512]) for i in range(8)]
        tmps = [Buf(tmp[:, 512 * i:512 * i + 512]) for i in range(6)]

        ident = const[:, K_ID:K_ID + 128]
        mcau = const[:, K_MC:K_MC + 512].rearrange("p (t k) -> p t k", t=2)
        mdil = const[:, K_MD:K_MD + 512].rearrange("p (t k) -> p t k", t=2)
        cdil = const[:, K_CD:K_CD + 512].rearrange("p (t k) -> p t k", t=2)
        ones = const[:, K_ONE:K_ONE + 128]
        iota = const[:, K_IO:K_IO + 16]
        x3 = x[:, :].rearrange("p (t d) -> p t d", t=2)
        hT3 = hT[:, :].rearrange("p (k t) -> p k t", k=8)
        gates = arena[:, 0:6144].rearrange("p (t b d) -> p t b d", t=2, b=3)
        proj = arena[:, 6144:11264].rearrange("p (t d) -> p t d", t=2)
        qkT = arena[:, 11264:15360].rearrange("p (b t) -> p b t", b=16)
        mkv3 = mkv[:, :].rearrange("p (t d) -> p t d", t=2)
        osb3 = osb[:, :].rearrange("p (t d) -> p t d", t=2)
        kk4 = kk[:, :].rearrange("p (a h n) -> p a h n", a=2, h=8)
        rgw4 = rgw[:, :].rearrange("p (a b n) -> p a b n", a=2, b=2)
        wf3 = wf[:, :].rearrange("p (k n) -> p k n", k=8)

        def landing(name):
            return [sem(name), 0]

        def load(queue, landed, dst, src, *after):
            return queue.dma(landed, lambda e: e.dma_start(dst, src), *after)

        ld_x = load(S, landing("l_x"), x3, T["x"].rearrange("(t p) d -> p t d", p=P))
        ld_c = load(A, landing("l_c"), const[:, :], T["const"])
        ld_v = load(A, landing("l_v"), vecs[:, :], T["vecs"])
        mem3 = osb3
        ld_m = load(A, landing("l_m"), mem3, T["mem"].rearrange("(t p) d -> p t d", p=P))
        ld_p = load(A, landing("l_p"), posi[:, :], T["pos"])
        ld_r = load(A, landing("l_r"), rows[:, :], T["rows"][:, 0:384])
        row_landed = [landing(f"l_g{i}") for i in range(ROWS)]
        l_kk, l_rg, l_wf = landing("l_kk"), landing("l_rg"), landing("l_wf")

        def cols(w, c0, n, kb=8, k0=0, at=0, width=512):
            src = w[k0 * P:(k0 + kb) * P, c0:c0 + n].rearrange("(k p) n -> p k n", p=P)
            return lambda slot: (slot[:, 0:kb * width].rearrange("p (k n) -> p k n", k=kb)[:, :, at:at + n], src)

        slabs = [[cols(T["w_in"], 512 * c, 512)] for c in range(5)]
        slabs += [[cols(T["w_mem_kv"], 0, 512)]]
        slabs += [[cols(T["w_in"], 512 * c, 512)] for c in range(5, 11)]
        slabs += [[cols(T["w_branch_moba"], 0, 1024, 3, width=1024)], [cols(T["w_branch_dil"], 0, 1024, 3, width=1024)],
                  [cols(T["w_branch_mem"], 0, 1024, 2, width=1024)]]
        slabs += [[cols(T["w_out"], 512 * c, 512)] for c in range(2)]
        slabs += [[cols(T["w_ffn_up"], 256 * c, 256), cols(T["w_ffn_up"], 2816 + 256 * c, 256, at=256)] for c in range(11)]
        slabs += [[cols(T["w_ffn_down"], 0, 1024, min(4, 22 - k), k, width=1024)] for k in range(0, 22, 4)]
        for l in range(2):
            w = T["w_in_2"][l]
            slabs += [[cols(w, c, 512)] for c in (0, 512, 1024, 1544, 2056)]
            slabs += [[cols(T["w_out_2"][l], 512 * c, 512)] for c in range(2)]
            slabs += [[cols(T["peer_wq"][l], 512 * c, 512)] for c in range(4)]

        slot_landed = [landing(f"l_s{i}") for i in range(NSLOT)]
        loaded = []
        taken = [0, 0]

        def fetch(after):
            n = len(loaded)
            if n == len(slabs):
                return
            at = n % NSLOT
            slot = ring[:, at * SLOT:(at + 1) * SLOT]
            for part in slabs[n]:
                dst, src = part(slot)
                step = load(S, slot_landed[at], dst, src, after)
            loaded.append(step)

        for _ in range(NSLOT):
            fetch(None)

        def slab():
            n = taken[0]
            taken[0] += 1
            return ring[:, (n % NSLOT) * SLOT:(n % NSLOT + 1) * SLOT], loaded[n]

        def matmuls(dst, pairs, *after):
            for i, (a, b) in enumerate(pairs):
                step = E(lambda e, a=a, b=b, i=i: e.matmul(dst, a, b, start=(i == 0), stop=(i == len(pairs) - 1)),
                         *(after if i == 0 else ()))
            return step

        turn = [0]

        def evac(dst, src, *after):
            turn[0] += 1
            if turn[0] % 2:
                return A(lambda e: e.activation(dst, src, ACT.Copy), *after)
            return V(lambda e: e.tensor_copy(dst, src), *after)

        def transposes(b, srcs, *after):
            for i, src in enumerate(srcs):
                step = E(lambda e, i=i, src=src: e.transpose(b.ap[:, 128 * i:128 * i + 128], src, ident),
                         ld_c, *(list(after) + b.free if i == 0 else ()))
            return step

        def inv_root(ms, y, t, *after):
            s = A(lambda e: e.activation(y, ms, ACT.Ln), *after)
            s = A(lambda e: e.activation(y, y, ACT.Exp, scale=-0.5), s)
            s = V(lambda e: e.tensor_tensor(t, y, y, ALU.mult), s)
            s = V(lambda e: e.tensor_tensor(t, t, ms, ALU.mult), s)
            s = V(lambda e: e.tensor_scalar(t, t, -0.5, 1.5, ALU.mult, ALU.add), s)
            return V(lambda e: e.tensor_tensor(y, y, t, ALU.mult), s)

        def rms(src3, dst3, at, *after):
            ss, y, t = sm[:, at:at + 2], sm[:, at + 2:at + 4], sm[:, at + 4:at + 6]
            s = [A(lambda e, t_=t_: e.activation(dst3[:, t_, :], src3[:, t_, :], ACT.Square, accum_out=sm[:, at + t_:at + t_ + 1]),
                   *after) for t_ in range(2)]
            s = V(lambda e: e.tensor_scalar(ss, ss, 1.0 / 1024, EPS, ALU.mult, ALU.add), s)
            return y, inv_root(ss, y, t, s)

        def turned(src3, dstT, gain, banks, *after):
            done = []
            for n, (t_, half) in enumerate((a, b) for a in range(2) for b in range(2)):
                b = bank[banks[n % len(banks)]]
                s = transposes(b, [src3[:, t_, 128 * (4 * half + i):128 * (4 * half + i) + 128] for i in range(4)], *after)
                dst = dstT[:, 4 * half:4 * half + 4, 128 * t_:128 * t_ + 128]
                src = b.ap[:, :].rearrange("p (k n) -> p k n", k=4)
                if gain is None:
                    s = evac(dst, src, s)
                else:
                    gg = gain[:, 4 * half:4 * half + 4].unsqueeze(2).to_broadcast([P, 4, 128])
                    s = V(lambda e, dst=dst, src=src, gg=gg: e.tensor_tensor(dst, src, gg, ALU.mult), s, ld_v)
                b.free = [s]
                done.append(s)
            return done

        def scaled(dst3, src3, r, *after):
            return [V(lambda e, t_=t_: e.tensor_scalar(dst3[:, t_, :], src3[:, t_, :], r[:, t_:t_ + 1], None, ALU.mult), *after)
                    for t_ in range(2)]

        def token_major(hT_, ready, banks, use):
            slot, here = slab()
            w = slot[:, :].rearrange("p (k n) -> p k n", k=8)
            for t_ in range(2):
                b = bank[banks[t_]]
                s = matmuls(b.ap[:, :], [(hT_[:, k, 128 * t_:128 * t_ + 128], w[:, k, :]) for k in range(8)], here, ready, b.free)
                b.free = [use(t_, b, s)]
            fetch(s)

        def feature_major(hT_, ready, banks, use):
            slot, here = slab()
            w = slot[:, :].rearrange("p (k n) -> p k n", k=8)
            for j in range(2):
                b = bank[banks[j]]
                for i in range(2):
                    c = 128 * (2 * j + i)
                    s = matmuls(b.ap[:, 256 * i:256 * i + 256], [(w[:, k, c:c + 128], hT_[:, k, :]) for k in range(8)],
                                here, ready, b.free if i == 0 else None)
                b.free = [use(j, b, s)]
            fetch(s)

        def attention(units, out3, free_v):
            S_b, T_b, O_b = (0, 6), (2, 3), (4, 5)
            Sm, Eb, Pt = tmps[0:2], tmps[2:4], tmps[4:6]
            for b in tmps:
                b.free = b.free + list(_flat([free_v]))
            den = sm[:, 600:664].rearrange("p (t h) -> p t h", t=2)
            mx = sm[:, 664:668].rearrange("p (a h) -> p a h", a=2)
            groups = []
            for u in units:
                if not groups or groups[-1][0] != u["group"]:
                    groups.append((u["group"], []))
                groups[-1][1].append(u)
                u["o"] = bank[O_b[(len(groups) - 1) % 2]]
                u["first"] = len(groups[-1][1]) == 1
                u["members"] = groups[-1][1]
            done = []

            def scores(i):
                u = units[i]
                t_, nk = u["t"], u["nk"]
                n = S_b[i % 2]
                sm_, e_ = Sm[i % 2], Eb[i % 2]
                s3 = psum[:, 512 * n:512 * n + 1024].rearrange("p (h k) -> p h k", h=2)[:, :, 0:nk]
                d3 = sm_.ap.rearrange("p (h k) -> p h k", h=2)[:, :, 0:nk]
                x3_ = e_.ap.rearrange("p (h k) -> p h k", h=2)[:, :, 0:nk]
                for h in range(2):
                    pairs = [(u["q"](h), u["k"](h))] + ([u["bias"](h)] if u["bias"] else [])
                    s = matmuls(s3[:, h, :], pairs, u["ready"], bank[n + h].free)
                m2 = mx[:, i % 2, :]
                mb = m2.unsqueeze(2).to_broadcast([P, 2, nk])
                src = s3
                if u["mask"] is not None:
                    mk = u["mask"][:, t_, 0:nk].unsqueeze(1).to_broadcast([P, 2, nk])
                    s = V(lambda e: e.tensor_tensor(d3, s3, mk, ALU.add), s, sm_.free)
                    src = d3
                s_m = V(lambda e: e.tensor_reduce(m2, src, AX, ALU.max), s)
                s = V(lambda e: e.tensor_tensor(d3, src, mb, ALU.subtract), s_m, sm_.free)
                bank[n].free = bank[n + 1].free = [s]
                s = A(lambda e: e.activation(x3_, d3, ACT.Exp, scale=0.125), s, e_.free)
                sm_.free = [s]
                u["e"], u["e3"] = s, x3_

            def weights(i):
                u = units[i]
                t_, nk, x3_ = u["t"], u["nk"], u["e3"]
                s = u["e"]
                if u["counts"] is not None:
                    ck = u["counts"][:, t_, 0:nk].unsqueeze(1).to_broadcast([P, 2, nk])
                    s = V(lambda e: e.tensor_tensor(x3_, x3_, ck, ALU.mult), s)
                h0 = u["col"] // 64
                u["den"] = V(lambda e: e.tensor_reduce(den[:, t_, h0:h0 + 2], x3_, AX, ALU.add), s)
                b, pt = bank[T_b[i % 2]], Pt[i % 2]
                nb = nk // 128
                last = transposes(b, [x3_[:, h, 128 * c:128 * c + 128] for h in range(2) for c in range(nb)], s)
                Eb[i % 2].free = [last, u["den"]]
                p_ = pt.ap[:, 0:256 * nb]
                s = A(lambda e: e.activation(p_, b.ap[:, 0:256 * nb], ACT.Copy), last, pt.free)
                b.free = [s]
                u["p"], u["p3"] = s, p_.rearrange("p (h c q) -> p h c q", h=2, c=nb)

            def values(i):
                u = units[i]
                o, nb = u["o"], u["nk"] // 128
                for h in range(2):
                    c0 = u["col"] - u["members"][0]["col"] + 64 * h
                    s = matmuls(o.ap[:, c0:c0 + 64], [(u["p3"][:, h, c, :], u["v"](h, c)) for c in range(nb)],
                                u["p"], o.free if u["first"] and h == 0 else None)
                Pt[i % 2].free = [s]
                if u is u["members"][-1]:
                    t_, n = u["t"], 2 * len(u["members"])
                    c0 = u["members"][0]["col"]
                    dd = den[:, t_, c0 // 64:c0 // 64 + n]
                    r = V(lambda e: e.reciprocal(dd, dd), u["den"])
                    o3 = o.ap[:, 0:64 * n].rearrange("p (h d) -> p h d", h=n)
                    y3 = out3[:, t_, c0:c0 + 64 * n].rearrange("p (h d) -> p h d", h=n)
                    rb = dd.unsqueeze(2).to_broadcast([P, n, 64])
                    r = V(lambda e: e.tensor_tensor(y3, o3, rb, ALU.mult), r, s)
                    o.free = [r]
                    done.append(r)

            for i in range(len(units) + 2):
                if i < len(units):
                    scores(i)
                if 1 <= i <= len(units):
                    weights(i - 1)
                if i >= 2:
                    values(i - 2)
            return done

        def add_to_x(t_, half, b, s):
            d = x3[:, t_, 512 * half:512 * half + 512]
            return V(lambda e: e.tensor_tensor(d, d, b.ap[:, :], ALU.add), s)

        s = V(lambda e: e.tensor_copy(posf[:, :], posi[:, :]), ld_p)
        ang, kf = junk[:, 0:128].rearrange("p (a t f) -> p a t f", a=2, t=2), junk[:, 128:256].rearrange("p (a t f) -> p a t f", a=2, t=2)
        invf = const[:, K_IF:K_IF + 32]
        ss = []
        for t_ in range(2):
            a0 = V(lambda e, t_=t_: e.tensor_scalar(ang[:, 0, t_, :], invf, posf[:, t_:t_ + 1], None, ALU.mult), s, ld_c)
            ss.append(V(lambda e, t_=t_: e.tensor_copy(ang[:, 1, t_, :], ang[:, 0, t_, :]), a0))
        for a in range(2):
            s1 = V(lambda e, a=a: e.tensor_scalar(kf[:, a], ang[:, a], 1.0 / TWO_PI, 0.25 * a, ALU.mult, ALU.add), ss)
            s1 = V(lambda e, a=a: e.tensor_scalar(kf[:, a], kf[:, a], MAGIC, None, ALU.add), s1)
            s1 = V(lambda e, a=a: e.tensor_scalar(kf[:, a], kf[:, a], -MAGIC, None, ALU.add), s1)
            for c in (C1, C2, C3):
                s1 = V(lambda e, a=a, c=c: e.scalar_tensor_tensor(ang[:, a], kf[:, a], -c, ang[:, a], ALU.mult, ALU.add), s1)
            if a:
                s1 = V(lambda e, a=a: e.tensor_scalar(ang[:, a], ang[:, a], TWO_PI / 4, None, ALU.add), s1)
            s1 = V(lambda e, a=a: e.tensor_scalar(ang[:, a], ang[:, a], 3.1415925, -3.1415925, ALU.min, ALU.max), s1)
            s1 = A(lambda e, a=a: e.activation(ang[:, a], ang[:, a], ACT.Sin), s1)
            ss.append(s1)
        cs4 = cs[:, :].rearrange("p (t c f) -> p t c f", t=2, c=4)
        cs_ready = [V(lambda e, c=c: e.tensor_copy(cs4[:, :, c, :], ang[:, 1]), ss) for c in range(2)]
        cs_ready.append(V(lambda e: e.tensor_scalar(cs4[:, :, 2, :], ang[:, 0], -1.0, None, ALU.mult), ss))
        cs_ready.append(V(lambda e: e.tensor_copy(cs4[:, :, 3, :], ang[:, 0]), ss))

        xs = arena[:, 0:2048].rearrange("p (t d) -> p t d", t=2)
        ms_ = arena[:, 2048:4096].rearrange("p (t d) -> p t d", t=2)
        memT = qkT[:, 0:8, :]
        r, s = rms(x3, xs, 0, ld_x, cs_ready)
        s = scaled(xs, x3, r, s)
        h_ready = turned(xs, hT3, vecs[:, V_MIX:V_MIX + 8], (6, 7), s)
        r, s = rms(mem3, ms_, 8, ld_m, cs_ready)
        s_ms = scaled(ms_, mem3, r, s)
        mem_ready = turned(ms_, memT, vecs[:, V_MEM:V_MEM + 8], (4, 5), s_ms)

        qkv = []
        for c in range(5):
            def use(t_, b, s, c=c):
                qkv.append(evac(proj[:, t_, 512 * c:512 * c + 512], b.ap[:, :], s))
                return qkv[-1]
            token_major(hT3, h_ready, ((0, 1), (2, 3))[c % 2], use)

        mem_done = []
        def use(t_, b, s):
            mem_done.append(evac(mkv3[:, t_, :], b.ap[:, :], s))
            return mem_done[-1]
        token_major(memT, mem_ready, (2, 3), use)

        gates_done = []
        for c in range(6):
            def use(t_, b, s, c=c):
                d = gates[:, t_, c // 2, 512 * (c % 2):512 * (c % 2) + 512]
                gates_done.append(A(lambda e: e.activation(d, b.ap[:, :], ACT.Sigmoid), s, mem_ready, h_ready))
                return gates_done[-1]
            token_major(hT3, h_ready, ((0, 1), (2, 3))[c % 2], use)

        def seg(src, h0, n, at, g):
            return [(t_, src[:, t_, 64 * h0:64 * (h0 + n)].rearrange("p (h d) -> p h d", h=n), n, at, g) for t_ in range(2)]
        segs = (seg(proj, 0, 6, 0, 0) + seg(proj, 6, 6, 6, 1) + seg(proj, 18, 6, 12, 2) + seg(proj, 24, 6, 18, 3)
                + seg(proj, 36, 4, 24, 4) + seg(mkv3, 0, 4, 28, 5))
        hs = sm[:, 16:80].rearrange("p (t h) -> p t h", t=2)
        hy = sm[:, 80:144].rearrange("p (t h) -> p t h", t=2)
        s_sum = []
        sq = [Buf(tmp[:, 384 * i:384 * i + 384]) for i in range(8)]
        for i, (t_, v3, n, at, g) in enumerate(segs):
            q = sq[i % 2]
            q3 = q.ap[:, 0:64 * n].rearrange("p (h d) -> p h d", h=n)
            s = V(lambda e, q3=q3, v3=v3: e.tensor_tensor(q3, v3, v3, ALU.mult), qkv, mem_done, q.free)
            s = V(lambda e, q3=q3, t_=t_, at=at, n=n: e.tensor_reduce(hs[:, t_, at:at + n], q3, AX, ALU.add), s)
            q.free = [s]
            s_sum.append(s)
        s = V(lambda e: e.tensor_scalar(sm[:, 16:80], sm[:, 16:80], 1.0 / 64, EPS, ALU.mult, ALU.add), s_sum)
        s_inv = inv_root(sm[:, 16:80], sm[:, 80:144], sm[:, 144:208], s)
        normed = {}
        for i, (t_, v3, n, at, g) in enumerate(segs):
            rb = hy[:, t_, at:at + n].unsqueeze(2).to_broadcast([P, n, 64])
            gb = rows[:, B_HEAD + 64 * g:B_HEAD + 64 * g + 64].unsqueeze(1).to_broadcast([P, n, 64])
            s = V(lambda e, v3=v3, rb=rb: e.tensor_tensor(v3, v3, rb, ALU.mult), s_inv)
            s = V(lambda e, v3=v3, gb=gb: e.tensor_tensor(v3, v3, gb, ALU.mult), s, ld_r)
            if g < 4:
                q = sq[2 + i % 2]
                q3 = q.ap[:, :].rearrange("p (h d) -> p h d", h=n)
                cc = cs4[:, t_, 0:2, :].rearrange("p c f -> p (c f)").unsqueeze(1).to_broadcast([P, n, 64])
                ns = cs4[:, t_, 2, :].unsqueeze(1).to_broadcast([P, n, 32])
                ps_ = cs4[:, t_, 3, :].unsqueeze(1).to_broadcast([P, n, 32])
                s1 = V(lambda e, q3=q3, v3=v3, ns=ns: e.tensor_tensor(q3[:, :, 0:32], v3[:, :, 32:64], ns, ALU.mult), s, q.free)
                s2 = V(lambda e, q3=q3, v3=v3, ps_=ps_: e.tensor_tensor(q3[:, :, 32:64], v3[:, :, 0:32], ps_, ALU.mult), s)
                s3 = V(lambda e, v3=v3, cc=cc: e.tensor_tensor(v3, v3, cc, ALU.mult), s1, s2)
                s = V(lambda e, v3=v3, q3=q3: e.tensor_tensor(v3, v3, q3, ALU.add), s3)
                q.free = [s]
            normed[(g, t_)] = s

        pair_at = {0: 0, 1: 3, 2: 6, 3: 9, 4: 12, 5: 14}
        src_of = {0: (proj, 0, 3), 1: (proj, 384, 3), 2: (proj, 1152, 3), 3: (proj, 1536, 3), 4: (proj, 2304, 2), 5: (mkv3, 0, 2)}
        todo = [(g, j) for g in range(6) for j in range(src_of[g][2])]
        qk_ready = []
        for n in range(0, 16, 2):
            b = bank[6 + (n // 2) % 2]
            srcs, waits = [], []
            for g, j in todo[n:n + 2]:
                sr, c, _ = src_of[g]
                for t_ in range(2):
                    srcs.append(sr[:, t_, c + 128 * j:c + 128 * j + 128])
                    waits.append(normed[(g, t_)])
            s = transposes(b, srcs, waits)
            s = evac(qkT[:, n:n + 2, :].rearrange("p b t -> p (b t)"), b.ap[:, :], s, mem_done)
            b.free = [s]
            qk_ready.append(s)

        units = []
        for g, (qg, kg, n, col, vsrc, mask, counts) in enumerate((
                (0, 1, 3, 0, (proj, 768), mcau, None), (2, 3, 3, 384, (proj, 1920), mdil, cdil), (4, 5, 2, 768, (mkv3, 256), None, None))):
            for t_ in range(2):
                for j in range(n):
                    nk = 128 if t_ == 0 and mask is not None else 256
                    def q(h, p_=pair_at[qg] + j, t_=t_):
                        return qkT[64 * h:64 * h + 64, p_, 128 * t_:128 * t_ + 128]
                    def k(h, p_=pair_at[kg] + j, nk=nk):
                        return qkT[64 * h:64 * h + 64, p_, 0:nk]
                    def v(h, c, j=j, vs=vsrc):
                        return vs[0][:, c, vs[1] + 128 * j + 64 * h:vs[1] + 128 * j + 64 * h + 64]
                    units.append(dict(group=(g, t_), col=col + 128 * j, t=t_, nk=nk, q=q, k=k, v=v, mask=mask, counts=counts,
                                      bias=None, ready=qk_ready))
        att = attention(units, osb3, [list(normed.values()), s_ms])

        oT = qkT[:, 0:8, :]
        s_oT = turned(osb3, oT, None, (6, 7), att)
        merged = proj[:, :, 0:1024]
        merge = []
        held = {}
        for br, (kb, k0) in enumerate(((3, 0), (3, 3), (2, 6))):
            slot, here = slab()
            w = slot[:, 0:kb * 1024].rearrange("p (k n) -> p k n", k=kb)
            for t_ in range(2):
                for half in range(2):
                    b = bank[2 * t_ + half + 4 * (br % 2)]
                    c = slice(512 * half, 512 * half + 512)
                    s_last = matmuls(b.ap[:, :], [(oT[:, k0 + k, 128 * t_:128 * t_ + 128], w[:, k, c]) for k in range(kb)],
                                     here, s_oT, b.free)
                    m, gt = merged[:, t_, c], gates[:, t_, br, c]
                    if br == 0:
                        s = V(lambda e, m=m, gt=gt, b=b: e.tensor_tensor(m, b.ap[:, :], gt, ALU.mult), s_last, gates_done)
                        b.free = [s]
                    else:
                        s = V(lambda e, gt=gt, b=b: e.tensor_tensor(gt, b.ap[:, :], gt, ALU.mult), s_last, gates_done)
                        b.free = [s]
                        s = V(lambda e, m=m, gt=gt: e.tensor_tensor(m, m, gt, ALU.add), s, held[(t_, half)])
                    held[(t_, half)] = s
            fetch(s_last)
        mT = turned(merged, hT3, None, (6, 7), list(held.values()))
        xs_done = []
        for c in range(2):
            def use(t_, b, s, c=c):
                xs_done.append(add_to_x(t_, c, b, s))
                return xs_done[-1]
            token_major(hT3, mT, ((0, 1), (2, 3))[c], use)

        xs = proj[:, :, 0:1024]
        r, s = rms(x3, xs, 0, xs_done, mT)
        s = scaled(xs, x3, r, s, mT)
        h_ready = turned(xs, hT3, vecs[:, V_FFN:V_FFN + 8], (6, 7), s, xs_done)
        act = arena[:, 0:5632].rearrange("p (f t) -> p f t", f=22)
        ub = [Buf(tmp[:, 512 * i:512 * i + 512]) for i in range(6)]
        act_done = []
        for c in range(11):
            slot, here = slab()
            w = slot[:, :].rearrange("p (k n) -> p k n", k=8)
            for i in range(2):
                f = 2 * c + i
                b, u = bank[f % 4], ub[f % 3]
                for gv in range(2):
                    cw = 256 * gv + 128 * i
                    s = matmuls(b.ap[:, 256 * gv:256 * gv + 256], [(w[:, k, cw:cw + 128], hT3[:, k, :]) for k in range(8)],
                                here, h_ready, b.free if gv == 0 else None)
                taps, first = [], []
                for gv in range(2):
                    j = f + 22 * gv
                    ps_, d = b.ap[:, 256 * gv:256 * gv + 256], u.ap[:, 256 * gv:256 * gv + 256]
                    wv = vecs[:, V_CW + 3 * j:V_CW + 3 * j + 3]
                    bv = vecs[:, V_CB + j:V_CB + j + 1]
                    first.append(A(lambda e, d=d, ps_=ps_, wv=wv, bv=bv: e.activation(
                        d, ps_, ACT.Identity, bias=bv, scale=wv[:, 2:3]), s, u.free, att))
                for gv in range(2):
                    j = f + 22 * gv
                    ps_, d = b.ap[:, 256 * gv:256 * gv + 256], u.ap[:, 256 * gv:256 * gv + 256]
                    wv = vecs[:, V_CW + 3 * j:V_CW + 3 * j + 3]
                    q = first
                    for k in (1, 2):
                        q = V(lambda e, d=d, ps_=ps_, wv=wv, k=k: e.scalar_tensor_tensor(
                            d[:, k:256], ps_[:, 0:256 - k], wv[:, 2 - k:3 - k], d[:, k:256], ALU.mult, ALU.add), q)
                    taps.append(q)
                b.free = taps
                d = u.ap[:, 0:256]
                q = A(lambda e, d=d: e.activation(d, d, ACT.Silu), taps[0])
                q = V(lambda e, u=u, f=f: e.tensor_tensor(act[:, f, :], u.ap[:, 0:256], u.ap[:, 256:512], ALU.mult), q, taps[1])
                u.free = [q]
                act_done.append(q)
            fetch(s)
        for c in range(6):
            slot, here = slab()
            kb = min(4, 22 - 4 * c)
            w = slot[:, 0:kb * 1024].rearrange("p (k n) -> p k n", k=kb)
            for k in range(kb):
                f = 4 * c + k
                for t_ in range(2):
                    for half in range(2):
                        b = bank[4 + 2 * t_ + half]
                        s = E(lambda e, b=b, f=f, t_=t_, half=half, w=w, k=k: e.matmul(
                            b.ap[:, :], act[:, f, 128 * t_:128 * t_ + 128], w[:, k, 512 * half:512 * half + 512],
                            start=(f == 0), stop=(f == 21)), here, act_done[f], b.free if f == 0 else None)
            fetch(s)
        ready = []
        for t_ in range(2):
            for half in range(2):
                b = bank[4 + 2 * t_ + half]
                q = add_to_x(t_, half, b, s)
                b.free = [q]
                ready.append(q)
        prior = [act_done, s, h_ready]

        def log1p(e_, z, z2, p_, *after):
            s = V(lambda e: e.tensor_scalar(z, e_, 2.0, None, ALU.add), *after)
            s = V(lambda e: e.reciprocal(z, z), s)
            s = V(lambda e: e.tensor_tensor(z, z, e_, ALU.mult), s)
            s = V(lambda e: e.tensor_tensor(z2, z, z, ALU.mult), s)
            s = V(lambda e: e.tensor_scalar(p_, z2, 2.0 / 19, None, ALU.mult), s)
            for n in range(17, 1, -2):
                s = V(lambda e, n=n: e.scalar_tensor_tensor(p_, p_, 2.0 / n, z2, ALU.add, ALU.mult), s)
            return V(lambda e: e.scalar_tensor_tensor(p_, p_, 2.0, z, ALU.add, ALU.mult), s)

        l_row = landing("l_row")
        free_row = None
        free_kk = free_rg = free_wf = None
        for l in range(2):
            lv = V_L + L_END * l
            ld_kk = load(S, l_kk, kk[:, :], T["keys"][l], free_kk)
            ld_rg = load(S, l_rg, rgw[:, :], T["rgw"][l], free_rg)
            ld_wf = load(S, l_wf, wf[:, :], T["wf"][l], free_wf)
            ld_row = load(S, l_row, rowg[:, :], T["rows"][:, B_N2 + 1024 * l:B_N2 + 1024 * l + 1024], free_row)

            xs = osb3
            r, s = rms(x3, xs, 0, ready, prior)
            s = scaled(xs, x3, r, s, prior)
            h_ready = turned(xs, hT3, vecs[:, V_N1 + 8 * l:V_N1 + 8 * l + 8], (6, 7), s, prior)

            qT2 = qkT[:, 0:8, :]
            qk = []
            for c in range(2):
                def use(j, b, s, c=c):
                    qk.append(evac(qkT[:, 4 * c + 2 * j:4 * c + 2 * j + 2, :].rearrange("p b t -> p (b t)"), b.ap[:, :], s))
                    return qk[-1]
                feature_major(hT3, h_ready, ((0, 1), (2, 3))[c], use)
            v_done = []
            def use(t_, b, s):
                v_done.append(evac(mkv3[:, t_, :], b.ap[:, :], s))
                return v_done[-1]
            token_major(hT3, h_ready, (0, 1), use)

            b = bank[4]
            s_f = matmuls(b.ap[0:104, 0:256], [(wf3[:, k, :], hT3[:, k, :]) for k in range(8)], ld_wf, h_ready, b.free)
            free_wf = s_f
            base = 6144
            fz, fa, fe, f1, f2, f3, R = (arena[0:104, base + 256 * i:base + 256 * i + 256] for i in range(7))
            Lh = arena[0:104, base + 1792:base + 1792 + 1024].rearrange("p (h t) -> p h t", h=4)
            s = V(lambda e: e.tensor_scalar(fz, b.ap[0:104, 0:256], vecs[0:104, lv + L_BF:lv + L_BF + 1], None, ALU.add), s_f, ld_v)
            b.free = [s]
            s = V(lambda e: e.tensor_scalar(fa, fz, -1.0, None, ALU.mult), s)
            s = V(lambda e: e.tensor_tensor(fa, fa, fz, ALU.max), s)
            s_e = A(lambda e: e.activation(fe, fa, ACT.Exp, scale=-1.0), s)
            s = log1p(fe, f1, f2, f3, s_e)
            s = V(lambda e: e.scalar_tensor_tensor(fz, fz, 0.0, f3, ALU.min, ALU.subtract), s)
            s = V(lambda e: e.memset(f2, 1.0), s)
            s = V(lambda e: e.tensor_tensor_scan(fa, f2, fz, 0.0, ALU.mult, ALU.add), s)
            lr = []
            for h in range(4):
                lr.append(V(lambda e, h=h: e.tensor_scalar(Lh[:, h, :], fa, const[0:104, K_SEL + h:K_SEL + h + 1],
                                                          const[0:104, K_SEL + 5 + h:K_SEL + 6 + h], ALU.mult, ALU.add), s))
            lr.append(V(lambda e: e.tensor_scalar(R, fa, const[0:104, K_SEL + 4:K_SEL + 5],
                                                  const[0:104, K_SEL + 9:K_SEL + 10], ALU.mult, ALU.add), s))

            mixT = arena[:, 0:2048].rearrange("p (k t) -> p k t", k=8)
            ypad = arena[:, 2048:2048 + 572].rearrange("p (b t) -> p b t", b=2)
            xpad = arena[:, 2624:2624 + 518].rearrange("p (b t) -> p b t", b=2)
            gg = arena[:, 3200:3712]
            yc = arena[:, 3712:4224].rearrange("p (b t) -> p b t", b=2)
            xc = arena[:, 4224:4736].rearrange("p (b t) -> p b t", b=2)
            z1 = V(lambda e: e.memset(ypad[:, :, 0:30], 0.0), prior, h_ready)
            z2 = V(lambda e: e.memset(xpad[:, :, 0:3], 0.0), prior, h_ready)
            hold = []
            def use(j, b, s):
                if j == 0:
                    s = A(lambda e: e.activation(yc.rearrange("p b t -> p (b t)"), b.ap[:, :], ACT.Copy), s, prior)
                    hold.append(s)
                    return s
                s = A(lambda e: e.activation(gg, b.ap[:, :], ACT.Sigmoid), s, prior)
                hold.append(s)
                return s
            feature_major(hT3, h_ready, (2, 3), use)
            s_y = V(lambda e: e.tensor_tensor(ypad[:, :, 30:286], yc, gg.rearrange("p (b t) -> p b t", b=2), ALU.mult), hold)
            hold2 = []
            def use(j, b, s):
                if j == 0:
                    s = V(lambda e: e.tensor_copy(xpad[:, :, 3:259], b.ap[:, :].rearrange("p (b t) -> p b t", b=2)), s, prior)
                else:
                    s = A(lambda e: e.activation(gg, b.ap[:, :], ACT.Gelu_apprx_tanh), s, s_y)
                hold2.append(s)
                return s
            feature_major(hT3, h_ready, (0, 1), use)

            w = vecs[:, lv + L_RW:lv + L_RW + 8].rearrange("p (b k) -> p b k", b=2)
            xcd = []
            for bl in range(2):
                s = V(lambda e, bl=bl: e.tensor_scalar(xc[:, bl, :], xpad[:, bl, 3:259], w[:, bl, 3:4],
                                                       vecs[:, lv + L_RB + bl:lv + L_RB + bl + 1], ALU.mult, ALU.add), hold2, z2)
                for k in range(3):
                    s = V(lambda e, bl=bl, k=k: e.scalar_tensor_tensor(xc[:, bl, :], xpad[:, bl, k:k + 256], w[:, bl, k:k + 1],
                                                                       xc[:, bl, :], ALU.mult, ALU.add), s)
                xcd.append(s)
            ri = []
            rg_t = [tmps[0], tmps[1]]
            for g in range(2):
                b = bank[2 + g]
                for bl in range(2):
                    s = matmuls(b.ap[:, 256 * bl:256 * bl + 256], [(rgw4[:, g, bl, :], xc[:, bl, :])], ld_rg, xcd,
                                b.free if bl == 0 else None)
                ac = []
                for bl in range(2):
                    c = lv + (L_BR, L_BI)[g] + bl
                    d = rg_t[g].ap[:, 256 * bl:256 * bl + 256]
                    ac.append(A(lambda e, d=d, b=b, bl=bl, c=c: e.activation(d, b.ap[:, 256 * bl:256 * bl + 256], ACT.Sigmoid,
                                                                           bias=vecs[:, c:c + 1]), s, prior))
                b.free = ac
                ri.append(ac)
            free_rg = s
            lam = vecs[:, lv + L_LAM:lv + L_LAM + 2]
            l0, l1, l2, l3, l4 = (sm[:, 700 + 2 * i:702 + 2 * i] for i in range(5))
            s = V(lambda e: e.tensor_scalar(l0, lam, -1.0, None, ALU.mult), ld_v)
            s = V(lambda e: e.tensor_tensor(l1, l0, lam, ALU.max), s)
            s = A(lambda e: e.activation(l1, l1, ACT.Exp, scale=-1.0), s)
            s = log1p(l1, l2, l3, l4, s)
            s = V(lambda e: e.scalar_tensor_tensor(l4, l0, 0.0, l4, ALU.max, ALU.add), s)
            s_c = V(lambda e: e.tensor_scalar(l4, l4, 8.0, None, ALU.mult), s)
            nl = tmps[0].ap
            aa, tt, dd = tmps[2].ap, tmps[3].ap, tmps[4].ap
            s = [V(lambda e, bl=bl: e.tensor_scalar(nl[:, 256 * bl:256 * bl + 256], nl[:, 256 * bl:256 * bl + 256], l4[:, bl:bl + 1],
                                                    None, ALU.mult), s_c, ri) for bl in range(2)]
            s_a = A(lambda e: e.activation(aa, nl, ACT.Exp, scale=-1.0), s)
            s = A(lambda e: e.activation(tt, nl, ACT.Tanh), s)
            s = V(lambda e: e.tensor_scalar(dd, tt, 0.5, 0.5, ALU.mult, ALU.add), s)
            s = V(lambda e: e.reciprocal(dd, dd), s)
            s = V(lambda e: e.tensor_tensor(tt, tt, dd, ALU.mult), s)
            s = A(lambda e: e.activation(tt, tt, ACT.Sqrt), s)
            ii = tmps[1].ap
            s1 = V(lambda e: e.tensor_tensor(ii, ii, xc.rearrange("p b t -> p (b t)"), ALU.mult), ri)
            s = V(lambda e: e.tensor_tensor(tt, tt, ii, ALU.mult), s, s1)
            s = [V(lambda e, bl=bl: e.tensor_tensor_scan(dd[:, 256 * bl:256 * bl + 256], aa[:, 256 * bl:256 * bl + 256],
                                                         tt[:, 256 * bl:256 * bl + 256], 0.0, ALU.mult, ALU.add), s, s_a)
                 for bl in range(2)]
            s_rnn = V(lambda e: e.tensor_tensor(mixT[:, 6:8, :].rearrange("p b t -> p (b t)"), dd, gg, ALU.mult), s, hold2)

            w31 = vecs[:, lv + L_DW:lv + L_DW + 62].rearrange("p (b k) -> p b k", b=2)
            cd = []
            for bl in range(2):
                s = V(lambda e, bl=bl: e.tensor_scalar(yc[:, bl, :], ypad[:, bl, 30:286], w31[:, bl, 30:31],
                                                       vecs[:, lv + L_DB + bl:lv + L_DB + bl + 1], ALU.mult, ALU.add), s_y, z1)
                for k in range(30):
                    s = V(lambda e, bl=bl, k=k: e.scalar_tensor_tensor(yc[:, bl, :], ypad[:, bl, k:k + 256], w31[:, bl, k:k + 1],
                                                                       yc[:, bl, :], ALU.mult, ALU.add), s)
                cd.append(s)
            b = bank[2]
            s = matmuls(b.ap[:, 0:256], [(ones, yc[:, bl, :]) for bl in range(2)], cd, b.free)
            mean, var, rr, r2 = (tmps[5].ap[:, 0:256], tmps[5].ap[:, 256:512], junk[:, 0:256], junk[:, 256:512])
            s = V(lambda e: e.tensor_scalar(mean, b.ap[:, 0:256], 1.0 / 256, None, ALU.mult), s)
            b.free = [s]
            s_d = V(lambda e: e.tensor_tensor(yc, yc, mean.unsqueeze(1).to_broadcast([P, 2, 256]), ALU.subtract), s)
            sq3 = junk[:, 512:1024].rearrange("p (b t) -> p b t", b=2)
            s = V(lambda e: e.tensor_tensor(sq3, yc, yc, ALU.mult), s_d)
            b = bank[3]
            s = matmuls(b.ap[:, 0:256], [(ones, sq3[:, bl, :]) for bl in range(2)], s, b.free)
            s = V(lambda e: e.tensor_scalar(var, b.ap[:, 0:256], 1.0 / 256, EPS, ALU.mult, ALU.add), s)
            b.free = [s]
            s = inv_root(var, rr, r2, s)
            s = V(lambda e: e.tensor_tensor(yc, yc, rr.unsqueeze(1).to_broadcast([P, 2, 256]), ALU.mult), s)
            cd = [A(lambda e, bl=bl: e.activation(mixT[:, 4 + bl, :], yc[:, bl, :], ACT.Silu,
                                                  bias=vecs[:, lv + L_B + bl:lv + L_B + bl + 1],
                                                  scale=vecs[:, lv + L_G + bl:lv + L_G + bl + 1]), s) for bl in range(2)]

            units = []
            for t_ in range(2):
                nk = 128 * (t_ + 1)
                for j in range(4):
                    def q(h, j=j, t_=t_):
                        return qkT[64 * h:64 * h + 64, j, 128 * t_:128 * t_ + 128]
                    def k(h, j=j, nk=nk):
                        return qkT[64 * h:64 * h + 64, 4 + j, 0:nk]
                    def v(h, c, j=j):
                        return mkv3[:, c, 128 * j + 64 * h:128 * j + 64 * h + 64]
                    def bias(h, j=j, t_=t_, nk=nk):
                        return Lh[64 * h:64 * h + 40, j, 128 * t_:128 * t_ + 128], R[64 * h:64 * h + 40, 0:nk]
                    units.append(dict(group=(0, t_), col=128 * j, t=t_, nk=nk, q=q, k=k, v=v, mask=mcau, counts=None,
                                      bias=bias, ready=[qk, v_done, lr]))
            att = attention(units, osb3, [s_rnn, cd, h_ready])
            done = []
            for t_ in range(2):
                b = bank[6 + t_]
                s = transposes(b, [osb3[:, t_, 128 * i:128 * i + 128] for i in range(4)], att)
                s = evac(mixT[:, 0:4, 128 * t_:128 * t_ + 128], b.ap[:, :].rearrange("p (k n) -> p k n", k=4), s)
                b.free = [s]
                done.append(s)
            mix_ready = [done, s_rnn, cd]
            xs_done = []
            for c in range(2):
                def use(t_, b, s, c=c):
                    xs_done.append(add_to_x(t_, c, b, s))
                    return xs_done[-1]
                token_major(mixT, mix_ready, ((0, 1), (2, 3))[c], use)

            xn = osb3
            r, s = rms(x3, xn, 0, xs_done, done)
            s = [V(lambda e, t_=t_: e.scalar_tensor_tensor(xn[:, t_, :], x3[:, t_, :], r[:, t_:t_ + 1],
                                                           rowg[:, :], ALU.mult, ALU.mult),
                   s, ld_row, done) for t_ in range(2)]
            free_row = s
            h_ready = turned(xn, hT3, None, (6, 7), s)
            qp = []
            for c in range(4):
                def use(j, b, s, c=c):
                    qp.append(evac(qkT[:, 4 * c + 2 * j:4 * c + 2 * j + 2, :].rearrange("p b t -> p (b t)"), b.ap[:, :], s, att))
                    return qp[-1]
                feature_major(hT3, h_ready, ((0, 1), (2, 3))[c % 2], use)

            top = sm[:, 0:256].rearrange("p (a h k) -> p a h k", a=2, h=8)
            topi = smi[:, 0:256].rearrange("p (a h k) -> p a h k", a=2, h=8)
            topf = junk[:, 0:256].rearrange("p (a h k) -> p a h k", a=2, h=8)
            best = sm[:, 256:384].rearrange("p (h k) -> p h k", h=8)
            besti = smi[:, 256:384].rearrange("p (h k) -> p h k", h=8)
            hilo = smi[:, 384:512]
            hf = junk[:, 256:512].rearrange("p (a h k) -> p a h k", a=2, h=8)
            ef = junk[:, 512:768].rearrange("p (a h k) -> p a h k", a=2, h=8)
            cand = arena[:, 0:2048]
            cand3 = cand.rearrange("p (h c) -> p h c", h=8)
            cand4 = cand.rearrange("p (h i j) -> p h i j", h=8, i=16)
            oh = arena[:, 2048:4096]
            oh4 = oh.rearrange("p (h k j) -> p h k j", h=8, k=16)
            gate = [sm[:, 384 + 128 * t_:512 + 128 * t_] for t_ in range(2)]
            routed = []
            last_v = None
            s_scores = None
            for t_ in range(2):
                for a in range(2):
                    for hh in range(2):
                        b = bank[2 * a + hh]
                        for h in range(4):
                            s = matmuls(b.ap[:, 128 * h:128 * h + 128],
                                        [(qkT[:, 2 * (4 * hh + h) + a, 128 * t_:128 * t_ + 128], kk4[:, a, 4 * hh + h, :])],
                                        ld_kk, qp, b.free if h == 0 else None)
                        s_scores = s
                        for h in range(4):
                            src = b.ap[:, 128 * h:128 * h + 128]
                            h8 = 4 * hh + h
                            lo, hi = top[:, a, h8, 0:8], top[:, a, h8, 8:16]
                            li, hi_i = topi[:, a, h8, 0:8], topi[:, a, h8, 8:16]
                            rest = oh[:, 1024 * a + 128 * h8:1024 * a + 128 * h8 + 128]
                            q1 = V(lambda e, lo=lo, src=src: e.max(lo, src), s, last_v)
                            q2 = V(lambda e, lo=lo, li=li, src=src: e.max_index(li, lo, src), q1)
                            q3 = V(lambda e, lo=lo, rest=rest, src=src: e.match_replace(rest, lo, src, -3e38), q1)
                            q4 = V(lambda e, hi=hi, rest=rest: e.max(hi, rest), q3)
                            q5 = V(lambda e, hi=hi, hi_i=hi_i, rest=rest: e.max_index(hi_i, hi, rest), q4)
                        b.free = [q3]
                free_kk = s_scores
                s = V(lambda e: e.tensor_copy(topf, topi), q5)
                s1 = V(lambda e: e.tensor_tensor(cand4, top[:, 0].unsqueeze(3).to_broadcast([P, 8, 16, 16]),
                                                 top[:, 1].unsqueeze(2).to_broadcast([P, 8, 16, 16]), ALU.add), q5)
                for h in range(8):
                    src, rest = cand3[:, h, :], oh[:, 256 * h:256 * h + 256]
                    lo, hi = best[:, h, 0:8], best[:, h, 8:16]
                    li, hi_i = besti[:, h, 0:8], besti[:, h, 8:16]
                    q1 = V(lambda e, lo=lo, src=src: e.max(lo, src), s1)
                    q2 = V(lambda e, lo=lo, li=li, src=src: e.max_index(li, lo, src), q1)
                    q3 = V(lambda e, lo=lo, rest=rest, src=src: e.match_replace(rest, lo, src, -3e38), q1)
                    q4 = V(lambda e, hi=hi, rest=rest: e.max(hi, rest), q3)
                    q5 = V(lambda e, hi=hi, hi_i=hi_i, rest=rest: e.max_index(hi_i, hi, rest), q4)
                bi = smi[:, 256:384]
                for a in range(2):
                    if a == 0:
                        q = V(lambda e: e.tensor_scalar(hilo, bi, 4, None, ALU.logical_shift_right), q5)
                    else:
                        q = V(lambda e: e.tensor_scalar(hilo, bi, 15, None, ALU.bitwise_and), q)
                    q = V(lambda e, a=a: e.tensor_copy(hf[:, a].rearrange("p h k -> p (h k)"), hilo), q)
                    q = V(lambda e, a=a: e.tensor_tensor(oh4, hf[:, a].unsqueeze(3).to_broadcast([P, 8, 16, 16]),
                                                         iota.unsqueeze(1).unsqueeze(1).to_broadcast([P, 8, 16, 16]), ALU.is_equal), q, q5)
                    q = V(lambda e, a=a: e.tensor_tensor(oh4, oh4, topf[:, a].unsqueeze(2).to_broadcast([P, 8, 16, 16]), ALU.mult), q, s)
                    q = V(lambda e, a=a: e.tensor_reduce(ef[:, a], oh4, AX, ALU.add), q)
                e1, e2 = (junk[:, 512 + 128 * a:640 + 128 * a] for a in range(2))
                q = V(lambda e: e.tensor_scalar(e1, e1, 128.0, float(16384 * l), ALU.mult, ALU.add), q)
                q = V(lambda e, t_=t_: e.tensor_tensor(eidx[:, 128 * t_:128 * t_ + 128], e1, e2, ALU.add), q)
                routed.append(q)
                g3 = gate[t_].rearrange("p (h k) -> p h k", h=8)
                gs = sm[:, 720:728]
                q = V(lambda e, g3=g3: e.tensor_tensor(g3, best, best[:, :, 0:1].to_broadcast([P, 8, 16]), ALU.subtract), q5, q)
                q = A(lambda e, g=gate[t_]: e.activation(g, g, ACT.Exp), q)
                q = V(lambda e, g3=g3: e.tensor_reduce(gs, g3, AX, ALU.add), q)
                q = V(lambda e: e.reciprocal(gs, gs), q)
                q = V(lambda e, g3=g3: e.tensor_tensor(g3, g3, gs.unsqueeze(2).to_broadcast([P, 8, 16]), ALU.mult), q)
                last_v = q

            u_tab = T["peer_u"].rearrange("l e d -> (l e) d")
            v_tab = T["peer_v"].rearrange("l e d -> (l e) d")
            slots = [Buf(arena[:, 1024 * i:1024 * i + 1024]) for i in range(ROWS)]
            for b in slots:
                b.free = [last_v, s_scores]
            nslot = [0]
            acc_free = [bank[4].free + bank[5].free, bank[6].free + bank[7].free]

            def gather(tab, t_, k):
                i = nslot[0] % ROWS
                nslot[0] += 1
                sl = slots[i]
                step = M.dma(row_landed[i], lambda e: e.indirect_dma_start(
                    sl.ap, None, tab, bass.IndirectOffsetOnAxis(ap=eidx[:, 128 * t_ + k:128 * t_ + k + 1], axis=0)),
                    sl.free, routed[t_])
                return sl, step

            def up(t_, g):
                last = []
                for k in range(G * g, G * g + G):
                    sl, here = gather(u_tab, t_, k)
                    c = 128 * t_ + k
                    s = V(lambda e, sl=sl, c=c, t_=t_: e.tensor_tensor_reduce(
                        out=sl.ap, in0=sl.ap, in1=xn[:, t_, :], scale=1.0, scalar=0.0, op0=ALU.mult, op1=ALU.add,
                        accum_out=hid[:, c:c + 1]), here)
                    sl.free = [s]
                c = 128 * t_ + G * g
                s = A(lambda e: e.activation(wexp[:, c:c + G], hid[:, c:c + G], ACT.Gelu_apprx_tanh), s)
                return V(lambda e, t_=t_: e.tensor_tensor(wexp[:, c:c + G], wexp[:, c:c + G],
                                                         gate[t_][:, G * g:G * g + G], ALU.mult), s)

            def down(t_, g, ready_w):
                for k in range(G * g, G * g + G):
                    sl, here = gather(v_tab, t_, k)
                    dg = diags[ndiag[0] % 4]
                    ndiag[0] += 1
                    c = 128 * t_ + k
                    s_dg = A(lambda e, dg=dg, c=c: e.activation(dg.ap, ident, ACT.Copy, scale=wexp[:, c:c + 1]), ready_w, dg.free)
                    for half in range(2):
                        b = bank[4 + 2 * t_ + half]
                        s = E(lambda e, b=b, dg=dg, sl=sl, half=half, k=k: e.matmul(
                            b.ap[:, :], dg.ap, sl.ap[:, 512 * half:512 * half + 512], start=(k == 0), stop=(k == 127)),
                            here, s_dg, acc_free[t_] if k == 0 and half == 0 else None)
                    dg.free = [s]
                    sl.free = [s]
                if g == 128 // G - 1:
                    for half in range(2):
                        b = bank[4 + 2 * t_ + half]
                        q = add_to_x(t_, half, b, s)
                        b.free = [q]
                        ready.append(q)
                return s

            ready = []
            before = None
            for t_ in range(2):
                for g in range(128 // G):
                    w_ = up(t_, g)
                    if before:
                        s_last = down(*before)
                    before = (t_, g, w_)
            s_last = down(*before)
            prior = [s_last, ready, w_]

        r, s = rms(x3, osb3, 0, ready, prior)
        ld_row = load(S, l_row, rowg[:, :], T["rows"][:, B_FIN:B_FIN + 1024], free_row)
        y = osb3
        stores = []
        l_out = landing("l_out")
        o3 = out.rearrange("(t p) d -> p t d", p=P)
        for t_ in range(2):
            q = V(lambda e, t_=t_: e.scalar_tensor_tensor(y[:, t_, :], x3[:, t_, :], r[:, t_:t_ + 1],
                                                          rowg[:, :], ALU.mult, ALU.mult), s, prior, ld_row)
            stores.append(load(S, l_out, o3[:, t_, :], y[:, t_, :], q))
        S(lambda e: e.nop(), stores)

        for q in (S, A, V, E, M):
            q.number()
        block = ctx.enter_context(nc.Block())

        @block.sync
        def _(eng):
            S.emit(eng)

        @block.scalar
        def _(eng):
            A.emit(eng)

        @block.vector
        def _(eng):
            V.emit(eng)

        @block.tensor
        def _(eng):
            E.emit(eng)

        @block.gpsimd
        def _(eng):
            M.emit(eng)


def constants():
    c = np.zeros((P, K_END), np.float32)
    c[:, K_ID:K_ID + 128] = np.eye(P)
    i = np.arange(256)[:, None]
    j = np.arange(256)[None, :]
    causal = j <= i
    d = i - j
    counts = causal * ((d <= 128).astype(int) + (d % 4 == 0) + (d % 16 == 0))
    for at, m in ((K_MC, np.where(causal, 0.0, NEG)), (K_MD, np.where(counts > 0, 0.0, NEG)), (K_CD, counts)):
        c[:, at:at + 512] = m.reshape(2, P, 256).transpose(1, 0, 2).reshape(P, 512)
    c[:, K_ONE:K_ONE + 128] = 1.0
    c[:, K_IO:K_IO + 16] = np.arange(16)
    c[:, K_IF:K_IF + 32] = np.float32(10000.0) ** (-np.arange(32, dtype=np.float32) / np.float32(32))
    for h in range(8):
        at = 64 * (h % 2) + h
        c[at + 32, K_SEL + h // 2] = 8.0
        c[at, K_SEL + 5 + h // 2] = 1.0
    for at in (0, 64):
        c[at:at + 8, K_SEL + 4] = -8.0
        c[at + 32:at + 40, K_SEL + 9] = 1.0
    return c


def kernel(**inputs):
    import concourse.bacc as _bacc
    from concourse.bass_utils import run_bass_kernel_spmd as _run

    a = {k: np.asarray(v) for k, v in inputs.items()}

    def col(v):
        return v.reshape(-1, P).T

    def pad(v, n):
        out = np.zeros((P, n), v.dtype)
        out[:v.shape[0]] = v.reshape(v.shape[0], -1)
        return out

    def forget(v):
        out = np.zeros(v.shape[:-1] + (104,), v.dtype)
        for at in (0, 32, 64, 96):
            out[..., at:at + 8] = v
        return out

    parts = [col(a["mix_norm_g"][0]), col(a["mem_norm_g"][0]), col(a["ffn_norm_g"][0]),
             col(a["norm1_g_2"][0]), col(a["norm1_g_2"][1]),
             a["ffn_conv_w"][0].reshape(3, 44, P).transpose(2, 1, 0).reshape(P, 132), col(a["ffn_conv_b"][0])]
    for l in range(2):
        parts += [a["conv_dw_w_2"][l].reshape(31, 2, P).transpose(2, 1, 0).reshape(P, 62), col(a["conv_dw_b_2"][l]),
                  col(a["conv_ln_g_2"][l]), col(a["conv_ln_b_2"][l]),
                  a["rg_conv_w_2"][l].reshape(4, 2, P).transpose(2, 1, 0).reshape(P, 8), col(a["rg_conv_b_2"][l]),
                  col(a["rg_b_r_2"][l]), col(a["rg_b_i_2"][l]), col(a["rg_lambda_2"][l]),
                  pad(forget(a["b_forget_2"][l]), 1)]
    vecs = np.concatenate(parts, axis=1)
    row = np.concatenate([a[n][0] for n in ("moba_q_norm_g", "moba_k_norm_g", "dil_q_norm_g", "dil_k_norm_g",
                                            "mem_q_norm_g", "mem_k_norm_g")]
                         + [a["norm2_g_2"][0], a["norm2_g_2"][1], a["final_g_2"]])
    keys = np.stack([a["peer_k1_2"], a["peer_k2_2"]], axis=1).transpose(0, 4, 1, 2, 3).reshape(2, P, 2048)
    rg = np.zeros((2, 2, 2, P, P), np.float32)
    for g, n in enumerate(("rg_w_r_2", "rg_w_i_2")):
        for h in range(4):
            o = 64 * (h % 2)
            rg[:, g, h // 2, o:o + 64, o:o + 64] = a[n][:, h]
    rgw = rg.transpose(0, 3, 1, 2, 4).reshape(2, P, 512)
    wf = forget(a["w_in_2"][:, :, 1536:1544]).reshape(2, 8, P, 104).transpose(0, 2, 1, 3).reshape(2, P, 832)
    arrays = {
        "x": a["x"][0], "mem": a["mem"][0], "pos": a["positions"][0].reshape(2, P).T,
        "const": constants(), "vecs": vecs, "rows": np.broadcast_to(row, (P, row.size)),
        "keys": keys, "rgw": rgw, "wf": wf,
        "w_in": a["w_in"][0], "w_mem_kv": a["w_mem_kv"][0], "w_branch_moba": a["w_branch_moba"][0],
        "w_branch_dil": a["w_branch_dil"][0], "w_branch_mem": a["w_branch_mem"][0], "w_out": a["w_out"][0],
        "w_ffn_up": a["w_ffn_up"][0], "w_ffn_down": a["w_ffn_down"][0],
        "w_in_2": a["w_in_2"], "w_out_2": a["w_out_2"], "peer_wq": a["peer_wq_2"],
        "peer_u": a["peer_u_2"], "peer_v": a["peer_v_2"],
    }
    nc = _bacc.Bacc("TRN2", target_bir_lowering=False, num_devices=1)
    feeds, T = {}, {}
    for name, v in arrays.items():
        v = np.ascontiguousarray(v)
        feeds[f"in_{name}_dram"] = v
        T[name] = nc.dram_tensor(f"in_{name}_dram", v.shape, mybir.dt.from_np(v.dtype), kind="ExternalInput").ap()
    out = nc.dram_tensor("out_0_dram", (256, 1024), F32, kind="ExternalOutput").ap()
    program(nc, T, out)
    r = _run(nc, [feeds], core_ids=[0])
    return r.results[0]["out_0_dram"].reshape(1, 256, 1024)
```

```python
from contextlib import ExitStack

import numpy as np

import concourse.bass as bass
from concourse import mybir

ALU = mybir.AluOpType
ACT = mybir.ActivationFunctionType
AX = mybir.AxisListType.X
F32 = mybir.dt.float32
I32 = mybir.dt.int32
U32 = mybir.dt.uint32

P = 128
EPS = 1e-6
TWO_PI = 6.283185307179586
C1 = 6.28125
C2 = 0.0019350051879882812
C3 = TWO_PI - C1 - C2
MAGIC = 12582912.0
NEG = -1e30
SLOT = 4096
NSLOT = 3
ROWS = 12
G = 8
LAG = 10

K_ID, K_MC, K_MD, K_CD, K_ONE, K_IO, K_IF, K_SEL, K_END = 0, 128, 640, 1152, 1664, 1792, 1808, 1840, 1850
V_MIX, V_MEM, V_FFN, V_N1, V_CW, V_CB, V_L = 0, 8, 16, 24, 40, 172, 216
L_DW, L_DB, L_G, L_B, L_RW, L_RB, L_BR, L_BI, L_LAM, L_BF, L_END = 0, 62, 64, 66, 68, 76, 78, 80, 82, 84, 85
V_END = V_L + 2 * L_END
B_HEAD, B_N2, B_FIN, B_END = 0, 384, 384 + 2048, 384 + 3072


class Ops:

    def activation(self, *a, **k):
        self.call = lambda e: e.activation(*a, **k)

    def dma_start(self, *a, **k):
        self.call = lambda e: e.dma_start(*a, **k)

    def indirect_dma_start(self, *a, **k):
        self.call = lambda e: e.indirect_dma_start(*a, **k)

    def match_replace(self, *a, **k):
        self.call = lambda e: e.match_replace(*a, **k)

    def matmul(self, *a, **k):
        self.call = lambda e: e.matmul(*a, **k)

    def max(self, *a, **k):
        self.call = lambda e: e.max(*a, **k)

    def max_index(self, *a, **k):
        self.call = lambda e: e.max_index(*a, **k)

    def memset(self, *a, **k):
        self.call = lambda e: e.memset(*a, **k)

    def nop(self, *a, **k):
        self.call = lambda e: e.nop(*a, **k)

    def reciprocal(self, *a, **k):
        self.call = lambda e: e.reciprocal(*a, **k)

    def scalar_tensor_tensor(self, *a, **k):
        self.call = lambda e: e.scalar_tensor_tensor(*a, **k)

    def tensor_copy(self, *a, **k):
        self.call = lambda e: e.tensor_copy(*a, **k)

    def tensor_reduce(self, *a, **k):
        self.call = lambda e: e.tensor_reduce(*a, **k)

    def tensor_scalar(self, *a, **k):
        self.call = lambda e: e.tensor_scalar(*a, **k)

    def tensor_tensor(self, *a, **k):
        self.call = lambda e: e.tensor_tensor(*a, **k)

    def tensor_tensor_reduce(self, *a, **k):
        self.call = lambda e: e.tensor_tensor_reduce(*a, **k)

    def tensor_tensor_scan(self, *a, **k):
        self.call = lambda e: e.tensor_tensor_scan(*a, **k)

    def transpose(self, *a, **k):
        self.call = lambda e: e.transpose(*a, **k)


class Step:

    def __init__(self, queue, fn, after):
        self.queue, self.fn, self.after = queue, fn, after
        self.sem = self.value = None
        self.marked = False


def _flat(steps):
    for s in steps:
        if isinstance(s, (list, tuple)):
            yield from _flat(s)
        elif s is not None:
            yield s


class Queue:

    def __init__(self, sem):
        self.sem, self.steps, self.pending = sem, [], []

    def __call__(self, fn, *after):
        after = list(_flat(after)) + self.pending
        self.pending = []
        for a in after:
            a.marked = True
        ops = Ops()
        fn(ops)
        step = Step(self, ops.call, after)
        self.steps.append(step)
        return step

    def wait(self, *steps):
        self.pending += _flat(steps)

    def dma(self, landed, fn, *after):
        step = self(fn, *after)
        landed[1] += 16
        step.sem, step.value = landed
        return step

    def number(self):
        n = 0
        for s in self.steps:
            if s.sem is None and s.marked:
                n += 1
                s.value = n

    def emit(self, eng):
        seen = {}
        for s in self.steps:
            for a in s.after:
                sem = a.sem or a.queue.sem
                if seen.get(id(sem), 0) < a.value:
                    eng.wait_ge(sem, a.value)
                    seen[id(sem)] = a.value
            ins = s.fn(eng)
            if s.sem is not None:
                ins.then_inc(s.sem, 16)
            elif s.marked:
                ins.then_inc(self.sem, 1)


class Buf:

    def __init__(self, ap):
        self.ap, self.free = ap, []


def program(nc, T, out):
    ctx = ExitStack()
    with ctx:
        def sb(name, cols, dt=F32):
            return ctx.enter_context(nc.sbuf_tensor(name, [P, cols], dt))

        def sem(name):
            return ctx.enter_context(nc.semaphore(name))

        S, A, V, E, M = (Queue(sem(n)) for n in ("q_sp", "q_act", "q_dve", "q_pe", "q_pool"))

        const = sb("const", K_END)
        vecs = sb("vecs", V_END)
        rows = sb("rows", 384)
        rowg = sb("rowg", 1024)
        posi = sb("posi", 2, I32)
        posf = sb("posf", 2)
        x = sb("x", 2048)
        hT = sb("hT", 2048)
        ring = sb("ring", NSLOT * SLOT)
        kk = sb("kk", 2048)
        rgw = sb("rgw", 512)
        wf = sb("wf", 832)
        arena = sb("arena", 15360)
        mkv = sb("mkv", 1024)
        osb = sb("osb", 2048)
        work = sb("work", 4096)
        tmp = sb("tmp", 3072)
        junk = sb("junk", 1024)
        cs = sb("cs", 2 * 128)
        sm = sb("sm", 1024)
        smi = sb("smi", 512, U32)
        eidx = sb("eidx", 256, U32)
        hid = sb("hid", 256)
        wexp = sb("wexp", 256)
        diag = sb("diag", 4 * 128)
        diags, ndiag = [Buf(diag[:, 128 * i:128 * i + 128]) for i in range(4)], [0]
        psum = ctx.enter_context(nc.psum_tensor("psum", [P, 4096], F32))
        bank = [Buf(psum[:, 512 * i:512 * i + 512]) for i in range(8)]
        tmps = [Buf(tmp[:, 512 * i:512 * i + 512]) for i in range(6)]

        ident = const[:, K_ID:K_ID + 128]
        mcau = const[:, K_MC:K_MC + 512].rearrange("p (t k) -> p t k", t=2)
        mdil = const[:, K_MD:K_MD + 512].rearrange("p (t k) -> p t k", t=2)
        cdil = const[:, K_CD:K_CD + 512].rearrange("p (t k) -> p t k", t=2)
        ones = const[:, K_ONE:K_ONE + 128]
        iota = const[:, K_IO:K_IO + 16]
        x3 = x[:, :].rearrange("p (t d) -> p t d", t=2)
        hT3 = hT[:, :].rearrange("p (k t) -> p k t", k=8)
        gates = arena[:, 0:6144].rearrange("p (t b d) -> p t b d", t=2, b=3)
        proj = arena[:, 6144:11264].rearrange("p (t d) -> p t d", t=2)
        qkT = arena[:, 11264:15360].rearrange("p (b t) -> p b t", b=16)
        mkv3 = mkv[:, :].rearrange("p (t d) -> p t d", t=2)
        osb3 = osb[:, :].rearrange("p (t d) -> p t d", t=2)
        kk4 = kk[:, :].rearrange("p (a h n) -> p a h n", a=2, h=8)
        rgw4 = rgw[:, :].rearrange("p (a b n) -> p a b n", a=2, b=2)
        wf3 = wf[:, :].rearrange("p (k n) -> p k n", k=8)

        def landing(name):
            return [sem(name), 0]

        def load(queue, landed, dst, src, *after):
            return queue.dma(landed, lambda e: e.dma_start(dst, src), *after)

        ld_x = load(S, landing("l_x"), x3, T["x"].rearrange("(t p) d -> p t d", p=P))
        ld_c = load(A, landing("l_c"), const[:, :], T["const"])
        ld_v = load(A, landing("l_v"), vecs[:, :], T["vecs"])
        mem3 = osb3
        ld_m = load(A, landing("l_m"), mem3, T["mem"].rearrange("(t p) d -> p t d", p=P))
        ld_p = load(A, landing("l_p"), posi[:, :], T["pos"])
        ld_r = load(A, landing("l_r"), rows[:, :], T["rows"][:, 0:384])
        row_landed = [landing(f"l_g{i}") for i in range(ROWS)]
        l_kk, l_rg, l_wf = landing("l_kk"), landing("l_rg"), landing("l_wf")

        def cols(w, c0, n, kb=8, k0=0, at=0, width=512):
            src = w[k0 * P:(k0 + kb) * P, c0:c0 + n].rearrange("(k p) n -> p k n", p=P)
            return lambda slot: (slot[:, 0:kb * width].rearrange("p (k n) -> p k n", k=kb)[:, :, at:at + n], src)

        slabs = [[cols(T["w_in"], 512 * c, 512)] for c in range(5)]
        slabs += [[cols(T["w_mem_kv"], 0, 512)]]
        slabs += [[cols(T["w_in"], 512 * c, 512)] for c in range(5, 11)]
        slabs += [[cols(T["w_branch_moba"], 0, 1024, 3, width=1024)], [cols(T["w_branch_dil"], 0, 1024, 3, width=1024)],
                  [cols(T["w_branch_mem"], 0, 1024, 2, width=1024)]]
        slabs += [[cols(T["w_out"], 512 * c, 512)] for c in range(2)]
        slabs += [[cols(T["w_ffn_up"], 256 * c, 256), cols(T["w_ffn_up"], 2816 + 256 * c, 256, at=256)] for c in range(11)]
        slabs += [[cols(T["w_ffn_down"], 0, 1024, min(4, 22 - k), k, width=1024)] for k in range(0, 22, 4)]
        for l in (0, 0, 1, 1):
            w = T["w_in_2"][l]
            slabs += [[cols(w, c, 512)] for c in (0, 512, 1024, 1544, 2056)]
            slabs += [[cols(T["w_out_2"][l], 512 * c, 512)] for c in range(2)]
            slabs += [[cols(T["peer_wq"][l], 512 * c, 512)] for c in range(4)]

        slot_landed = [landing(f"l_s{i}") for i in range(NSLOT)]
        loaded = []
        taken = [0, 0]

        def fetch(after):
            n = len(loaded)
            if n == len(slabs):
                return
            at = n % NSLOT
            slot = ring[:, at * SLOT:(at + 1) * SLOT]
            for part in slabs[n]:
                dst, src = part(slot)
                step = load(S, slot_landed[at], dst, src, after)
            loaded.append(step)

        for _ in range(NSLOT):
            fetch(None)

        def slab():
            n = taken[0]
            taken[0] += 1
            return ring[:, (n % NSLOT) * SLOT:(n % NSLOT + 1) * SLOT], loaded[n]

        def matmuls(dst, pairs, *after):
            for i, (a, b) in enumerate(pairs):
                step = E(lambda e, a=a, b=b, i=i: e.matmul(dst, a, b, start=(i == 0), stop=(i == len(pairs) - 1)),
                         *(after if i == 0 else ()))
            return step

        turn = [0]

        def evac(dst, src, *after):
            turn[0] += 1
            if turn[0] % 2:
                return A(lambda e: e.activation(dst, src, ACT.Copy), *after)
            return V(lambda e: e.tensor_copy(dst, src), *after)

        def transposes(b, srcs, *after):
            for i, src in enumerate(srcs):
                step = E(lambda e, i=i, src=src: e.transpose(b.ap[:, 128 * i:128 * i + 128], src, ident),
                         ld_c, *(list(after) + b.free if i == 0 else ()))
            return step

        def inv_root(ms, y, t, *after):
            s = A(lambda e: e.activation(y, ms, ACT.Ln), *after)
            s = A(lambda e: e.activation(y, y, ACT.Exp, scale=-0.5), s)
            s = V(lambda e: e.tensor_tensor(t, y, y, ALU.mult), s)
            s = V(lambda e: e.tensor_tensor(t, t, ms, ALU.mult), s)
            s = V(lambda e: e.tensor_scalar(t, t, -0.5, 1.5, ALU.mult, ALU.add), s)
            return V(lambda e: e.tensor_tensor(y, y, t, ALU.mult), s)

        def rms(src3, dst3, at, *after):
            ss, y, t = sm[:, at:at + 2], sm[:, at + 2:at + 4], sm[:, at + 4:at + 6]
            s = [A(lambda e, t_=t_: e.activation(dst3[:, t_, :], src3[:, t_, :], ACT.Square, accum_out=sm[:, at + t_:at + t_ + 1]),
                   *after) for t_ in range(2)]
            s = V(lambda e: e.tensor_scalar(ss, ss, 1.0 / 1024, EPS, ALU.mult, ALU.add), s)
            return y, inv_root(ss, y, t, s)

        def turned(src3, dstT, gain, banks, *after):
            done = []
            for n, (t_, half) in enumerate((a, b) for a in range(2) for b in range(2)):
                b = bank[banks[n % len(banks)]]
                s = transposes(b, [src3[:, t_, 128 * (4 * half + i):128 * (4 * half + i) + 128] for i in range(4)], *after)
                dst = dstT[:, 4 * half:4 * half + 4, 128 * t_:128 * t_ + 128]
                src = b.ap[:, :].rearrange("p (k n) -> p k n", k=4)
                if gain is None:
                    s = evac(dst, src, s)
                else:
                    gg = gain[:, 4 * half:4 * half + 4].unsqueeze(2).to_broadcast([P, 4, 128])
                    s = V(lambda e, dst=dst, src=src, gg=gg: e.tensor_tensor(dst, src, gg, ALU.mult), s, ld_v)
                b.free = [s]
                done.append(s)
            return done

        def scaled(dst3, src3, r, *after):
            return [V(lambda e, t_=t_: e.tensor_scalar(dst3[:, t_, :], src3[:, t_, :], r[:, t_:t_ + 1], None, ALU.mult), *after)
                    for t_ in range(2)]

        def token_major(hT_, ready, banks, use):
            slot, here = slab()
            w = slot[:, :].rearrange("p (k n) -> p k n", k=8)
            for t_ in range(2):
                b = bank[banks[t_]]
                s = matmuls(b.ap[:, :], [(hT_[:, k, 128 * t_:128 * t_ + 128], w[:, k, :]) for k in range(8)], here, ready, b.free)
                b.free = [use(t_, b, s)]
            fetch(s)

        def feature_major(hT_, ready, banks, use):
            slot, here = slab()
            w = slot[:, :].rearrange("p (k n) -> p k n", k=8)
            for j in range(2):
                b = bank[banks[j]]
                for i in range(2):
                    c = 128 * (2 * j + i)
                    s = matmuls(b.ap[:, 256 * i:256 * i + 256], [(w[:, k, c:c + 128], hT_[:, k, :]) for k in range(8)],
                                here, ready, b.free if i == 0 else None)
                b.free = [use(j, b, s)]
            fetch(s)

        def attention(units, out3, free_v, T_b=(2, 3), O_b=(4, 5)):
            S_b = (0, 6)
            Sm, Eb, Pt = tmps[0:2], tmps[2:4], tmps[4:6]
            for b in tmps:
                b.free = b.free + list(_flat([free_v]))
            den = sm[:, 800:864].rearrange("p (t h) -> p t h", t=2)
            mx = sm[:, 864:868].rearrange("p (a h) -> p a h", a=2)
            groups = []
            for u in units:
                if not groups or groups[-1][0] != u["group"]:
                    groups.append((u["group"], []))
                groups[-1][1].append(u)
                u["o"] = bank[O_b[(len(groups) - 1) % len(O_b)]]
                u["first"] = len(groups[-1][1]) == 1
                u["members"] = groups[-1][1]
            done = []

            def scores(i):
                u = units[i]
                t_, nk = u["t"], u["nk"]
                n = S_b[i % 2]
                sm_, e_ = Sm[i % 2], Eb[i % 2]
                s3 = psum[:, 512 * n:512 * n + 1024].rearrange("p (h k) -> p h k", h=2)[:, :, 0:nk]
                d3 = sm_.ap.rearrange("p (h k) -> p h k", h=2)[:, :, 0:nk]
                x3_ = e_.ap.rearrange("p (h k) -> p h k", h=2)[:, :, 0:nk]
                for h in range(2):
                    pairs = [(u["q"](h), u["k"](h))] + ([u["bias"](h)] if u["bias"] else [])
                    s = matmuls(s3[:, h, :], pairs, u["ready"], bank[n + h].free)
                m2 = mx[:, i % 2, :]
                mb = m2.unsqueeze(2).to_broadcast([P, 2, nk])
                src = s3
                if u["mask"] is not None:
                    mk = u["mask"][:, t_, 0:nk].unsqueeze(1).to_broadcast([P, 2, nk])
                    s = V(lambda e: e.tensor_tensor(d3, s3, mk, ALU.add), s, sm_.free)
                    src = d3
                s_m = V(lambda e: e.tensor_reduce(m2, src, AX, ALU.max), s)
                s = V(lambda e: e.tensor_tensor(d3, src, mb, ALU.subtract), s_m, sm_.free)
                bank[n].free = bank[n + 1].free = [s]
                s = A(lambda e: e.activation(x3_, d3, ACT.Exp, scale=0.125), s, e_.free)
                sm_.free = [s]
                u["e"], u["e3"] = s, x3_

            def weights(i):
                u = units[i]
                t_, nk, x3_ = u["t"], u["nk"], u["e3"]
                s = u["e"]
                if u["counts"] is not None:
                    ck = u["counts"][:, t_, 0:nk].unsqueeze(1).to_broadcast([P, 2, nk])
                    s = V(lambda e: e.tensor_tensor(x3_, x3_, ck, ALU.mult), s)
                h0 = u["col"] // 64
                u["den"] = V(lambda e: e.tensor_reduce(den[:, t_, h0:h0 + 2], x3_, AX, ALU.add), s)
                b, pt = bank[T_b[i % len(T_b)]], Pt[i % 2]
                nb = nk // 128
                last = transposes(b, [x3_[:, h, 128 * c:128 * c + 128] for h in range(2) for c in range(nb)], s)
                Eb[i % 2].free = [last, u["den"]]
                p_ = pt.ap[:, 0:256 * nb]
                s = A(lambda e: e.activation(p_, b.ap[:, 0:256 * nb], ACT.Copy), last, pt.free)
                b.free = [s]
                u["p"], u["p3"] = s, p_.rearrange("p (h c q) -> p h c q", h=2, c=nb)

            def values(i):
                u = units[i]
                o, nb = u["o"], u["nk"] // 128
                for h in range(2):
                    c0 = u["col"] - u["members"][0]["col"] + 64 * h
                    s = matmuls(o.ap[:, c0:c0 + 64], [(u["p3"][:, h, c, :], u["v"](h, c)) for c in range(nb)],
                                u["p"], o.free if u["first"] and h == 0 else None)
                Pt[i % 2].free = [s]
                if u is u["members"][-1]:
                    t_, n = u["t"], 2 * len(u["members"])
                    c0 = u["members"][0]["col"]
                    dd = den[:, t_, c0 // 64:c0 // 64 + n]
                    r = V(lambda e: e.reciprocal(dd, dd), u["den"])
                    o3 = o.ap[:, 0:64 * n].rearrange("p (h d) -> p h d", h=n)
                    y3 = out3[:, t_, c0:c0 + 64 * n].rearrange("p (h d) -> p h d", h=n)
                    rb = dd.unsqueeze(2).to_broadcast([P, n, 64])
                    r = V(lambda e: e.tensor_tensor(y3, o3, rb, ALU.mult), r, s)
                    o.free = [r]
                    done.append(r)

            for i in range(len(units) + 2):
                if i < len(units):
                    scores(i)
                    yield
                if 1 <= i <= len(units):
                    weights(i - 1)
                    yield
                if i >= 2:
                    values(i - 2)
            return done

        def whole(steps):
            while True:
                try:
                    next(steps)
                except StopIteration as end:
                    return end.value

        def add_to_x(t_, half, b, s):
            d = x3[:, t_, 512 * half:512 * half + 512]
            return V(lambda e: e.tensor_tensor(d, d, b.ap[:, :], ALU.add), s)

        s = V(lambda e: e.tensor_copy(posf[:, :], posi[:, :]), ld_p)
        ang, kf = junk[:, 0:128].rearrange("p (a t f) -> p a t f", a=2, t=2), junk[:, 128:256].rearrange("p (a t f) -> p a t f", a=2, t=2)
        invf = const[:, K_IF:K_IF + 32]
        ss = []
        for t_ in range(2):
            a0 = V(lambda e, t_=t_: e.tensor_scalar(ang[:, 0, t_, :], invf, posf[:, t_:t_ + 1], None, ALU.mult), s, ld_c)
            ss.append(V(lambda e, t_=t_: e.tensor_copy(ang[:, 1, t_, :], ang[:, 0, t_, :]), a0))
        for a in range(2):
            s1 = V(lambda e, a=a: e.tensor_scalar(kf[:, a], ang[:, a], 1.0 / TWO_PI, 0.25 * a, ALU.mult, ALU.add), ss)
            s1 = V(lambda e, a=a: e.tensor_scalar(kf[:, a], kf[:, a], MAGIC, None, ALU.add), s1)
            s1 = V(lambda e, a=a: e.tensor_scalar(kf[:, a], kf[:, a], -MAGIC, None, ALU.add), s1)
            for c in (C1, C2, C3):
                s1 = V(lambda e, a=a, c=c: e.scalar_tensor_tensor(ang[:, a], kf[:, a], -c, ang[:, a], ALU.mult, ALU.add), s1)
            if a:
                s1 = V(lambda e, a=a: e.tensor_scalar(ang[:, a], ang[:, a], TWO_PI / 4, None, ALU.add), s1)
            s1 = V(lambda e, a=a: e.tensor_scalar(ang[:, a], ang[:, a], 3.1415925, -3.1415925, ALU.min, ALU.max), s1)
            s1 = A(lambda e, a=a: e.activation(ang[:, a], ang[:, a], ACT.Sin), s1)
            ss.append(s1)
        cs4 = cs[:, :].rearrange("p (t c f) -> p t c f", t=2, c=4)
        cs_ready = [V(lambda e, c=c: e.tensor_copy(cs4[:, :, c, :], ang[:, 1]), ss) for c in range(2)]
        cs_ready.append(V(lambda e: e.tensor_scalar(cs4[:, :, 2, :], ang[:, 0], -1.0, None, ALU.mult), ss))
        cs_ready.append(V(lambda e: e.tensor_copy(cs4[:, :, 3, :], ang[:, 0]), ss))

        xs = arena[:, 0:2048].rearrange("p (t d) -> p t d", t=2)
        ms_ = arena[:, 2048:4096].rearrange("p (t d) -> p t d", t=2)
        memT = qkT[:, 0:8, :]
        r, s = rms(x3, xs, 0, ld_x, cs_ready)
        s = scaled(xs, x3, r, s)
        h_ready = turned(xs, hT3, vecs[:, V_MIX:V_MIX + 8], (6, 7), s)
        r, s = rms(mem3, ms_, 8, ld_m, cs_ready)
        s_ms = scaled(ms_, mem3, r, s)
        mem_ready = turned(ms_, memT, vecs[:, V_MEM:V_MEM + 8], (4, 5), s_ms)

        qkv = []
        for c in range(5):
            def use(t_, b, s, c=c):
                qkv.append(evac(proj[:, t_, 512 * c:512 * c + 512], b.ap[:, :], s))
                return qkv[-1]
            token_major(hT3, h_ready, ((0, 1), (2, 3))[c % 2], use)

        mem_done = []
        def use(t_, b, s):
            mem_done.append(evac(mkv3[:, t_, :], b.ap[:, :], s))
            return mem_done[-1]
        token_major(memT, mem_ready, (2, 3), use)

        gates_done = []
        for c in range(6):
            def use(t_, b, s, c=c):
                d = gates[:, t_, c // 2, 512 * (c % 2):512 * (c % 2) + 512]
                gates_done.append(A(lambda e: e.activation(d, b.ap[:, :], ACT.Sigmoid), s, mem_ready, h_ready))
                return gates_done[-1]
            token_major(hT3, h_ready, ((0, 1), (2, 3))[c % 2], use)

        def seg(src, h0, n, at, g):
            return [(t_, src[:, t_, 64 * h0:64 * (h0 + n)].rearrange("p (h d) -> p h d", h=n), n, at, g) for t_ in range(2)]
        segs = (seg(proj, 0, 6, 0, 0) + seg(proj, 6, 6, 6, 1) + seg(proj, 18, 6, 12, 2) + seg(proj, 24, 6, 18, 3)
                + seg(proj, 36, 4, 24, 4) + seg(mkv3, 0, 4, 28, 5))
        hs = sm[:, 16:80].rearrange("p (t h) -> p t h", t=2)
        hy = sm[:, 80:144].rearrange("p (t h) -> p t h", t=2)
        s_sum = []
        sq = [Buf(tmp[:, 384 * i:384 * i + 384]) for i in range(8)]
        for i, (t_, v3, n, at, g) in enumerate(segs):
            q = sq[i % 2]
            q3 = q.ap[:, 0:64 * n].rearrange("p (h d) -> p h d", h=n)
            s = V(lambda e, q3=q3, v3=v3: e.tensor_tensor(q3, v3, v3, ALU.mult), qkv, mem_done, q.free)
            s = V(lambda e, q3=q3, t_=t_, at=at, n=n: e.tensor_reduce(hs[:, t_, at:at + n], q3, AX, ALU.add), s)
            q.free = [s]
            s_sum.append(s)
        s = V(lambda e: e.tensor_scalar(sm[:, 16:80], sm[:, 16:80], 1.0 / 64, EPS, ALU.mult, ALU.add), s_sum)
        s_inv = inv_root(sm[:, 16:80], sm[:, 80:144], sm[:, 144:208], s)
        normed = {}
        for i, (t_, v3, n, at, g) in enumerate(segs):
            rb = hy[:, t_, at:at + n].unsqueeze(2).to_broadcast([P, n, 64])
            gb = rows[:, B_HEAD + 64 * g:B_HEAD + 64 * g + 64].unsqueeze(1).to_broadcast([P, n, 64])
            s = V(lambda e, v3=v3, rb=rb: e.tensor_tensor(v3, v3, rb, ALU.mult), s_inv)
            s = V(lambda e, v3=v3, gb=gb: e.tensor_tensor(v3, v3, gb, ALU.mult), s, ld_r)
            if g < 4:
                q = sq[2 + i % 2]
                q3 = q.ap[:, :].rearrange("p (h d) -> p h d", h=n)
                cc = cs4[:, t_, 0:2, :].rearrange("p c f -> p (c f)").unsqueeze(1).to_broadcast([P, n, 64])
                ns = cs4[:, t_, 2, :].unsqueeze(1).to_broadcast([P, n, 32])
                ps_ = cs4[:, t_, 3, :].unsqueeze(1).to_broadcast([P, n, 32])
                s1 = V(lambda e, q3=q3, v3=v3, ns=ns: e.tensor_tensor(q3[:, :, 0:32], v3[:, :, 32:64], ns, ALU.mult), s, q.free)
                s2 = V(lambda e, q3=q3, v3=v3, ps_=ps_: e.tensor_tensor(q3[:, :, 32:64], v3[:, :, 0:32], ps_, ALU.mult), s)
                s3 = V(lambda e, v3=v3, cc=cc: e.tensor_tensor(v3, v3, cc, ALU.mult), s1, s2)
                s = V(lambda e, v3=v3, q3=q3: e.tensor_tensor(v3, v3, q3, ALU.add), s3)
                q.free = [s]
            normed[(g, t_)] = s

        pair_at = {0: 0, 1: 3, 2: 6, 3: 9, 4: 12, 5: 14}
        src_of = {0: (proj, 0, 3), 1: (proj, 384, 3), 2: (proj, 1152, 3), 3: (proj, 1536, 3), 4: (proj, 2304, 2), 5: (mkv3, 0, 2)}
        todo = [(g, j) for g in range(6) for j in range(src_of[g][2])]
        qk_ready = []
        for n in range(0, 16, 2):
            b = bank[6 + (n // 2) % 2]
            srcs, waits = [], []
            for g, j in todo[n:n + 2]:
                sr, c, _ = src_of[g]
                for t_ in range(2):
                    srcs.append(sr[:, t_, c + 128 * j:c + 128 * j + 128])
                    waits.append(normed[(g, t_)])
            s = transposes(b, srcs, waits)
            s = evac(qkT[:, n:n + 2, :].rearrange("p b t -> p (b t)"), b.ap[:, :], s, mem_done)
            b.free = [s]
            qk_ready.append(s)

        units = []
        for g, (qg, kg, n, col, vsrc, mask, counts) in enumerate((
                (0, 1, 3, 0, (proj, 768), mcau, None), (2, 3, 3, 384, (proj, 1920), mdil, cdil), (4, 5, 2, 768, (mkv3, 256), None, None))):
            for t_ in range(2):
                for j in range(n):
                    nk = 128 if t_ == 0 and mask is not None else 256
                    def q(h, p_=pair_at[qg] + j, t_=t_):
                        return qkT[64 * h:64 * h + 64, p_, 128 * t_:128 * t_ + 128]
                    def k(h, p_=pair_at[kg] + j, nk=nk):
                        return qkT[64 * h:64 * h + 64, p_, 0:nk]
                    def v(h, c, j=j, vs=vsrc):
                        return vs[0][:, c, vs[1] + 128 * j + 64 * h:vs[1] + 128 * j + 64 * h + 64]
                    units.append(dict(group=(g, t_), col=col + 128 * j, t=t_, nk=nk, q=q, k=k, v=v, mask=mask, counts=counts,
                                      bias=None, ready=qk_ready))
        att = attention(units, osb3, [list(normed.values()), s_ms])
        att = whole(att)

        oT = qkT[:, 0:8, :]
        s_oT = turned(osb3, oT, None, (6, 7), att)
        merged = proj[:, :, 0:1024]
        merge = []
        held = {}
        for br, (kb, k0) in enumerate(((3, 0), (3, 3), (2, 6))):
            slot, here = slab()
            w = slot[:, 0:kb * 1024].rearrange("p (k n) -> p k n", k=kb)
            for t_ in range(2):
                for half in range(2):
                    b = bank[2 * t_ + half + 4 * (br % 2)]
                    c = slice(512 * half, 512 * half + 512)
                    s_last = matmuls(b.ap[:, :], [(oT[:, k0 + k, 128 * t_:128 * t_ + 128], w[:, k, c]) for k in range(kb)],
                                     here, s_oT, b.free)
                    m, gt = merged[:, t_, c], gates[:, t_, br, c]
                    if br == 0:
                        s = V(lambda e, m=m, gt=gt, b=b: e.tensor_tensor(m, b.ap[:, :], gt, ALU.mult), s_last, gates_done)
                        b.free = [s]
                    else:
                        s = V(lambda e, gt=gt, b=b: e.tensor_tensor(gt, b.ap[:, :], gt, ALU.mult), s_last, gates_done)
                        b.free = [s]
                        s = V(lambda e, m=m, gt=gt: e.tensor_tensor(m, m, gt, ALU.add), s, held[(t_, half)])
                    held[(t_, half)] = s
            fetch(s_last)
        mT = turned(merged, hT3, None, (6, 7), list(held.values()))
        xs_done = []
        for c in range(2):
            def use(t_, b, s, c=c):
                xs_done.append(add_to_x(t_, c, b, s))
                return xs_done[-1]
            token_major(hT3, mT, ((0, 1), (2, 3))[c], use)

        xs = proj[:, :, 0:1024]
        r, s = rms(x3, xs, 0, xs_done, mT)
        s = scaled(xs, x3, r, s, mT)
        h_ready = turned(xs, hT3, vecs[:, V_FFN:V_FFN + 8], (6, 7), s, xs_done)
        act = arena[:, 0:5632].rearrange("p (f t) -> p f t", f=22)
        ub = [Buf(tmp[:, 512 * i:512 * i + 512]) for i in range(6)]
        act_done = []
        for c in range(11):
            slot, here = slab()
            w = slot[:, :].rearrange("p (k n) -> p k n", k=8)
            for i in range(2):
                f = 2 * c + i
                b, u = bank[f % 4], ub[f % 3]
                for gv in range(2):
                    cw = 256 * gv + 128 * i
                    s = matmuls(b.ap[:, 256 * gv:256 * gv + 256], [(w[:, k, cw:cw + 128], hT3[:, k, :]) for k in range(8)],
                                here, h_ready, b.free if gv == 0 else None)
                taps, first = [], []
                for gv in range(2):
                    j = f + 22 * gv
                    ps_, d = b.ap[:, 256 * gv:256 * gv + 256], u.ap[:, 256 * gv:256 * gv + 256]
                    wv = vecs[:, V_CW + 3 * j:V_CW + 3 * j + 3]
                    bv = vecs[:, V_CB + j:V_CB + j + 1]
                    first.append(A(lambda e, d=d, ps_=ps_, wv=wv, bv=bv: e.activation(
                        d, ps_, ACT.Identity, bias=bv, scale=wv[:, 2:3]), s, u.free, att))
                for gv in range(2):
                    j = f + 22 * gv
                    ps_, d = b.ap[:, 256 * gv:256 * gv + 256], u.ap[:, 256 * gv:256 * gv + 256]
                    wv = vecs[:, V_CW + 3 * j:V_CW + 3 * j + 3]
                    q = first
                    for k in (1, 2):
                        q = V(lambda e, d=d, ps_=ps_, wv=wv, k=k: e.scalar_tensor_tensor(
                            d[:, k:256], ps_[:, 0:256 - k], wv[:, 2 - k:3 - k], d[:, k:256], ALU.mult, ALU.add), q)
                    taps.append(q)
                b.free = taps
                d = u.ap[:, 0:256]
                q = A(lambda e, d=d: e.activation(d, d, ACT.Silu), taps[0])
                q = V(lambda e, u=u, f=f: e.tensor_tensor(act[:, f, :], u.ap[:, 0:256], u.ap[:, 256:512], ALU.mult), q, taps[1])
                u.free = [q]
                act_done.append(q)
            fetch(s)
        for c in range(6):
            slot, here = slab()
            kb = min(4, 22 - 4 * c)
            w = slot[:, 0:kb * 1024].rearrange("p (k n) -> p k n", k=kb)
            for k in range(kb):
                f = 4 * c + k
                for t_ in range(2):
                    for half in range(2):
                        b = bank[4 + 2 * t_ + half]
                        s = E(lambda e, b=b, f=f, t_=t_, half=half, w=w, k=k: e.matmul(
                            b.ap[:, :], act[:, f, 128 * t_:128 * t_ + 128], w[:, k, 512 * half:512 * half + 512],
                            start=(f == 0), stop=(f == 21)), here, act_done[f], b.free if f == 0 else None)
            fetch(s)
        ready = []
        for t_ in range(2):
            for half in range(2):
                b = bank[4 + 2 * t_ + half]
                q = add_to_x(t_, half, b, s)
                b.free = [q]
                ready.append(q)
        prior = [act_done, s, h_ready]

        def log1p(e_, z, z2, p_, *after):
            s = V(lambda e: e.tensor_scalar(z, e_, 2.0, None, ALU.add), *after)
            s = V(lambda e: e.reciprocal(z, z), s)
            s = V(lambda e: e.tensor_tensor(z, z, e_, ALU.mult), s)
            s = V(lambda e: e.tensor_tensor(z2, z, z, ALU.mult), s)
            s = V(lambda e: e.tensor_scalar(p_, z2, 2.0 / 19, None, ALU.mult), s)
            for n in range(17, 1, -2):
                s = V(lambda e, n=n: e.scalar_tensor_tensor(p_, p_, 2.0 / n, z2, ALU.add, ALU.mult), s)
            return V(lambda e: e.scalar_tensor_tensor(p_, p_, 2.0, z, ALU.add, ALU.mult), s)

        l_row = landing("l_row")
        xs = work[:, 0:1024]
        o_t = work[:, 0:512]
        qT = work[:, 1024:1536].rearrange("p (b t) -> p b t", b=4)
        kT = work[:, 1536:2560].rearrange("p (b t) -> p b t", b=4)
        ypad = work[:, 2560:3132].rearrange("p (b t) -> p b t", b=2)
        xpad = work[:, 3132:3650].rearrange("p (b t) -> p b t", b=2)
        cum = work[0:104, 3650:3906]
        hlast = work[:, 3906:3908]
        hTt = hT[:, 0:1024].rearrange("p (k t) -> p k t", k=8)
        mixT = hT[:, 1024:2048].rearrange("p (k t) -> p k t", k=8)
        base = 1024 * ROWS
        Lh = arena[0:104, base:base + 512].rearrange("p (h t) -> p h t", h=4)
        R = arena[0:104, base + 512:base + 768]
        fz, fa, fe, f1, f2, f3 = (arena[0:104, base + 768 + 128 * i:base + 896 + 128 * i] for i in range(6))
        gg, gr, yc, xc = (arena[:, base + 1536 + 256 * i:base + 1792 + 256 * i] for i in range(4))
        b2 = lambda ap: ap.rearrange("p (b t) -> p b t", b=2)
        row_y = [osb[:, 1024 * t_:1024 * t_ + 1024] for t_ in range(2)]
        top = sm[:, 0:256].rearrange("p (a h k) -> p a h k", a=2, h=8)
        topi = smi[:, 0:256].rearrange("p (a h k) -> p a h k", a=2, h=8)
        topf = junk[:, 0:256].rearrange("p (a h k) -> p a h k", a=2, h=8)
        best = sm[:, 256:384].rearrange("p (h k) -> p h k", h=8)
        besti = smi[:, 256:384].rearrange("p (h k) -> p h k", h=8)
        hilo = smi[:, 384:512]
        hf = junk[:, 256:512].rearrange("p (a h k) -> p a h k", a=2, h=8)
        ef = junk[:, 512:768].rearrange("p (a h k) -> p a h k", a=2, h=8)
        cand = tmp[:, 2048:3072]
        qp = tmp[:, 0:2048].rearrange("p (b t) -> p b t", b=16)
        gate = [sm[:, 384 + 128 * t_:512 + 128 * t_] for t_ in range(2)]
        left = dict(kk=None, rg=None, wf=None, row=None, mixer=prior, x=[list(ready), list(ready)], cum=None, h=None)
        routed = {}
        landed_l = {}

        def feature_tile(b, hT_, after):
            slot, here = slab()
            w = slot[:, :].rearrange("p (k n) -> p k n", k=8)
            for i in range(4):
                s = matmuls(b.ap[:, 128 * i:128 * i + 128], [(w[:, k, 128 * i:128 * i + 128], hT_[:, k, :]) for k in range(8)],
                            here, after, b.free if i == 0 else None)
                yield
            fetch(s)
            return s

        def token_tile(b, hT_, after):
            slot, here = slab()
            w = slot[:, :].rearrange("p (k n) -> p k n", k=8)
            for k in range(8):
                s = E(lambda e, k=k: e.matmul(b.ap[:, :], hT_[:, k, :], w[:, k, :], start=(k == 0), stop=(k == 7)),
                      *([here, after, b.free] if k == 0 else []))
                if k % 2:
                    yield
            fetch(s)
            return s

        def inv_root_tile(ms, y, t, *after):
            s = A(lambda e: e.activation(y, ms, ACT.Ln), *after)
            s = A(lambda e: e.activation(y, y, ACT.Exp, scale=-0.5), s)
            yield
            s = V(lambda e: e.tensor_tensor(t, y, y, ALU.mult), s)
            s = V(lambda e: e.tensor_tensor(t, t, ms, ALU.mult), s)
            s = V(lambda e: e.tensor_scalar(t, t, -0.5, 1.5, ALU.mult, ALU.add), s)
            return V(lambda e: e.tensor_tensor(y, y, t, ALU.mult), s)

        def rms_tile(t_, scratch, *after):
            ss, y, t = (sm[:, 640 + 3 * t_ + i:641 + 3 * t_ + i] for i in range(3))
            s = A(lambda e: e.activation(scratch, x3[:, t_, :], ACT.Square, accum_out=ss), *after)
            yield
            s = V(lambda e: e.tensor_scalar(ss, ss, 1.0 / 1024, EPS, ALU.mult, ALU.add), s)
            s = yield from inv_root_tile(ss, y, t, s)
            return y, s

        def turn_tile(src, gain, banks, after):
            done = []
            for half in range(2):
                b = bank[banks[half]]
                s = transposes(b, [src[:, 128 * (4 * half + i):128 * (4 * half + i) + 128] for i in range(4)], after)
                yield
                dst, src4 = hTt[:, 4 * half:4 * half + 4, :], b.ap[:, :].rearrange("p (k n) -> p k n", k=4)
                if gain is None:
                    s = A(lambda e: e.activation(dst, src4, ACT.Copy), s)
                else:
                    g_ = gain[:, 4 * half:4 * half + 4].unsqueeze(2).to_broadcast([P, 4, 128])
                    s = V(lambda e: e.tensor_tensor(dst, src4, g_, ALU.mult), s)
                b.free = [s]
                done.append(s)
            yield
            return done

        def mixer(l, t_):
            lv = V_L + L_END * l
            if t_ == 0:
                landed_l["kk"] = load(S, l_kk, kk[:, :], T["keys"][l], left["kk"])
                landed_l["rg"] = load(S, l_rg, rgw[:, :], T["rgw"][l], left["rg"])
                landed_l["wf"] = load(S, l_wf, wf[:, :], T["wf"][l], left["wf"])
                landed_l["row"] = load(S, l_row, rowg[:, :], T["rows"][:, B_N2 + 1024 * l:B_N2 + 1024 * l + 1024], left["row"])
            tok = slice(128 * t_, 128 * t_ + 128)
            for q in (V, A, E):
                q.wait(left["mixer"])
            r, s = yield from rms_tile(t_, xs, left["x"][t_])
            s = V(lambda e: e.tensor_scalar(xs, x3[:, t_, :], r, None, ALU.mult), s)
            yield
            h_ready = yield from turn_tile(xs, vecs[:, V_N1 + 8 * l:V_N1 + 8 * l + 8], (6, 7), s)

            four = lambda b: b.ap[:, :].rearrange("p (b t) -> p b t", b=4)
            s = yield from feature_tile(bank[0], hTt, h_ready)
            q_done = A(lambda e: e.activation(qT, four(bank[0]), ACT.Copy), s)
            bank[0].free = [q_done]
            s = yield from feature_tile(bank[1], hTt, h_ready)
            k_done = A(lambda e: e.activation(kT[:, :, tok], four(bank[1]), ACT.Copy), s)
            bank[1].free = [k_done]
            s = yield from token_tile(bank[2], hTt, h_ready)
            v_done = A(lambda e: e.activation(mkv3[:, t_, :], bank[2].ap[:, :], ACT.Copy), s)
            bank[2].free = [v_done]

            b = bank[3]
            s_f = matmuls(b.ap[0:104, 0:128], [(wf3[:, k, :], hTt[:, k, :]) for k in range(8)], landed_l["wf"], b.free)
            left["wf"] = s_f
            yield
            s = V(lambda e: e.tensor_scalar(fz, b.ap[0:104, 0:128], vecs[0:104, lv + L_BF:lv + L_BF + 1], None, ALU.add), s_f)
            b.free = [s]
            s = V(lambda e: e.tensor_scalar(fa, fz, -1.0, None, ALU.mult), s)
            s = V(lambda e: e.tensor_tensor(fa, fa, fz, ALU.max), s)
            s_e = A(lambda e: e.activation(fe, fa, ACT.Exp, scale=-1.0), s)
            yield
            s = log1p(fe, f1, f2, f3, s_e)
            yield
            s = V(lambda e: e.scalar_tensor_tensor(fz, fz, 0.0, f3, ALU.min, ALU.subtract), s)
            s = V(lambda e: e.memset(f2, 1.0), s)
            start = cum[:, 127:128] if t_ else 0.0
            s = V(lambda e: e.tensor_tensor_scan(cum[:, tok], f2, fz, start, ALU.mult, ALU.add), s, left["cum"])
            left["cum"] = s
            lr = [V(lambda e: e.tensor_scalar(Lh[:, h, :], cum[:, tok], const[0:104, K_SEL + h:K_SEL + h + 1],
                                              const[0:104, K_SEL + 5 + h:K_SEL + 6 + h], ALU.mult, ALU.add), s) for h in range(4)]
            lr.append(V(lambda e: e.tensor_scalar(R[:, tok], cum[:, tok], const[0:104, K_SEL + 4:K_SEL + 5],
                                                  const[0:104, K_SEL + 9:K_SEL + 10], ALU.mult, ALU.add), s))
            yield

            z1 = z2 = None
            if t_ == 0:
                z1 = V(lambda e: e.memset(ypad[:, :, 0:30], 0.0))
                z2 = V(lambda e: e.memset(xpad[:, :, 0:3], 0.0))
            b = bank[0]
            s = yield from feature_tile(b, hTt, h_ready)
            s = A(lambda e: e.activation(gg, b.ap[:, 256:512], ACT.Sigmoid), s)
            yield
            s_y = V(lambda e: e.tensor_tensor(ypad[:, :, 30 + 128 * t_:158 + 128 * t_], b2(b.ap[:, 0:256]), b2(gg), ALU.mult), s)
            b.free = [s_y]
            b = bank[1]
            s = yield from feature_tile(b, hTt, h_ready)
            s_gr = A(lambda e: e.activation(gr, b.ap[:, 256:512], ACT.Gelu_apprx_tanh), s)
            yield
            s_x = V(lambda e: e.tensor_copy(xpad[:, :, 3 + 128 * t_:131 + 128 * t_], b2(b.ap[:, 0:256])), s_gr)
            b.free = [s_x]

            w = vecs[:, lv + L_RW:lv + L_RW + 8].rearrange("p (b k) -> p b k", b=2)
            o = 128 * t_
            xcd = []
            for bl in range(2):
                d = xc[:, 128 * bl:128 * bl + 128]
                s = V(lambda e: e.tensor_scalar(d, xpad[:, bl, 3 + o:131 + o], w[:, bl, 3:4],
                                                vecs[:, lv + L_RB + bl:lv + L_RB + bl + 1], ALU.mult, ALU.add), s_x, z2)
                for k in range(3):
                    s = V(lambda e: e.scalar_tensor_tensor(d, xpad[:, bl, k + o:k + o + 128], w[:, bl, k:k + 1], d,
                                                           ALU.mult, ALU.add), s)
                xcd.append(s)
                yield
            b = bank[2]
            for g in range(2):
                for bl in range(2):
                    c = 256 * g + 128 * bl
                    s = matmuls(b.ap[:, c:c + 128], [(rgw4[:, g, bl, :], xc[:, 128 * bl:128 * bl + 128])],
                                landed_l["rg"], xcd, b.free if c == 0 else None)
            left["rg"] = s
            yield
            ri = tmp[:, 0:512]
            acts = []
            for g in range(2):
                for bl in range(2):
                    c = lv + (L_BR, L_BI)[g] + bl
                    at = slice(256 * g + 128 * bl, 256 * g + 128 * bl + 128)
                    acts.append(A(lambda e: e.activation(ri[:, at], b.ap[:, at], ACT.Sigmoid, bias=vecs[:, c:c + 1]), s))
            b.free = acts
            lam = vecs[:, lv + L_LAM:lv + L_LAM + 2]
            l0, l1, l2, l3, l4 = (sm[:, 700 + 2 * i:702 + 2 * i] for i in range(5))
            s = V(lambda e: e.tensor_scalar(l0, lam, -1.0, None, ALU.mult))
            s = V(lambda e: e.tensor_tensor(l1, l0, lam, ALU.max), s)
            s = A(lambda e: e.activation(l1, l1, ACT.Exp, scale=-1.0), s)
            yield
            s = log1p(l1, l2, l3, l4, s)
            s = V(lambda e: e.scalar_tensor_tensor(l4, l0, 0.0, l4, ALU.max, ALU.add), s)
            s_c = V(lambda e: e.tensor_scalar(l4, l4, 8.0, None, ALU.mult), s)
            yield
            nl, ii, aa, tt, dd = ri[:, 0:256], ri[:, 256:512], tmp[:, 512:768], tmp[:, 768:1024], tmp[:, 1024:1280]
            s = [V(lambda e: e.tensor_scalar(nl[:, 128 * bl:128 * bl + 128], nl[:, 128 * bl:128 * bl + 128], l4[:, bl:bl + 1],
                                             None, ALU.mult), s_c, acts) for bl in range(2)]
            s_a = A(lambda e: e.activation(aa, nl, ACT.Exp, scale=-1.0), s)
            s = A(lambda e: e.activation(tt, nl, ACT.Tanh), s)
            s1 = V(lambda e: e.tensor_tensor(ii, ii, xc, ALU.mult), acts)
            yield
            s = V(lambda e: e.tensor_scalar(dd, tt, 0.5, 0.5, ALU.mult, ALU.add), s)
            s = V(lambda e: e.reciprocal(dd, dd), s)
            s = V(lambda e: e.tensor_tensor(tt, tt, dd, ALU.mult), s)
            s = A(lambda e: e.activation(tt, tt, ACT.Sqrt), s)
            yield
            s = V(lambda e: e.tensor_tensor(tt, tt, ii, ALU.mult), s, s1)
            s = [V(lambda e: e.tensor_tensor_scan(dd[:, 128 * bl:128 * bl + 128], aa[:, 128 * bl:128 * bl + 128],
                                                  tt[:, 128 * bl:128 * bl + 128], hlast[:, bl:bl + 1] if t_ else 0.0,
                                                  ALU.mult, ALU.add), s, s_a, left["h"]) for bl in range(2)]
            if t_ == 0:
                left["h"] = V(lambda e: e.tensor_copy(hlast, b2(dd)[:, :, 127]), s)
            s_rnn = V(lambda e: e.tensor_tensor(mixT[:, 6:8, :].rearrange("p b t -> p (b t)"), dd, gr, ALU.mult), s, s_gr)
            yield

            w31 = vecs[:, lv + L_DW:lv + L_DW + 62].rearrange("p (b k) -> p b k", b=2)
            cd = []
            for bl in range(2):
                d = yc[:, 128 * bl:128 * bl + 128]
                s = V(lambda e: e.tensor_scalar(d, ypad[:, bl, 30 + o:158 + o], w31[:, bl, 30:31],
                                                vecs[:, lv + L_DB + bl:lv + L_DB + bl + 1], ALU.mult, ALU.add), s_y, z1)
                for k in range(30):
                    s = V(lambda e: e.scalar_tensor_tensor(d, ypad[:, bl, k + o:k + o + 128], w31[:, bl, k:k + 1], d,
                                                           ALU.mult, ALU.add), s)
                    if k % 6 == 5:
                        yield
                cd.append(s)
            b = bank[3]
            s = matmuls(b.ap[:, 0:128], [(ones, yc[:, 128 * bl:128 * bl + 128]) for bl in range(2)], cd, b.free)
            yield
            mean, var, rr, r2 = (junk[:, 128 * i:128 * i + 128] for i in range(4))
            twice = lambda ap: ap.unsqueeze(1).to_broadcast([P, 2, 128])
            s = V(lambda e: e.tensor_scalar(mean, b.ap[:, 0:128], 1.0 / 256, None, ALU.mult), s)
            b.free = [s]
            s_d = V(lambda e: e.tensor_tensor(b2(yc), b2(yc), twice(mean), ALU.subtract), s)
            sq3 = junk[:, 512:768]
            s = V(lambda e: e.tensor_tensor(sq3, yc, yc, ALU.mult), s_d)
            s = matmuls(b.ap[:, 0:128], [(ones, sq3[:, 128 * bl:128 * bl + 128]) for bl in range(2)], s)
            yield
            s = V(lambda e: e.tensor_scalar(var, b.ap[:, 0:128], 1.0 / 256, EPS, ALU.mult, ALU.add), s)
            b.free = [s]
            s = yield from inv_root_tile(var, rr, r2, s)
            s = V(lambda e: e.tensor_tensor(b2(yc), b2(yc), twice(rr), ALU.mult), s)
            s_conv = [A(lambda e: e.activation(mixT[:, 4 + bl, :], yc[:, 128 * bl:128 * bl + 128], ACT.Silu,
                                               bias=vecs[:, lv + L_B + bl:lv + L_B + bl + 1],
                                               scale=vecs[:, lv + L_G + bl:lv + L_G + bl + 1]), s) for bl in range(2)]
            yield

            units = []
            nk = 128 * (t_ + 1)
            for j in range(4):
                units.append(dict(
                    group=0, col=128 * j, t=t_, nk=nk, mask=mcau, counts=None, ready=[q_done, k_done, v_done, lr],
                    q=lambda h, j=j: qT[64 * h:64 * h + 64, j, :],
                    k=lambda h, j=j: kT[64 * h:64 * h + 64, j, 0:nk],
                    v=lambda h, c, j=j: mkv3[:, c, 128 * j + 64 * h:128 * j + 64 * h + 64],
                    bias=lambda h, j=j: (Lh[64 * h:64 * h + 40, j, :], R[64 * h:64 * h + 40, 0:nk])))
            att = yield from attention(units, o_t.unsqueeze(1).to_broadcast([P, 2, 512]), [s_rnn, s_conv, acts],
                                       (2,), (3,))
            yield
            b = bank[0]
            s = transposes(b, [o_t[:, 128 * i:128 * i + 128] for i in range(4)], att)
            s_o = A(lambda e: e.activation(mixT[:, 0:4, :], four(b), ACT.Copy), s)
            b.free = [s_o]
            yield
            mix_ready = [s_o, s_rnn, s_conv]
            added = []
            for c in range(2):
                b = bank[6 + c]
                s = yield from token_tile(b, mixT, mix_ready)
                added.append(add_to_x(t_, c, b, s))
                b.free = [added[-1]]
                yield

            xn = row_y[t_]
            r, s = yield from rms_tile(t_, xn, added, left.get(("xn", t_)))
            s = V(lambda e: e.scalar_tensor_tensor(xn, x3[:, t_, :], r, rowg[:, :], ALU.mult, ALU.mult), s, landed_l["row"])
            left["row"] = s
            xn_done[(l, t_)] = s
            yield
            h_ready = yield from turn_tile(xn, None, (6, 7), s)
            qpd = []
            for c in range(4):
                b = bank[c]
                s = yield from feature_tile(b, hTt, h_ready)
                qpd.append(A(lambda e: e.activation(qp[:, 4 * c:4 * c + 4, :], four(b), ACT.Copy), s, att))
                b.free = [qpd[-1]]
            yield
            for a in range(2):
                for hh in range(2):
                    b = bank[2 * a + hh]
                    for h in range(4):
                        s = matmuls(b.ap[:, 128 * h:128 * h + 128],
                                    [(qp[:, 2 * (4 * hh + h) + a, :], kk4[:, a, 4 * hh + h, :])],
                                    landed_l["kk"], qpd, b.free if h == 0 else None)
                    b.scores = s
                    yield
            left["kk"] = s
            rests = [Buf(xs[:, 256 * i:256 * i + 256]) for i in range(4)]
            turns = [0]

            def top16(vals, ids, src, after):
                rest = rests[turns[0] % 4]
                turns[0] += 1
                rr_ = rest.ap[:, 0:src.shape[-1]]
                q1 = V(lambda e: e.max(vals[:, 0:8], src), after)
                V(lambda e: e.max_index(ids[:, 0:8], vals[:, 0:8], src), q1)
                q3 = V(lambda e: e.match_replace(rr_, vals[:, 0:8], src, -3e38), q1, rest.free)
                q4 = V(lambda e: e.max(vals[:, 8:16], rr_), q3)
                q5 = V(lambda e: e.max_index(ids[:, 8:16], vals[:, 8:16], rr_), q4)
                rest.free = [q5]
                return q3, q5

            for a in range(2):
                for hh in range(2):
                    b = bank[2 * a + hh]
                    for h in range(4):
                        q3, q5 = top16(top[:, a, 4 * hh + h, :], topi[:, a, 4 * hh + h, :], b.ap[:, 128 * h:128 * h + 128], b.scores)
                        yield
                    b.free = [q3]
            s_tf = V(lambda e: e.tensor_copy(topf, topi), q5)
            q_e = None
            for half in range(2):
                hs_ = slice(4 * half, 4 * half + 4)
                c4 = cand.rearrange("p (h i j) -> p h i j", h=4, i=16)
                s1 = V(lambda e: e.tensor_tensor(c4, top[:, 0, hs_].unsqueeze(3).to_broadcast([P, 4, 16, 16]),
                                                 top[:, 1, hs_].unsqueeze(2).to_broadcast([P, 4, 16, 16]), ALU.add), q5, q_e)
                yield
                for h in range(4):
                    q3, q5 = top16(best[:, 4 * half + h, :], besti[:, 4 * half + h, :], cand[:, 256 * h:256 * h + 256], s1)
                    q_e = q5
                    yield
            bi = smi[:, 256:384]
            oh = cand.rearrange("p (h k j) -> p h k j", h=4, k=16)
            q = q5
            for a in range(2):
                if a == 0:
                    q = V(lambda e: e.tensor_scalar(hilo, bi, 4, None, ALU.logical_shift_right), q)
                else:
                    q = V(lambda e: e.tensor_scalar(hilo, bi, 15, None, ALU.bitwise_and), q)
                q = V(lambda e: e.tensor_copy(hf[:, a].rearrange("p h k -> p (h k)"), hilo), q)
                for half in range(2):
                    hs_ = slice(4 * half, 4 * half + 4)
                    q = V(lambda e: e.tensor_tensor(oh, hf[:, a, hs_].unsqueeze(3).to_broadcast([P, 4, 16, 16]),
                                                    iota.unsqueeze(1).unsqueeze(1).to_broadcast([P, 4, 16, 16]), ALU.is_equal), q)
                    yield
                    q = V(lambda e: e.tensor_tensor(oh, oh, topf[:, a, hs_].unsqueeze(2).to_broadcast([P, 4, 16, 16]), ALU.mult),
                          q, s_tf)
                    yield
                    q = V(lambda e: e.tensor_reduce(ef[:, a, hs_], oh, AX, ALU.add), q)
                    yield
            e1, e2 = (junk[:, 512 + 128 * a:640 + 128 * a] for a in range(2))
            q = V(lambda e: e.tensor_scalar(e1, e1, 128.0, float(16384 * l), ALU.mult, ALU.add), q)
            q = V(lambda e: e.tensor_tensor(eidx[:, 128 * t_:128 * t_ + 128], e1, e2, ALU.add), q, left.get(("idx", t_)))
            routed[(l, t_)] = q
            g3 = gate[t_].rearrange("p (h k) -> p h k", h=8)
            gs = sm[:, 720:728]
            q = V(lambda e: e.tensor_tensor(g3, best, best[:, :, 0:1].to_broadcast([P, 8, 16]), ALU.subtract), q)
            q = A(lambda e: e.activation(gate[t_], gate[t_], ACT.Exp), q)
            yield
            q = V(lambda e: e.tensor_reduce(gs, g3, AX, ALU.add), q)
            q = V(lambda e: e.reciprocal(gs, gs), q)
            q = V(lambda e: e.tensor_tensor(g3, g3, gs.unsqueeze(2).to_broadcast([P, 8, 16]), ALU.mult), q)
            gated[(l, t_)] = q
            left["mixer"] = [q, left["kk"], qpd]

        xn_done, gated = {}, {}
        u_tab = T["peer_u"].rearrange("l e d -> (l e) d")
        v_tab = T["peer_v"].rearrange("l e d -> (l e) d")
        slots = [Buf(arena[:, 1024 * i:1024 * i + 1024]) for i in range(ROWS)]
        for b in slots:
            b.free = [prior]
        nslot = [0]
        order = [(0, 0), (0, 1), (1, 0), (1, 1)]
        weighted = {}

        def gather(tab, l, t_, k):
            i = nslot[0] % ROWS
            nslot[0] += 1
            sl = slots[i]
            step = M.dma(row_landed[i], lambda e: e.indirect_dma_start(
                sl.ap, None, tab, bass.IndirectOffsetOnAxis(ap=eidx[:, 128 * t_ + k:128 * t_ + k + 1], axis=0)),
                sl.free, routed[(l, t_)])
            return sl, step

        def up(n):
            (l, t_), k = order[n // 128], n % 128
            sl, here = gather(u_tab, l, t_, k)
            c = 128 * t_ + k
            s = V(lambda e: e.tensor_tensor_reduce(out=sl.ap, in0=sl.ap, in1=row_y[t_], scale=1.0, scalar=0.0, op0=ALU.mult,
                                                   op1=ALU.add, accum_out=hid[:, c:c + 1]), here, xn_done[(l, t_)])
            sl.free = [s]
            if k == 127:
                left[("xn", t_)] = s
            if k % G == G - 1:
                c = 128 * t_ + k + 1 - G
                w_ = wexp[:, c:c + G]
                s = A(lambda e: e.activation(w_, hid[:, c:c + G], ACT.Gelu_apprx_tanh), s, left.get(("w", t_, k)))
                weighted[(l, t_, k // G)] = V(lambda e: e.tensor_tensor(w_, w_, gate[t_][:, k + 1 - G:k + 1], ALU.mult),
                                              s, gated[(l, t_)])

        def down(n):
            (l, t_), k = order[n // 128], n % 128
            sl, here = gather(v_tab, l, t_, k)
            if k == 127:
                left[("idx", t_)] = here
            dg = diags[n % 4]
            c = 128 * t_ + k
            s_dg = A(lambda e: e.activation(dg.ap, ident, ACT.Copy, scale=wexp[:, c:c + 1]), weighted[(l, t_, k // G)], dg.free)
            if k % G == G - 1:
                left[("w", t_, k)] = s_dg
            for half in range(2):
                b = bank[4 + half]
                s = E(lambda e: e.matmul(b.ap[:, :], dg.ap, sl.ap[:, 512 * half:512 * half + 512], start=(k == 0), stop=(k == 127)),
                      here, s_dg, b.free if k == 0 else None)
            dg.free = [s]
            sl.free = [s]
            if k == 127:
                left["x"][t_] = []
                for half in range(2):
                    b = bank[4 + half]
                    q = add_to_x(t_, half, b, s)
                    b.free = [q]
                    left["x"][t_].append(q)

        stores = []
        l_out = landing("l_out")
        o3 = out.rearrange("(t p) d -> p t d", p=P)

        def finish(t_):
            if t_ == 0:
                landed_l["row"] = load(S, l_row, rowg[:, :], T["rows"][:, B_FIN:B_FIN + 1024], left["row"])
            y = row_y[t_]
            r, s = yield from rms_tile(t_, y, left["x"][t_], left[("xn", t_)])
            q = V(lambda e: e.scalar_tensor_tensor(y, x3[:, t_, :], r, rowg[:, :], ALU.mult, ALU.mult), s, landed_l["row"])
            stores.append(load(S, l_out, o3[:, t_, :], y, q))

        count = sum(1 for _ in mixer(0, 0))
        todo = None
        credit = 0.0
        for n in range(512 + LAG):
            if n < 512:
                if n % 128 == 0 and n and todo:
                    for _ in todo:
                        pass
                    todo = None
                up(n)
            if n >= LAG:
                down(n - LAG)
            if n == 0:
                todo = mixer(0, 1)
            if n in (128 + LAG, 256 + LAG, 384 + LAG):
                todo = mixer(*order[n // 128 + 1]) if n < 384 else finish(0)
            credit += count / (118.0 - LAG)
            while todo and credit >= 1:
                credit -= 1
                if next(todo, "end") == "end":
                    todo = None
            credit = min(credit, 1.0)
        for _ in todo or ():
            pass
        for _ in finish(1):
            pass
        S(lambda e: e.nop(), stores)

        for q in (S, A, V, E, M):
            q.number()
        block = ctx.enter_context(nc.Block())

        @block.sync
        def _(eng):
            S.emit(eng)

        @block.scalar
        def _(eng):
            A.emit(eng)

        @block.vector
        def _(eng):
            V.emit(eng)

        @block.tensor
        def _(eng):
            E.emit(eng)

        @block.gpsimd
        def _(eng):
            M.emit(eng)


def constants():
    c = np.zeros((P, K_END), np.float32)
    c[:, K_ID:K_ID + 128] = np.eye(P)
    i = np.arange(256)[:, None]
    j = np.arange(256)[None, :]
    causal = j <= i
    d = i - j
    counts = causal * ((d <= 128).astype(int) + (d % 4 == 0) + (d % 16 == 0))
    for at, m in ((K_MC, np.where(causal, 0.0, NEG)), (K_MD, np.where(counts > 0, 0.0, NEG)), (K_CD, counts)):
        c[:, at:at + 512] = m.reshape(2, P, 256).transpose(1, 0, 2).reshape(P, 512)
    c[:, K_ONE:K_ONE + 128] = 1.0
    c[:, K_IO:K_IO + 16] = np.arange(16)
    c[:, K_IF:K_IF + 32] = np.float32(10000.0) ** (-np.arange(32, dtype=np.float32) / np.float32(32))
    for h in range(8):
        at = 64 * (h % 2) + h
        c[at + 32, K_SEL + h // 2] = 8.0
        c[at, K_SEL + 5 + h // 2] = 1.0
    for at in (0, 64):
        c[at:at + 8, K_SEL + 4] = -8.0
        c[at + 32:at + 40, K_SEL + 9] = 1.0
    return c


def kernel(**inputs):
    import concourse.bacc as _bacc
    from concourse.bass_utils import run_bass_kernel_spmd as _run

    a = {k: np.asarray(v) for k, v in inputs.items()}

    def col(v):
        return v.reshape(-1, P).T

    def pad(v, n):
        out = np.zeros((P, n), v.dtype)
        out[:v.shape[0]] = v.reshape(v.shape[0], -1)
        return out

    def forget(v):
        out = np.zeros(v.shape[:-1] + (104,), v.dtype)
        for at in (0, 32, 64, 96):
            out[..., at:at + 8] = v
        return out

    parts = [col(a["mix_norm_g"][0]), col(a["mem_norm_g"][0]), col(a["ffn_norm_g"][0]),
             col(a["norm1_g_2"][0]), col(a["norm1_g_2"][1]),
             a["ffn_conv_w"][0].reshape(3, 44, P).transpose(2, 1, 0).reshape(P, 132), col(a["ffn_conv_b"][0])]
    for l in range(2):
        parts += [a["conv_dw_w_2"][l].reshape(31, 2, P).transpose(2, 1, 0).reshape(P, 62), col(a["conv_dw_b_2"][l]),
                  col(a["conv_ln_g_2"][l]), col(a["conv_ln_b_2"][l]),
                  a["rg_conv_w_2"][l].reshape(4, 2, P).transpose(2, 1, 0).reshape(P, 8), col(a["rg_conv_b_2"][l]),
                  col(a["rg_b_r_2"][l]), col(a["rg_b_i_2"][l]), col(a["rg_lambda_2"][l]),
                  pad(forget(a["b_forget_2"][l]), 1)]
    vecs = np.concatenate(parts, axis=1)
    row = np.concatenate([a[n][0] for n in ("moba_q_norm_g", "moba_k_norm_g", "dil_q_norm_g", "dil_k_norm_g",
                                            "mem_q_norm_g", "mem_k_norm_g")]
                         + [a["norm2_g_2"][0], a["norm2_g_2"][1], a["final_g_2"]])
    keys = np.stack([a["peer_k1_2"], a["peer_k2_2"]], axis=1).transpose(0, 4, 1, 2, 3).reshape(2, P, 2048)
    rg = np.zeros((2, 2, 2, P, P), np.float32)
    for g, n in enumerate(("rg_w_r_2", "rg_w_i_2")):
        for h in range(4):
            o = 64 * (h % 2)
            rg[:, g, h // 2, o:o + 64, o:o + 64] = a[n][:, h]
    rgw = rg.transpose(0, 3, 1, 2, 4).reshape(2, P, 512)
    wf = forget(a["w_in_2"][:, :, 1536:1544]).reshape(2, 8, P, 104).transpose(0, 2, 1, 3).reshape(2, P, 832)
    arrays = {
        "x": a["x"][0], "mem": a["mem"][0], "pos": a["positions"][0].reshape(2, P).T,
        "const": constants(), "vecs": vecs, "rows": np.broadcast_to(row, (P, row.size)),
        "keys": keys, "rgw": rgw, "wf": wf,
        "w_in": a["w_in"][0], "w_mem_kv": a["w_mem_kv"][0], "w_branch_moba": a["w_branch_moba"][0],
        "w_branch_dil": a["w_branch_dil"][0], "w_branch_mem": a["w_branch_mem"][0], "w_out": a["w_out"][0],
        "w_ffn_up": a["w_ffn_up"][0], "w_ffn_down": a["w_ffn_down"][0],
        "w_in_2": a["w_in_2"], "w_out_2": a["w_out_2"], "peer_wq": a["peer_wq_2"],
        "peer_u": a["peer_u_2"], "peer_v": a["peer_v_2"],
    }
    nc = _bacc.Bacc("TRN2", target_bir_lowering=False, num_devices=1)
    feeds, T = {}, {}
    for name, v in arrays.items():
        v = np.ascontiguousarray(v)
        feeds[f"in_{name}_dram"] = v
        T[name] = nc.dram_tensor(f"in_{name}_dram", v.shape, mybir.dt.from_np(v.dtype), kind="ExternalInput").ap()
    out = nc.dram_tensor("out_0_dram", (256, 1024), F32, kind="ExternalOutput").ap()
    program(nc, T, out)
    r = _run(nc, [feeds], core_ids=[0])
    return r.results[0]["out_0_dram"].reshape(1, 256, 1024)
```

```python
from collections import deque
from contextlib import ExitStack
from itertools import chain

import numpy as np

import concourse.bass as bass
from concourse import mybir

ALU = mybir.AluOpType
ACT = mybir.ActivationFunctionType
AX = mybir.AxisListType.X
F32 = mybir.dt.float32
I32 = mybir.dt.int32
U32 = mybir.dt.uint32

P = 128
EPS = 1e-6
TWO_PI = 6.283185307179586
C1 = 6.28125
C2 = 0.0019350051879882812
C3 = TWO_PI - C1 - C2
MAGIC = 12582912.0
NEG = -1e30
SLOT = 4096
NSLOT = 3
ROWS = 8
G = 8
LAG = 10
AHEAD = 2
ADD = (0, 2)
SHARE = (1, 2)
WAITS = 3
RATIO = (0.9, 1.0)
SIDE = 1
FIRST = 460
SECOND = 340

K_ID, K_MC, K_MD, K_CD, K_ONE, K_IO, K_IF, K_SEL, K_END = 0, 128, 640, 1152, 1664, 1792, 1808, 1840, 1850
V_MIX, V_MEM, V_FFN, V_N1, V_CW, V_CB, V_L = 0, 8, 16, 24, 40, 172, 216
L_DW, L_DB, L_G, L_B, L_RW, L_RB, L_BR, L_BI, L_LAM, L_BF, L_END = 0, 62, 64, 66, 68, 76, 78, 80, 82, 84, 85
V_END = V_L + 2 * L_END
B_HEAD, B_N2, B_FIN, B_END = 0, 384, 384 + 2048, 384 + 3072


class Ops:

    def activation(self, *a, **k):
        self.call = lambda e: e.activation(*a, **k)

    def dma_start(self, *a, **k):
        self.call = lambda e: e.dma_start(*a, **k)

    def indirect_dma_start(self, *a, **k):
        self.call = lambda e: e.indirect_dma_start(*a, **k)

    def match_replace(self, *a, **k):
        self.call = lambda e: e.match_replace(*a, **k)

    def matmul(self, *a, **k):
        self.call = lambda e: e.matmul(*a, **k)

    def max(self, *a, **k):
        self.call = lambda e: e.max(*a, **k)

    def max_index(self, *a, **k):
        self.call = lambda e: e.max_index(*a, **k)

    def memset(self, *a, **k):
        self.call = lambda e: e.memset(*a, **k)

    def nop(self, *a, **k):
        self.call = lambda e: e.nop(*a, **k)

    def reciprocal(self, *a, **k):
        self.call = lambda e: e.reciprocal(*a, **k)

    def scalar_tensor_tensor(self, *a, **k):
        self.call = lambda e: e.scalar_tensor_tensor(*a, **k)

    def tensor_copy(self, *a, **k):
        self.call = lambda e: e.tensor_copy(*a, **k)

    def tensor_reduce(self, *a, **k):
        self.call = lambda e: e.tensor_reduce(*a, **k)

    def tensor_scalar(self, *a, **k):
        self.call = lambda e: e.tensor_scalar(*a, **k)

    def tensor_tensor(self, *a, **k):
        self.call = lambda e: e.tensor_tensor(*a, **k)

    def tensor_tensor_reduce(self, *a, **k):
        self.call = lambda e: e.tensor_tensor_reduce(*a, **k)

    def tensor_tensor_scan(self, *a, **k):
        self.call = lambda e: e.tensor_tensor_scan(*a, **k)

    def transpose(self, *a, **k):
        self.call = lambda e: e.transpose(*a, **k)


class Step:

    def __init__(self, queue, fn, after):
        self.queue, self.fn, self.after = queue, None, after
        self.sem = self.value = None
        self.marked = False
        if fn:
            self.fill(fn)

    def fill(self, fn):
        ops = Ops()
        fn(ops)
        self.fn = ops.call


def _flat(steps):
    for s in steps:
        if isinstance(s, (list, tuple)):
            yield from _flat(s)
        elif s is not None:
            yield s


class Queue:

    def __init__(self, sem):
        self.sem, self.steps, self.pending = sem, [], []

    def __call__(self, fn, *after):
        after = list(_flat(after)) + self.pending
        self.pending = []
        for a in after:
            a.marked = True
        step = Step(self, fn, after)
        self.steps.append(step)
        return step

    def wait(self, *steps):
        self.pending += _flat(steps)

    def dma(self, landed, fn, *after):
        step = self(fn, *after)
        landed[1] += 16
        step.sem, step.value = landed
        return step

    def number(self):
        n = 0
        for s in self.steps:
            if s.sem is None and s.marked:
                n += 1
                s.value = n

    def emit(self, eng):
        seen = {}
        for s in self.steps:
            if s.fn is None:
                continue
            for a in s.after:
                sem = a.sem or a.queue.sem
                if seen.get(id(sem), 0) < a.value:
                    eng.wait_ge(sem, a.value)
                    seen[id(sem)] = a.value
            ins = s.fn(eng)
            if s.sem is not None:
                ins.then_inc(s.sem, 16)
            elif s.marked:
                ins.then_inc(self.sem, 1)


class Buf:

    def __init__(self, ap):
        self.ap, self.free = ap, []


class Room:

    def __init__(self, banks, order, S, T, O, scr, hT, tmp):
        self.bank = [banks[i] for i in order]
        self.S, self.T, self.O = S, T, O
        self.scr, self.hT, self.tmp = scr, hT, tmp
        self.tmps = [Buf(tmp[:, 512 * i:512 * i + 512]) for i in range(6)]


def program(nc, T, out):
    ctx = ExitStack()
    with ctx:
        def sb(name, cols, dt=F32):
            return ctx.enter_context(nc.sbuf_tensor(name, [P, cols], dt))

        def sem(name):
            return ctx.enter_context(nc.semaphore(name))

        S, A, V, E, M = (Queue(sem(n)) for n in ("q_sp", "q_act", "q_dve", "q_pe", "q_pool"))

        const = sb("const", K_END)
        vecs = sb("vecs", V_END)
        rows = sb("rows", 384)
        rowg = sb("rowg", 1024)
        posi = sb("posi", 2, I32)
        posf = sb("posf", 2)
        x = sb("x", 2048)
        hT = sb("hT", 2048)
        edge = sb("edge", 16)
        ring = sb("ring", NSLOT * SLOT)
        kk = sb("kk", 2048)
        rgw = sb("rgw", 512)
        wf = sb("wf", 832)
        arena = sb("arena", 1024 * ROWS)
        kv1 = sb("kv1", 4096)
        v2 = sb("v2", 1024)
        osb = sb("osb", 2048)
        scr = sb("scr", 2816)
        keep = sb("keep", 2630)
        mixs = sb("mixs", 1024)
        tmp = sb("tmp", 3072)
        junk = sb("junk", 1024)
        cs = sb("cs", 2 * 128)
        sm = sb("sm", 1024)
        smi = sb("smi", 512, U32)
        eidx = sb("eidx", 256, U32)
        hid = sb("hid", 256)
        wexp = sb("wexp", 256)
        diag = sb("diag", 4 * 128)
        diags = [Buf(diag[:, 128 * i:128 * i + 128]) for i in range(4)]
        psum = ctx.enter_context(nc.psum_tensor("psum", [P, 4096], F32))
        bank = [Buf(psum[:, 512 * i:512 * i + 512]) for i in range(8)]

        ident = const[:, K_ID:K_ID + 128]
        mcau = const[:, K_MC:K_MC + 512].rearrange("p (t k) -> p t k", t=2)
        mdil = const[:, K_MD:K_MD + 512].rearrange("p (t k) -> p t k", t=2)
        cdil = const[:, K_CD:K_CD + 512].rearrange("p (t k) -> p t k", t=2)
        ones = const[:, K_ONE:K_ONE + 128]
        iota = const[:, K_IO:K_IO + 16]
        x3 = x[:, :].rearrange("p (t d) -> p t d", t=2)
        k1T = kv1[:, 0:2048].rearrange("p (b t) -> p b t", b=8)
        v1 = kv1[:, 2048:4096].rearrange("p (t d) -> p t d", t=2)
        v23 = v2[:, :].rearrange("p (t d) -> p t d", t=2)
        kk4 = kk[:, :].rearrange("p (a h n) -> p a h n", a=2, h=8)
        rgw4 = rgw[:, :].rearrange("p (a b n) -> p a b n", a=2, b=2)
        wf3 = wf[:, :].rearrange("p (k n) -> p k n", k=8)

        def landing(name):
            return [sem(name), 0]

        def load(queue, landed, dst, src, *after):
            return queue.dma(landed, lambda e: e.dma_start(dst, src), *after)

        x_in = T["x"].rearrange("(t p) d -> p t d", p=P)
        ld_x = [load(S, landing("l_x0"), x3[:, 0, :], x_in[:, 0, :])]
        ld_c = load(S, landing("l_c"), const[:, :], T["const"])
        ld_v = load(S, landing("l_v"), vecs[:, :], T["vecs"])
        row_landed = [landing(f"l_g{i}") for i in range(ROWS)]
        l_kk, l_rg, l_wf = landing("l_kk"), landing("l_rg"), landing("l_wf")

        def cols(w, c0, n, kb=8, k0=0, at=0, width=512):
            src = w[k0 * P:(k0 + kb) * P, c0:c0 + n].rearrange("(k p) n -> p k n", p=P)
            return lambda slot: (slot[:, 0:kb * width].rearrange("p (k n) -> p k n", k=kb)[:, :, at:at + n], src)

        def first_block_slabs(t_):
            qkv = [cols(T["w_in"], 512 * c, 512) for c in range(5)]
            gates = [cols(T["w_in"], 512 * c, 512) for c in range(5, 11)]
            branches = [cols(T["w_branch_" + n], 0, 1024, kb, width=1024) for n, kb in (("moba", 3), ("dil", 3), ("mem", 2))]
            if t_ == 0:
                r = qkv + [cols(T["w_mem_kv"], 0, 512)] + gates + branches
            else:
                r = qkv + [w for b in range(3) for w in gates[2 * b:2 * b + 2] + branches[b:b + 1]]
            r += [cols(T["w_out"], 512 * c, 512) for c in range(2)]
            r += [(cols(T["w_ffn_up"], 256 * c, 256), cols(T["w_ffn_up"], 2816 + 256 * c, 256, at=256)) for c in range(11)]
            return iter(r + [cols(T["w_ffn_down"], 0, 1024, min(4, 22 - k), k, width=1024) for k in range(0, 22, 4)])

        def second_block_slabs(l):
            w = T["w_in_2"][l]
            return iter([cols(w, c, 512) for c in (0, 512, 1024, 1544, 2056)]
                        + [cols(T["w_out_2"][l], 512 * c, 512) for c in range(2)]
                        + [cols(T["peer_wq"][l], 512 * c, 512) for c in range(4)])

        slot_landed = [landing(f"l_s{i}") for i in range(NSLOT)]
        loaded = []
        taken = [0, 0]

        def fetch(after, at):
            loaded.append((at, [S.dma(slot_landed[at], None, after), S.dma(slot_landed[at], None)]))

        fetch(None, 0)
        fetch(None, 1)
        ld_p = load(S, landing("l_p"), posi[:, :], T["pos"])
        ld_r = load(S, landing("l_r"), rows[:, :], T["rows"][:, 0:384])
        mem3 = osb[:, :].rearrange("p (t d) -> p t d", t=2)
        ld_m = load(S, landing("l_m"), mem3, T["mem"].rearrange("(t p) d -> p t d", p=P))
        for i in range(2, NSLOT):
            fetch(None, i)
        ld_x.append(load(S, landing("l_x1"), x3[:, 1, :], x_in[:, 1, :]))

        def slab(weights):
            n = taken[0]
            taken[0] += 1
            at, steps = loaded[n]
            slot = ring[:, at * SLOT:(at + 1) * SLOT]
            part = next(weights)
            if isinstance(part, tuple):
                halves = [p(slot) for p in part]
            else:
                dst, src = part(slot)
                kb = dst.shape[1]
                halves = [(dst[:, 0:kb // 2, :], src[:, 0:kb // 2, :]), (dst[:, kb // 2:kb, :], src[:, kb // 2:kb, :])]
            for step, (d, w) in zip(steps, halves):
                step.fill(lambda e: e.dma_start(d, w))
            return slot, steps, at

        def matmuls(dst, pairs, *after):
            for i, (a, b) in enumerate(pairs):
                step = E(lambda e, a=a, b=b, i=i: e.matmul(dst, a, b, start=(i == 0), stop=(i == len(pairs) - 1)),
                         *(after if i == 0 else ()))
            return step

        def transposes(b, srcs, *after):
            for i, src in enumerate(srcs):
                step = E(lambda e, i=i, src=src: e.transpose(b.ap[:, 128 * i:128 * i + 128], src, ident),
                         ld_c, *(list(after) + b.free if i == 0 else ()))
            return step

        def inv_root(ms, y, t, *after):
            s = V(lambda e: e.reciprocal(y, ms), *after)
            s = A(lambda e: e.activation(y, y, ACT.Sqrt), s)
            s = V(lambda e: e.tensor_tensor(t, y, y, ALU.mult), s)
            s = V(lambda e: e.tensor_tensor(t, t, ms, ALU.mult), s)
            s = V(lambda e: e.tensor_scalar(t, t, -0.5, 1.5, ALU.mult, ALU.add), s)
            return V(lambda e: e.tensor_tensor(y, y, t, ALU.mult), s)

        def rms(src3, dst3, at, *after):
            ss, y, t = sm[:, at:at + 2], sm[:, at + 2:at + 4], sm[:, at + 4:at + 6]
            s = [A(lambda e, t_=t_: e.activation(dst3[:, t_, :], src3[:, t_, :], ACT.Square, accum_out=sm[:, at + t_:at + t_ + 1]),
                   *after) for t_ in range(2)]
            s = V(lambda e: e.tensor_scalar(ss, ss, 1.0 / 1024, EPS, ALU.mult, ALU.add), s)
            return y, inv_root(ss, y, t, s)

        def attention(units, out3, free_v, room):
            S_b, T_b, O_b, tmps = room.S, room.T, room.O, room.tmps
            Sm, Eb, Pt = tmps[0:2], tmps[2:4], tmps[4:6]
            for b in tmps:
                b.free = b.free + list(_flat([free_v]))
            den = sm[:, 800:864].rearrange("p (t h) -> p t h", t=2)
            mx = sm[:, 864 + 8 * units[0]["t"]:872 + 8 * units[0]["t"]].rearrange("p (a h) -> p a h", a=4)
            groups = []
            for u in units:
                if not groups or groups[-1][0] != u["group"]:
                    groups.append((u["group"], []))
                groups[-1][1].append(u)
                u["o"] = bank[O_b[(len(groups) - 1) % len(O_b)]]
                u["first"] = len(groups[-1][1]) == 1
                u["members"] = groups[-1][1]
            done = []

            def scores(i):
                u = units[i]
                t_, nk = u["t"], u["nk"]
                n = S_b[i % len(S_b)]
                sm_, e_ = Sm[i % 2], Eb[i % 2]
                s3 = psum[:, 512 * n:512 * n + 1024].rearrange("p (h k) -> p h k", h=2)[:, :, 0:nk]
                d3 = sm_.ap.rearrange("p (h k) -> p h k", h=2)[:, :, 0:nk]
                x3_ = e_.ap.rearrange("p (h k) -> p h k", h=2)[:, :, 0:nk]
                for h in range(2):
                    pairs = [(u["q"](h), u["k"](h))] + ([u["bias"](h)] if u["bias"] else [])
                    s = matmuls(s3[:, h, :], pairs, u["ready"], bank[n + h].free)
                m2, n2 = mx[:, i % 2, :], mx[:, 2 + i % 2, :]
                h0 = u["col"] // 64
                if u["mask"] is not None:
                    tops = [V(lambda e: e.tensor_tensor_reduce(out=d3[:, h, :], in0=s3[:, h, :], in1=u["mask"][:, t_, 0:nk], scale=1.0,
                                                               scalar=-3e38, op0=ALU.add, op1=ALU.max, accum_out=m2[:, h:h + 1]),
                              s, sm_.free) for h in range(2)]
                    bank[n].free = bank[n + 1].free = tops
                    src = d3
                else:
                    tops = V(lambda e: e.tensor_reduce(m2, s3, AX, ALU.max), s)
                    src = s3
                s = V(lambda e: e.tensor_scalar(n2, m2, -0.125, None, ALU.mult), tops)
                u["e"] = [A(lambda e: e.activation(x3_[:, h, :], src[:, h, :], ACT.Exp, bias=n2[:, h:h + 1], scale=0.125,
                                                   accum_out=den[:, t_, h0 + h:h0 + h + 1]), s, e_.free) for h in range(2)]
                if u["mask"] is None:
                    bank[n].free = bank[n + 1].free = list(u["e"])
                sm_.free = list(u["e"])
                u["e3"] = x3_

            def weights(i):
                u = units[i]
                t_, nk, x3_ = u["t"], u["nk"], u["e3"]
                s = u["den"] = u["e"]
                if u["counts"] is not None:
                    h0 = u["col"] // 64
                    s = u["den"] = [V(lambda e: e.tensor_tensor_reduce(
                        out=x3_[:, h, :], in0=x3_[:, h, :], in1=u["counts"][:, t_, 0:nk], scale=1.0, scalar=0.0, op0=ALU.mult,
                        op1=ALU.add, accum_out=den[:, t_, h0 + h:h0 + h + 1]), u["e"]) for h in range(2)]
                b, pt = bank[T_b[i % len(T_b)]], Pt[i % 2]
                nb = nk // 128
                last = transposes(b, [x3_[:, h, 128 * c:128 * c + 128] for h in range(2) for c in range(nb)], s)
                Eb[i % 2].free = [last, u["den"]]
                p_ = pt.ap[:, 0:256 * nb]
                s = A(lambda e: e.activation(p_, b.ap[:, 0:256 * nb], ACT.Copy), last, pt.free)
                b.free = [s]
                u["p"], u["p3"] = s, p_.rearrange("p (h c q) -> p h c q", h=2, c=nb)

            def values(i):
                u = units[i]
                o, nb = u["o"], u["nk"] // 128
                for h in range(2):
                    c0 = u["col"] - u["members"][0]["col"] + 64 * h
                    s = matmuls(o.ap[:, c0:c0 + 64], [(u["p3"][:, h, c, :], u["v"](h, c)) for c in range(nb)],
                                u["p"], o.free if u["first"] and h == 0 else None)
                Pt[i % 2].free = [s]
                if u is u["members"][-1]:
                    t_, n = u["t"], 2 * len(u["members"])
                    c0 = u["members"][0]["col"]
                    dd = den[:, t_, c0 // 64:c0 // 64 + n]
                    r = V(lambda e: e.reciprocal(dd, dd), u["den"])
                    o3 = o.ap[:, 0:64 * n].rearrange("p (h d) -> p h d", h=n)
                    y3 = out3[:, t_, c0:c0 + 64 * n].rearrange("p (h d) -> p h d", h=n)
                    rb = dd.unsqueeze(2).to_broadcast([P, n, 64])
                    r = V(lambda e: e.tensor_tensor(y3, o3, rb, ALU.mult), r, s)
                    o.free = [r]
                    done.append(r)

            for i in range(len(units) + 2):
                if i < len(units):
                    scores(i)
                    yield
                if 1 <= i <= len(units):
                    weights(i - 1)
                    yield
                if i >= 2:
                    values(i - 2)
            return done

        def whole(steps):
            while True:
                try:
                    next(steps)
                except StopIteration as end:
                    return end.value

        def add_to_x(t_, half, b, s):
            d = x3[:, t_, 512 * half:512 * half + 512]
            return V(lambda e: e.tensor_tensor(d, d, b.ap[:, :], ALU.add), s)

        def log1p(e_, z, z2, p_, *after):
            s = V(lambda e: e.tensor_scalar(z, e_, 2.0, None, ALU.add), *after)
            s = V(lambda e: e.reciprocal(z, z), s)
            s = V(lambda e: e.tensor_tensor(z, z, e_, ALU.mult), s)
            s = V(lambda e: e.tensor_tensor(z2, z, z, ALU.mult), s)
            s = V(lambda e: e.tensor_scalar(p_, z2, 2.0 / 19, None, ALU.mult), s)
            for n in range(17, 1, -2):
                s = V(lambda e, n=n: e.scalar_tensor_tensor(p_, p_, 2.0 / n, z2, ALU.add, ALU.mult), s)
            return V(lambda e: e.scalar_tensor_tensor(p_, p_, 2.0, z, ALU.add, ALU.mult), s)

        l_row = landing("l_row")
        kT = keep[:, 0:1024].rearrange("p (b t) -> p b t", b=4)
        ypad = keep[:, 1024:1596].rearrange("p (b t) -> p b t", b=2)
        xpad = keep[:, 1596:2114].rearrange("p (b t) -> p b t", b=2)
        cum = keep[0:104, 2114:2370]
        R = keep[0:104, 2370:2626]
        hlast = keep[:, 2626:2628]
        edge3 = edge[:, :].rearrange("p (k t) -> p k t", k=8)
        gg, gr, yc, xc = (mixs[:, 256 * i:256 * i + 256] for i in range(4))
        b2 = lambda ap: ap.rearrange("p (b t) -> p b t", b=2)
        row_y = [osb[:, 1024 * t_:1024 * t_ + 1024] for t_ in range(2)]
        top = sm[:, 0:256].rearrange("p (a h k) -> p a h k", a=2, h=8)
        topi = smi[:, 0:256].rearrange("p (a h k) -> p a h k", a=2, h=8)
        topf = junk[:, 0:256].rearrange("p (a h k) -> p a h k", a=2, h=8)
        best = sm[:, 256:384].rearrange("p (h k) -> p h k", h=8)
        besti = smi[:, 256:384].rearrange("p (h k) -> p h k", h=8)
        hilo = smi[:, 384:512]
        hf = junk[:, 256:512].rearrange("p (a h k) -> p a h k", a=2, h=8)
        ef = junk[:, 512:768].rearrange("p (a h k) -> p a h k", a=2, h=8)
        gate = [sm[:, 384 + 128 * t_:512 + 128 * t_] for t_ in range(2)]
        left = dict(kk=None, rg=None, wf=None, row=None, first=None, mixer=None, x=list(ld_x), cum=None, h=None)
        routed = {}
        landed_l = {}

        def feature_tile(b, hT_, after, ws):
            slot, here, at = slab(ws)
            w = slot[:, :].rearrange("p (k n) -> p k n", k=8)
            for i in range(4):
                s = matmuls(b.ap[:, 128 * i:128 * i + 128], [(w[:, k, 128 * i:128 * i + 128], hT_[:, k, :]) for k in range(8)],
                            here, after, b.free if i == 0 else None)
                yield 1
            fetch(s, at)
            return s

        def token_tile(b, hT_, after, ws):
            slot, here, at = slab(ws)
            w = slot[:, :].rearrange("p (k n) -> p k n", k=8)
            for k in range(8):
                s = E(lambda e, k=k: e.matmul(b.ap[:, :], hT_[:, k, :], w[:, k, :], start=(k == 0), stop=(k == 7)),
                      *([here, after, b.free] if k == 0 else []))
                if k % 2:
                    yield 1
            fetch(s, at)
            return s

        def inv_root_tile(ms, y, t, *after):
            s = V(lambda e: e.reciprocal(y, ms), *after)
            s = A(lambda e: e.activation(y, y, ACT.Sqrt), s)
            yield
            s = V(lambda e: e.tensor_tensor(t, y, y, ALU.mult), s)
            s = V(lambda e: e.tensor_tensor(t, t, ms, ALU.mult), s)
            s = V(lambda e: e.tensor_scalar(t, t, -0.5, 1.5, ALU.mult, ALU.add), s)
            return V(lambda e: e.tensor_tensor(y, y, t, ALU.mult), s)

        def rms_tile(t_, scratch, *after):
            ss, y, t = (sm[:, 640 + 3 * t_ + i:641 + 3 * t_ + i] for i in range(3))
            s = A(lambda e: e.activation(scratch, x3[:, t_, :], ACT.Square, accum_out=ss), *after)
            yield
            s = V(lambda e: e.tensor_scalar(ss, ss, 1.0 / 1024, EPS, ALU.mult, ALU.add), s)
            s = yield from inv_root_tile(ss, y, t, s)
            return y, s

        def turn_tile(src, gain, banks, after, dst):
            done = []
            for half in range(2):
                b = banks[half]
                s = transposes(b, [src[:, 128 * (4 * half + i):128 * (4 * half + i) + 128] for i in range(4)], after)
                yield
                to, src4 = dst[:, 4 * half:4 * half + 4, :], b.ap[:, :].rearrange("p (k n) -> p k n", k=4)
                if gain is None:
                    s = A(lambda e: e.activation(to, src4, ACT.Copy), s)
                else:
                    g_ = gain[:, 4 * half:4 * half + 4].unsqueeze(2).to_broadcast([P, 4, 128])
                    s = V(lambda e: e.tensor_tensor(to, src4, g_, ALU.mult), s, ld_v)
                b.free = [s]
                done.append(s)
            yield
            return done

        def weave(main, filler):
            while True:
                try:
                    next(main)
                except StopIteration as end:
                    result = end.value
                    break
                next(filler, None)
                yield
            for _ in filler:
                yield
            return result

        def load_small(l):
            landed_l["kk"] = load(S, l_kk, kk[:, :], T["keys"][l], left["kk"])
            landed_l["rg"] = load(S, l_rg, rgw[:, :], T["rgw"][l], left["rg"])
            landed_l["wf"] = load(S, l_wf, wf[:, :], T["wf"][l], left["wf"])
            landed_l["row"] = load(S, l_row, rowg[:, :], T["rows"][:, B_N2 + 1024 * l:B_N2 + 1024 * l + 1024], left["row"])

        cs4 = cs[:, :].rearrange("p (t c f) -> p t c f", t=2, c=4)

        def rotary():
            s = V(lambda e: e.tensor_copy(posf[:, :], posi[:, :]), ld_p)
            ang, kf = junk[:, 0:128].rearrange("p (a t f) -> p a t f", a=2, t=2), junk[:, 128:256].rearrange("p (a t f) -> p a t f", a=2, t=2)
            invf = const[:, K_IF:K_IF + 32]
            ss = []
            for t_ in range(2):
                a0 = V(lambda e, t_=t_: e.tensor_scalar(ang[:, 0, t_, :], invf, posf[:, t_:t_ + 1], None, ALU.mult), s, ld_c)
                ss.append(V(lambda e, t_=t_: e.tensor_copy(ang[:, 1, t_, :], ang[:, 0, t_, :]), a0))
            for a in range(2):
                s1 = V(lambda e, a=a: e.tensor_scalar(kf[:, a], ang[:, a], 1.0 / TWO_PI, 0.25 * a, ALU.mult, ALU.add), ss)
                s1 = V(lambda e, a=a: e.tensor_scalar(kf[:, a], kf[:, a], MAGIC, None, ALU.add), s1)
                s1 = V(lambda e, a=a: e.tensor_scalar(kf[:, a], kf[:, a], -MAGIC, None, ALU.add), s1)
                for c in (C1, C2, C3):
                    s1 = V(lambda e, a=a, c=c: e.scalar_tensor_tensor(ang[:, a], kf[:, a], -c, ang[:, a], ALU.mult, ALU.add), s1)
                if a:
                    s1 = V(lambda e, a=a: e.tensor_scalar(ang[:, a], ang[:, a], TWO_PI / 4, None, ALU.add), s1)
                s1 = V(lambda e, a=a: e.tensor_scalar(ang[:, a], ang[:, a], 3.1415925, -3.1415925, ALU.min, ALU.max), s1)
                s1 = A(lambda e, a=a: e.activation(ang[:, a], ang[:, a], ACT.Sin), s1)
                ss.append(s1)
            cs_ready = [V(lambda e, c=c: e.tensor_copy(cs4[:, :, c, :], ang[:, 1]), ss) for c in range(2)]
            cs_ready.append(V(lambda e: e.tensor_scalar(cs4[:, :, 2, :], ang[:, 0], -1.0, None, ALU.mult), ss))
            cs_ready.append(V(lambda e: e.tensor_copy(cs4[:, :, 3, :], ang[:, 0]), ss))
            return cs_ready

        gates = arena[:, 0:3072].rearrange("p (b d) -> p b d", b=3)
        mem_k = arena[:, 3072:3584].rearrange("p (t d) -> p t d", t=2)
        mem_s = arena[:, 4096:6144].rearrange("p (t d) -> p t d", t=2)
        memT = arena[:, 6144:8192].rearrange("p (k t) -> p k t", k=8)
        cs_done = []

        def block1(t_, room):
            tok = slice(128 * t_, 128 * t_ + 128)
            bank, scr, hT, tmp, tmps = room.bank, room.scr, room.hT, room.tmp, room.tmps
            ws = first_block_slabs(t_)
            xs = o1 = merged = scr[:, 0:1024]
            raw = scr[:, 0:1792]
            qT1 = scr[:, 1792:2816].rearrange("p (b t) -> p b t", b=8)
            xs2 = scr[:, 1024:2048]
            act = scr[:, 0:2816].rearrange("p (f t) -> p f t", f=22)
            hTt = hT[:, 0:1024].rearrange("p (k t) -> p k t", k=8)
            hTe = hT[:, 0:1040].rearrange("p (k t) -> p k t", k=8)
            places = [(0, 768, raw[:, 0:768]), (768, 384, v1[:, t_, 0:384]), (1152, 768, raw[:, 768:1536]),
                      (1920, 384, v1[:, t_, 384:768]), (2304, 256, raw[:, 1536:1792])]
            for q in (V, A, E):
                q.wait(left["first"])
            r, s = yield from rms_tile(t_, xs, left["x"][t_])
            s = V(lambda e: e.tensor_scalar(xs, x3[:, t_, :], r, None, ALU.mult), s)
            yield
            h_ready = yield from turn_tile(xs, vecs[:, V_MIX:V_MIX + 8], bank[6:8], s, hTt)
            qkv = []
            for c in range(5):
                if t_ == 0 and c == 2:
                    y, s_m = rms(mem3, mem_s, 8, ld_m)
                    s_m = [V(lambda e: e.tensor_scalar(mem_s[:, u, :], mem3[:, u, :], y[:, u:u + 1], None, ALU.mult), s_m)
                           for u in range(2)]
                    left[("xn", 0)] = left[("xn", 1)] = s_m
                if t_ == 0 and c == 3:
                    cs_done.extend(rotary())
                b = bank[c % 2]
                s = yield from token_tile(b, hTt, h_ready, ws)
                b.free = []
                for first, width, to in places:
                    a0, a1 = max(first, 512 * c), min(first + width, 512 * c + 512)
                    if a0 < a1:
                        d, src = to[:, a0 - first:a1 - first], b.ap[:, a0 - 512 * c:a1 - 512 * c]
                        b.free.append(A(lambda e: e.activation(d, src, ACT.Copy), s))
                qkv += b.free
                yield
            mem_done = []
            if t_ == 0:
                mem_ready = []
                for u in range(2):
                    mem_ready += yield from turn_tile(mem_s[:, u, :], vecs[:, V_MEM:V_MEM + 8], bank[6:8], s_m,
                                                      memT[:, :, 128 * u:128 * u + 128])
                slot, here, at = slab(ws)
                w = slot[:, :].rearrange("p (k n) -> p k n", k=8)
                for u in range(2):
                    b = bank[2 + u]
                    s = matmuls(b.ap[:, :], [(memT[:, k, 128 * u:128 * u + 128], w[:, k, :]) for k in range(8)],
                                here, mem_ready, b.free)
                    b.free = [A(lambda e: e.activation(mem_k[:, u, :], b.ap[:, 0:256], ACT.Copy), s),
                              A(lambda e: e.activation(v1[:, u, 768:1024], b.ap[:, 256:512], ACT.Copy), s)]
                    mem_done += b.free
                    yield
                fetch(s, at)

            def gate_chunks():
                for c in range(6):
                    b = (bank[5], bank[3])[c % 2]
                    s = yield from token_tile(b, hTt, h_ready, ws)
                    d = gates[:, c // 2, 512 * (c % 2):512 * (c % 2) + 512]
                    b.free = [A(lambda e: e.activation(d, b.ap[:, :], ACT.Sigmoid), s)]
                    sig[c] = (d, b.free[0])

            def heads():
                def seg(src, c, n, at, g, u):
                    return (u, src[:, c:c + 64 * n].rearrange("p (h d) -> p h d", h=n), n, at, g)
                segs = [seg(raw, 0, 6, 0, 0, t_), seg(raw, 384, 6, 6, 1, t_), seg(raw, 768, 6, 12, 2, t_),
                        seg(raw, 1152, 6, 18, 3, t_), seg(raw, 1536, 4, 24, 4, t_)]
                if t_ == 0:
                    segs += [seg(mem_k[:, u, :], 0, 4, 28 + 4 * u, 5, u) for u in range(2)]
                nh = 36 if t_ == 0 else 28
                hs, hy, ht = (sm[:, 880 + 40 * i:880 + 40 * i + nh] for i in range(3))
                s_sum = []
                sq = [Buf(tmp[:, 384 * i:384 * i + 384]) for i in range(8)]
                for i, (u, v3, n, at, g) in enumerate(segs):
                    q = sq[i % 2]
                    q3 = q.ap[:, 0:64 * n].rearrange("p (h d) -> p h d", h=n)
                    s = V(lambda e: e.tensor_tensor(q3, v3, v3, ALU.mult), qkv, mem_done if g == 5 else None, q.free)
                    s = V(lambda e: e.tensor_reduce(hs[:, at:at + n], q3, AX, ALU.add), s)
                    q.free = [s]
                    s_sum.append(s)
                    yield
                s = V(lambda e: e.tensor_scalar(hs, hs, 1.0 / 64, EPS, ALU.mult, ALU.add), s_sum)
                s_inv = yield from inv_root_tile(hs, hy, ht, s)
                normed = {}
                for i, (u, v3, n, at, g) in enumerate(segs):
                    rb = hy[:, at:at + n].unsqueeze(2).to_broadcast([P, n, 64])
                    gb = rows[:, B_HEAD + 64 * g:B_HEAD + 64 * g + 64].unsqueeze(1).to_broadcast([P, n, 64])
                    s = V(lambda e: e.tensor_tensor(v3, v3, rb, ALU.mult), s_inv)
                    s = V(lambda e: e.tensor_tensor(v3, v3, gb, ALU.mult), s, ld_r)
                    if g < 4:
                        q = sq[2 + i % 2]
                        q3 = q.ap[:, :].rearrange("p (h d) -> p h d", h=n)
                        cc = cs4[:, t_, 0:2, :].rearrange("p c f -> p (c f)").unsqueeze(1).to_broadcast([P, n, 64])
                        ns = cs4[:, t_, 2, :].unsqueeze(1).to_broadcast([P, n, 32])
                        ps_ = cs4[:, t_, 3, :].unsqueeze(1).to_broadcast([P, n, 32])
                        s1 = V(lambda e: e.tensor_tensor(q3[:, :, 0:32], v3[:, :, 32:64], ns, ALU.mult), s, q.free, cs_done)
                        s2 = V(lambda e: e.tensor_tensor(q3[:, :, 32:64], v3[:, :, 0:32], ps_, ALU.mult), s)
                        s3 = V(lambda e: e.tensor_tensor(v3, v3, cc, ALU.mult), s1, s2)
                        s = V(lambda e: e.tensor_tensor(v3, v3, q3, ALU.add), s3)
                        q.free = [s]
                    normed[(g, u)] = s
                    yield
                block = lambda c: raw[:, 128 * c:128 * c + 128]
                qk_ready = []
                all_normed = list(normed.values())
                groups = [((0, 1, 2, 6), qT1[:, 0:4, :]), ((7, 8, 12, 13), qT1[:, 4:8, :]), ((3, 4, 5, 9), k1T[:, 0:4, tok]),
                          ((10, 11), k1T[:, 4:6, tok])]
                for i, (blocks, dst) in enumerate(groups):
                    b = bank[(0, 1)[i % 2]]
                    s = transposes(b, [block(c) for c in blocks], all_normed)
                    n = len(blocks)
                    s = A(lambda e: e.activation(dst, b.ap[:, 0:128 * n].rearrange("p (b t) -> p b t", b=n), ACT.Copy), s)
                    b.free = [s]
                    qk_ready.append(s)
                    yield
                if t_ == 0:
                    b = bank[0]
                    s = transposes(b, [mem_k[:, u, 128 * j:128 * j + 128] for j in range(2) for u in range(2)], all_normed)
                    s = A(lambda e: e.activation(k1T[:, 6:8, :].rearrange("p b t -> p (b t)"), b.ap[:, :], ACT.Copy), s)
                    b.free = [s]
                    qk_ready.append(s)
                units = []
                for g, (n, p0, vc, mask, counts) in enumerate(((3, 0, 0, mcau, None), (3, 3, 384, mdil, cdil), (2, 6, 768, None, None))):
                    for j in range(n):
                        nk = 128 if t_ == 0 and mask is not None else 256
                        units.append(dict(
                            group=g, col=128 * (p0 + j), t=t_, nk=nk, mask=mask, counts=counts, bias=None, ready=qk_ready,
                            q=lambda h, p_=p0 + j: qT1[64 * h:64 * h + 64, p_, :],
                            k=lambda h, p_=p0 + j, nk=nk: k1T[64 * h:64 * h + 64, p_, 0:nk],
                            v=lambda h, c, a=vc + 128 * j: v1[:, c, a + 64 * h:a + 64 * h + 64]))
                return (yield from attention(units, o1.unsqueeze(1).to_broadcast([P, 2, 1024]), all_normed, room))

            sig = {}
            if t_ == 0:
                att = yield from weave(heads(), gate_chunks())
                load_small(0)
            else:
                att = yield from heads()
            oT = qT1
            s_oT = yield from turn_tile(o1, None, bank[6:8], att, oT)
            held = {}
            for br, (kb, k0) in enumerate(((3, 0), (3, 3), (2, 6))):
                if t_:
                    for half in range(2):
                        b, d = bank[half], tmps[2 * (br % 2) + half]
                        s = yield from token_tile(b, hTt, h_ready, ws)
                        b.free = [A(lambda e: e.activation(d.ap, b.ap[:, :], ACT.Sigmoid), s, d.free)]
                        sig[2 * br + half] = (d.ap, b.free[0])
                slot, here, at = slab(ws)
                w = slot[:, 0:kb * 1024].rearrange("p (k n) -> p k n", k=kb)
                for half in range(2):
                    b = bank[2 + half]
                    c = slice(512 * half, 512 * half + 512)
                    s_last = matmuls(b.ap[:, :], [(oT[:, k0 + k, :], w[:, k, c]) for k in range(kb)], here, s_oT, b.free)
                    yield
                    m, (gt, s_g) = merged[:, c], sig[2 * br + half]
                    if br == 0:
                        s = V(lambda e: e.tensor_tensor(m, b.ap[:, :], gt, ALU.mult), s_last, s_g)
                        b.free = [s]
                    else:
                        s = V(lambda e: e.tensor_tensor(gt, b.ap[:, :], gt, ALU.mult), s_last, s_g)
                        b.free = [s]
                        s = V(lambda e: e.tensor_tensor(m, m, gt, ALU.add), s, held[half])
                    if t_:
                        tmps[2 * (br % 2) + half].free = [s]
                    held[half] = s
                fetch(s_last, at)
            mT = yield from turn_tile(merged, None, bank[6:8], list(held.values()), hTt)
            added = []
            for c in range(2):
                b = bank[c]
                s = yield from token_tile(b, hTt, mT, ws)
                added.append(add_to_x(t_, c, b, s))
                b.free = [added[-1]]

            r, s = yield from rms_tile(t_, xs2, added, mT)
            s = V(lambda e: e.tensor_scalar(xs2, x3[:, t_, :], r, None, ALU.mult), s)
            if t_ == 0:
                s_e = V(lambda e: e.memset(hTe[:, :, 0:2], 0.0), added)
            else:
                s_e = V(lambda e: e.tensor_copy(hTe[:, :, 0:2], edge3), added, left["edge"])
            yield
            h_ready = yield from turn_tile(xs2, vecs[:, V_FFN:V_FFN + 8], bank[6:8], [s, s_e], hTe[:, :, 2:130])
            if t_ == 0:
                left["edge"] = V(lambda e: e.tensor_copy(edge3, hTe[:, :, 128:130]), h_ready)
            ub = [Buf(tmp[:, 256 * i:256 * i + 256]) for i in range(4)]
            for u in ub:
                u.free = list(held.values())
            act_done = []
            for c in range(11):
                slot, here, at = slab(ws)
                w = slot[:, :].rearrange("p (k n) -> p k n", k=8)
                for i in range(2):
                    f = 2 * c + i
                    b, u = bank[f % 4], ub[f % 4]
                    for gv in range(2):
                        cw = 256 * gv + 128 * i
                        s = matmuls(b.ap[:, 256 * gv:256 * gv + 130], [(w[:, k, cw:cw + 128], hTe[:, k, :]) for k in range(8)],
                                    here, h_ready, s_e, b.free if gv == 0 else None)
                        yield 1
                    last = []
                    for gv in range(2):
                        j = f + 22 * gv
                        ps_, d = b.ap[:, 256 * gv:256 * gv + 130], u.ap[:, 128 * gv:128 * gv + 128]
                        wv = vecs[:, V_CW + 3 * j:V_CW + 3 * j + 3]
                        last.append(A(lambda e: e.activation(d, ps_[:, 2:130], ACT.Identity, bias=vecs[:, V_CB + j:V_CB + j + 1],
                                                             scale=wv[:, 2:3]), s, u.free))
                    first = list(last)
                    for gv in range(2):
                        j = f + 22 * gv
                        ps_, d = b.ap[:, 256 * gv:256 * gv + 130], u.ap[:, 128 * gv:128 * gv + 128]
                        wv = vecs[:, V_CW + 3 * j:V_CW + 3 * j + 3]
                        q = first
                        for k in (1, 2):
                            q = V(lambda e: e.scalar_tensor_tensor(d, ps_[:, 2 - k:130 - k], wv[:, 2 - k:3 - k], d,
                                                                   ALU.mult, ALU.add), q)
                        last[gv] = q
                    b.free = list(last)
                    d = u.ap[:, 0:128]
                    q = A(lambda e: e.activation(d, d, ACT.Silu), last[0])
                    u.free = [V(lambda e: e.tensor_tensor(act[:, f, :], u.ap[:, 0:128], u.ap[:, 128:256], ALU.mult), q, last[1])]
                    act_done.append(u.free[0])
                fetch(s, at)
            for c in range(6):
                slot, here, at = slab(ws)
                kb = min(4, 22 - 4 * c)
                w = slot[:, 0:kb * 1024].rearrange("p (k n) -> p k n", k=kb)
                for k in range(kb):
                    f = 4 * c + k
                    for half in range(2):
                        b = bank[6 + half]
                        s = E(lambda e: e.matmul(b.ap[:, :], act[:, f, :], w[:, k, 512 * half:512 * half + 512],
                                                 start=(f == 0), stop=(f == 21)), here, act_done[f], b.free if f == 0 else None)
                    yield 1
                fetch(s, at)
            left["x"][t_] = []
            for half in range(2):
                b = bank[6 + half]
                q = add_to_x(t_, half, b, s)
                b.free = [q]
                left["x"][t_].append(q)
            left["first"] = [act_done[-1], s, left["x"][t_]]

        def mixer(l, t_, room):
            lv = V_L + L_END * l
            if (l, t_) == (1, 0):
                load_small(1)
            tok = slice(128 * t_, 128 * t_ + 128)
            bank, scr, hT, tmp = room.bank, room.scr, room.hT, room.tmp
            ws = second_block_slabs(l)
            xs = scr[:, 0:1024]
            o_t = scr[:, 0:512]
            qT = scr[:, 1024:1536].rearrange("p (b t) -> p b t", b=4)
            Lh = scr[0:104, 1536:2048].rearrange("p (h t) -> p h t", h=4)
            fz, fa, fe, f1, f2, f3 = (scr[0:104, 2048 + 128 * i:2176 + 128 * i] for i in range(6))
            hTt = hT[:, 0:1024].rearrange("p (k t) -> p k t", k=8)
            mixT = hT[:, 1024:2048].rearrange("p (k t) -> p k t", k=8)
            cand = tmp[:, 2048:3072]
            qp = tmp[:, 0:2048].rearrange("p (b t) -> p b t", b=16)
            for q in (V, A, E):
                q.wait(left["first"], left["mixer"])
            r, s = yield from rms_tile(t_, xs, left["x"][t_])
            s = V(lambda e: e.tensor_scalar(xs, x3[:, t_, :], r, None, ALU.mult), s)
            yield
            h_ready = yield from turn_tile(xs, vecs[:, V_N1 + 8 * l:V_N1 + 8 * l + 8], bank[6:8], s, hTt)

            four = lambda b: b.ap[:, :].rearrange("p (b t) -> p b t", b=4)
            s = yield from feature_tile(bank[0], hTt, h_ready, ws)
            q_done = A(lambda e: e.activation(qT, four(bank[0]), ACT.Copy), s)
            bank[0].free = [q_done]
            s = yield from feature_tile(bank[1], hTt, h_ready, ws)
            k_done = A(lambda e: e.activation(kT[:, :, tok], four(bank[1]), ACT.Copy), s)
            bank[1].free = [k_done]
            s = yield from token_tile(bank[2], hTt, h_ready, ws)
            v_done = A(lambda e: e.activation(v23[:, t_, :], bank[2].ap[:, :], ACT.Copy), s)
            bank[2].free = [v_done]

            b = bank[3]
            s_f = matmuls(b.ap[0:104, 0:128], [(wf3[:, k, :], hTt[:, k, :]) for k in range(8)], landed_l["wf"], b.free)
            left["wf"] = s_f
            yield
            s = V(lambda e: e.tensor_scalar(fz, b.ap[0:104, 0:128], vecs[0:104, lv + L_BF:lv + L_BF + 1], None, ALU.add), s_f)
            b.free = [s]
            s = V(lambda e: e.tensor_scalar(fa, fz, -1.0, None, ALU.mult), s)
            s = V(lambda e: e.tensor_tensor(fa, fa, fz, ALU.max), s)
            s_e = A(lambda e: e.activation(fe, fa, ACT.Exp, scale=-1.0), s)
            yield
            s = log1p(fe, f1, f2, f3, s_e)
            yield
            s = V(lambda e: e.scalar_tensor_tensor(fz, fz, 0.0, f3, ALU.min, ALU.subtract), s)
            s = V(lambda e: e.memset(f2, 1.0), s)
            start = cum[:, 127:128] if t_ else 0.0
            s = V(lambda e: e.tensor_tensor_scan(cum[:, tok], f2, fz, start, ALU.mult, ALU.add), s, left["cum"])
            left["cum"] = s
            lr = [V(lambda e: e.tensor_scalar(Lh[:, h, :], cum[:, tok], const[0:104, K_SEL + h:K_SEL + h + 1],
                                              const[0:104, K_SEL + 5 + h:K_SEL + 6 + h], ALU.mult, ALU.add), s) for h in range(4)]
            lr.append(V(lambda e: e.tensor_scalar(R[:, tok], cum[:, tok], const[0:104, K_SEL + 4:K_SEL + 5],
                                                  const[0:104, K_SEL + 9:K_SEL + 10], ALU.mult, ALU.add), s))
            yield

            z1 = z2 = None
            if t_ == 0:
                z1 = V(lambda e: e.memset(ypad[:, :, 0:30], 0.0))
                z2 = V(lambda e: e.memset(xpad[:, :, 0:3], 0.0))
            b = bank[0]
            s = yield from feature_tile(b, hTt, h_ready, ws)
            s = A(lambda e: e.activation(gg, b.ap[:, 256:512], ACT.Sigmoid), s)
            yield
            s_y = V(lambda e: e.tensor_tensor(ypad[:, :, 30 + 128 * t_:158 + 128 * t_], b2(b.ap[:, 0:256]), b2(gg), ALU.mult), s)
            b.free = [s_y]
            b = bank[1]
            s = yield from feature_tile(b, hTt, h_ready, ws)
            s_gr = A(lambda e: e.activation(gr, b.ap[:, 256:512], ACT.Gelu_apprx_tanh), s)
            yield
            s_x = V(lambda e: e.tensor_copy(xpad[:, :, 3 + 128 * t_:131 + 128 * t_], b2(b.ap[:, 0:256])), s_gr)
            b.free = [s_x]

            w = vecs[:, lv + L_RW:lv + L_RW + 8].rearrange("p (b k) -> p b k", b=2)
            o = 128 * t_
            xcd = [None, None]
            for k in range(3, -1, -1):
                for bl in range(2):
                    d, u = xc[:, 128 * bl:128 * bl + 128], xpad[:, bl, k + o:k + o + 128]
                    if k == 3:
                        xcd[bl] = V(lambda e: e.tensor_scalar(d, u, w[:, bl, 3:4], vecs[:, lv + L_RB + bl:lv + L_RB + bl + 1],
                                                              ALU.mult, ALU.add), s_x, z2)
                    else:
                        xcd[bl] = V(lambda e: e.scalar_tensor_tensor(d, u, w[:, bl, k:k + 1], d, ALU.mult, ALU.add), xcd[bl])
                if k % 2 == 0:
                    yield
            b = bank[2]
            for g in range(2):
                for bl in range(2):
                    c = 256 * g + 128 * bl
                    s = matmuls(b.ap[:, c:c + 128], [(rgw4[:, g, bl, :], xc[:, 128 * bl:128 * bl + 128])],
                                landed_l["rg"], xcd, b.free if c == 0 else None)
            left["rg"] = s
            yield
            ri = tmp[:, 0:512]
            acts = []
            for g in range(2):
                for bl in range(2):
                    c = lv + (L_BR, L_BI)[g] + bl
                    at = slice(256 * g + 128 * bl, 256 * g + 128 * bl + 128)
                    acts.append(A(lambda e: e.activation(ri[:, at], b.ap[:, at], ACT.Sigmoid, bias=vecs[:, c:c + 1]), s))
            b.free = acts
            lam = vecs[:, lv + L_LAM:lv + L_LAM + 2]
            l0, l1, l2, l3, l4 = (sm[:, 700 + 2 * i:702 + 2 * i] for i in range(5))
            s = V(lambda e: e.tensor_scalar(l0, lam, -1.0, None, ALU.mult))
            s = V(lambda e: e.tensor_tensor(l1, l0, lam, ALU.max), s)
            s = A(lambda e: e.activation(l1, l1, ACT.Exp, scale=-1.0), s)
            yield
            s = log1p(l1, l2, l3, l4, s)
            s = V(lambda e: e.scalar_tensor_tensor(l4, l0, 0.0, l4, ALU.max, ALU.add), s)
            s_c = V(lambda e: e.tensor_scalar(l4, l4, 8.0, None, ALU.mult), s)
            yield
            nl, ii, aa, tt, dd = ri[:, 0:256], ri[:, 256:512], tmp[:, 512:768], tmp[:, 768:1024], tmp[:, 1024:1280]
            s = [V(lambda e: e.tensor_scalar(nl[:, 128 * bl:128 * bl + 128], nl[:, 128 * bl:128 * bl + 128], l4[:, bl:bl + 1],
                                             None, ALU.mult), s_c, acts) for bl in range(2)]
            s_a = A(lambda e: e.activation(aa, nl, ACT.Exp, scale=-1.0), s)
            s = A(lambda e: e.activation(tt, nl, ACT.Tanh), s)
            s1 = V(lambda e: e.tensor_tensor(ii, ii, xc, ALU.mult), acts)
            yield
            s = V(lambda e: e.tensor_scalar(dd, tt, 0.5, 0.5, ALU.mult, ALU.add), s)
            s = V(lambda e: e.reciprocal(dd, dd), s)
            s = V(lambda e: e.tensor_tensor(tt, tt, dd, ALU.mult), s)
            s = A(lambda e: e.activation(tt, tt, ACT.Sqrt), s)
            yield
            s = V(lambda e: e.tensor_tensor(tt, tt, ii, ALU.mult), s, s1)
            s = [V(lambda e: e.tensor_tensor_scan(dd[:, 128 * bl:128 * bl + 128], aa[:, 128 * bl:128 * bl + 128],
                                                  tt[:, 128 * bl:128 * bl + 128], hlast[:, bl:bl + 1] if t_ else 0.0,
                                                  ALU.mult, ALU.add), s, s_a, left["h"]) for bl in range(2)]
            if t_ == 0:
                left["h"] = V(lambda e: e.tensor_copy(hlast, b2(dd)[:, :, 127]), s)
            s_rnn = V(lambda e: e.tensor_tensor(mixT[:, 6:8, :].rearrange("p b t -> p (b t)"), dd, gr, ALU.mult), s, s_gr)
            yield

            units = []
            nk = 128 * (t_ + 1)
            for j in range(4):
                units.append(dict(
                    group=0, col=128 * j, t=t_, nk=nk, mask=mcau, counts=None, ready=[q_done, k_done, v_done, lr],
                    q=lambda h, j=j: qT[64 * h:64 * h + 64, j, :],
                    k=lambda h, j=j: kT[64 * h:64 * h + 64, j, 0:nk],
                    v=lambda h, c, j=j: v23[:, c, 128 * j + 64 * h:128 * j + 64 * h + 64],
                    bias=lambda h, j=j: (Lh[64 * h:64 * h + 40, j, :], R[64 * h:64 * h + 40, 0:nk])))
            w31 = vecs[:, lv + L_DW:lv + L_DW + 62].rearrange("p (b k) -> p b k", b=2)
            cd = [None, None]

            def convolve():
                for k in range(30, -1, -1):
                    for bl in range(2):
                        d, u = yc[:, 128 * bl:128 * bl + 128], ypad[:, bl, k + o:k + o + 128]
                        if k == 30:
                            cd[bl] = V(lambda e: e.tensor_scalar(d, u, w31[:, bl, 30:31], vecs[:, lv + L_DB + bl:lv + L_DB + bl + 1],
                                                                 ALU.mult, ALU.add), s_y, z1)
                        else:
                            cd[bl] = V(lambda e: e.scalar_tensor_tensor(d, u, w31[:, bl, k:k + 1], d, ALU.mult, ALU.add), cd[bl])
                    if k % 3 == 0:
                        yield

            att = yield from weave(attention(units, o_t.unsqueeze(1).to_broadcast([P, 2, 512]), [s_rnn, acts], room), convolve())

            b = bank[0]
            s = transposes(b, [o_t[:, 128 * i:128 * i + 128] for i in range(4)], att)
            s_o = A(lambda e: e.activation(mixT[:, 0:4, :], four(b), ACT.Copy), s)
            b.free = [s_o]

            b = bank[3]
            s = matmuls(b.ap[:, 0:128], [(ones, yc[:, 128 * bl:128 * bl + 128]) for bl in range(2)], cd, b.free)
            yield
            mean, var, rr, r2 = (junk[:, 128 * i:128 * i + 128] for i in range(4))
            twice = lambda ap: ap.unsqueeze(1).to_broadcast([P, 2, 128])
            s = V(lambda e: e.tensor_scalar(mean, b.ap[:, 0:128], 1.0 / 256, None, ALU.mult), s)
            b.free = [s]
            s_d = V(lambda e: e.tensor_tensor(b2(yc), b2(yc), twice(mean), ALU.subtract), s)
            sq3 = junk[:, 512:768]
            s = V(lambda e: e.tensor_tensor(sq3, yc, yc, ALU.mult), s_d)
            s = matmuls(b.ap[:, 0:128], [(ones, sq3[:, 128 * bl:128 * bl + 128]) for bl in range(2)], s)
            yield
            s = V(lambda e: e.tensor_scalar(var, b.ap[:, 0:128], 1.0 / 256, EPS, ALU.mult, ALU.add), s)
            b.free = [s]
            s = yield from inv_root_tile(var, rr, r2, s)
            s = V(lambda e: e.tensor_tensor(b2(yc), b2(yc), twice(rr), ALU.mult), s)
            s_conv = [A(lambda e: e.activation(mixT[:, 4 + bl, :], yc[:, 128 * bl:128 * bl + 128], ACT.Silu,
                                               bias=vecs[:, lv + L_B + bl:lv + L_B + bl + 1],
                                               scale=vecs[:, lv + L_G + bl:lv + L_G + bl + 1]), s) for bl in range(2)]
            yield
            mix_ready = [s_o, s_rnn, s_conv]
            added = []
            for c in range(2):
                b = bank[6 + c]
                s = yield from token_tile(b, mixT, mix_ready, ws)
                added.append(add_to_x(t_, c, b, s))
                b.free = [added[-1]]
                yield

            xn = row_y[t_]
            r, s = yield from rms_tile(t_, xn, added, left.get(("xn", t_)))
            s = V(lambda e: e.scalar_tensor_tensor(xn, x3[:, t_, :], r, rowg[:, :], ALU.mult, ALU.mult), s, landed_l["row"])
            left["row"] = s
            xn_done[(l, t_)] = s
            yield
            h_ready = yield from turn_tile(xn, None, bank[6:8], s, hTt)
            qpd = []
            for c in range(4):
                b = bank[c]
                s = yield from feature_tile(b, hTt, h_ready, ws)
                qpd.append(A(lambda e: e.activation(qp[:, 4 * c:4 * c + 4, :], four(b), ACT.Copy), s, att))
                b.free = [qpd[-1]]
            yield
            for hh in range(2):
                for a in range(2):
                    b = bank[2 * a + hh]
                    for h in range(4):
                        s = matmuls(b.ap[:, 128 * h:128 * h + 128],
                                    [(qp[:, 2 * (4 * hh + h) + a, :], kk4[:, a, 4 * hh + h, :])],
                                    landed_l["kk"], qpd, b.free if h == 0 else None)
                    b.scores = s
                    left["mixed"] = [s, qpd]
                    yield
            left["kk"] = s
            rests = [Buf(tmp[:, 1024 + 256 * i:1280 + 256 * i]) for i in range(4)]
            for b in rests:
                b.free = [s]
            turns = [0]

            def top16(rows_, after):
                use = []
                for _ in rows_:
                    use.append(rests[turns[0] % 4])
                    turns[0] += 1
                rr_ = [u.ap[:, 0:r[2].shape[-1]] for u, r in zip(use, rows_)]
                q1 = [V(lambda e: e.max(v[:, 0:8], src), after) for v, i, src in rows_]
                for (v, i, src), q in zip(rows_, q1):
                    V(lambda e: e.max_index(i[:, 0:8], v[:, 0:8], src), q)
                q3 = [V(lambda e: e.match_replace(r, v[:, 0:8], src, -3e38), q, u.free)
                      for (v, i, src), r, u, q in zip(rows_, rr_, use, q1)]
                q4 = [V(lambda e: e.max(v[:, 8:16], r), q) for (v, i, src), r, q in zip(rows_, rr_, q3)]
                q5 = [V(lambda e: e.max_index(i[:, 8:16], v[:, 8:16], r), q) for (v, i, src), r, q in zip(rows_, rr_, q4)]
                for u, q in zip(use, q5):
                    u.free = [q]
                return q3, q5

            q_e = [None, None]
            for hh in range(4):
                hs_ = slice(2 * hh, 2 * hh + 2)
                cand_ = cand[:, 512 * (hh % 2):512 * (hh % 2) + 512]
                c4 = cand_.rearrange("p (h i j) -> p h i j", h=2, i=16)
                oh = cand_.rearrange("p (h k j) -> p h k j", h=2, k=16)
                for a in range(2):
                    b = bank[2 * a + hh // 2]
                    c = 256 * (hh % 2)
                    q3, q5 = top16([(top[:, a, 2 * hh + i, :], topi[:, a, 2 * hh + i, :], b.ap[:, c + 128 * i:c + 128 * i + 128])
                                    for i in range(2)], b.scores)
                    yield
                    yield
                    b.free = q3
                s_tf = V(lambda e: e.tensor_copy(topf[:, :, hs_, :], topi[:, :, hs_, :]), q5)
                s1 = V(lambda e: e.tensor_tensor(c4, top[:, 0, hs_].unsqueeze(3).to_broadcast([P, 2, 16, 16]),
                                                 top[:, 1, hs_].unsqueeze(2).to_broadcast([P, 2, 16, 16]), ALU.add), q5, q_e[hh % 2])
                yield
                q3, q5 = top16([(best[:, 2 * hh + i, :], besti[:, 2 * hh + i, :], cand_[:, 256 * i:256 * i + 256])
                                for i in range(2)], s1)
                yield
                yield
                bi, hl = smi[:, 256 + 32 * hh:288 + 32 * hh], hilo[:, 32 * hh:32 * hh + 32]
                q = q5
                for a in range(2):
                    if a == 0:
                        q = V(lambda e: e.tensor_scalar(hl, bi, 4, None, ALU.logical_shift_right), q)
                    else:
                        q = V(lambda e: e.tensor_scalar(hl, bi, 15, None, ALU.bitwise_and), q)
                    q = V(lambda e: e.tensor_copy(hf[:, a, hs_].rearrange("p h k -> p (h k)"), hl), q)
                    q = V(lambda e: e.tensor_tensor(oh, hf[:, a, hs_].unsqueeze(3).to_broadcast([P, 2, 16, 16]),
                                                    iota.unsqueeze(1).unsqueeze(1).to_broadcast([P, 2, 16, 16]), ALU.is_equal), q)
                    yield
                    q = V(lambda e: e.tensor_tensor(oh, oh, topf[:, a, hs_].unsqueeze(2).to_broadcast([P, 2, 16, 16]), ALU.mult),
                          q, s_tf)
                    yield
                    q = q_e[hh % 2] = V(lambda e: e.tensor_reduce(ef[:, a, hs_], oh, AX, ALU.add), q)
                    yield
                e1, e2 = (junk[:, 512 + 128 * a + 32 * hh:544 + 128 * a + 32 * hh] for a in range(2))
                at = 128 * t_ + 32 * hh
                q = V(lambda e: e.tensor_scalar(e1, e1, 128.0, float(16384 * l), ALU.mult, ALU.add), q)
                routed[(l, t_, hh)] = V(lambda e: e.tensor_tensor(eidx[:, at:at + 32], e1, e2, ALU.add), q, left.get(("idx", t_)))
                gt = gate[t_][:, 32 * hh:32 * hh + 32]
                g3 = gt.rearrange("p (h k) -> p h k", h=2)
                gs = sm[:, 720 + 2 * hh:722 + 2 * hh]
                q = V(lambda e: e.tensor_tensor(g3, best[:, hs_], best[:, hs_, 0:1].to_broadcast([P, 2, 16]), ALU.subtract), q)
                q = A(lambda e: e.activation(gt, gt, ACT.Exp), q)
                yield
                q = V(lambda e: e.tensor_reduce(gs, g3, AX, ALU.add), q)
                q = V(lambda e: e.reciprocal(gs, gs), q)
                q = V(lambda e: e.tensor_tensor(g3, g3, gs.unsqueeze(2).to_broadcast([P, 2, 16]), ALU.mult), q)
                gated[(l, t_, hh)] = q
                yield
            left["mixer"] = [q, left["kk"], qpd]
            if (l, t_) == (0, 0):
                for i in range(6, ROWS):
                    slots[i].free = [q_e]
                    turns_at.appendleft(i)

        xn_done, gated, read = {}, {}, {}
        u_tab = T["peer_u"].rearrange("l e d -> (l e) d")
        v_tab = T["peer_v"].rearrange("l e d -> (l e) d")
        slots = [Buf(arena[:, 1024 * i:1024 * i + 1024]) for i in range(ROWS)]
        turns_at = deque(range(6))
        order = [(0, 0), (0, 1), (1, 0), (1, 1)]
        weighted = {}

        def gather(tab, l, t_, k):
            i = turns_at.popleft()
            turns_at.append(i)
            sl = slots[i]
            step = M.dma(row_landed[i], lambda e: e.indirect_dma_start(
                sl.ap, None, tab, bass.IndirectOffsetOnAxis(ap=eidx[:, 128 * t_ + k:128 * t_ + k + 1], axis=0)),
                sl.free, routed[(l, t_, k // 32)])
            return sl, step

        def up(n):
            (l, t_), k = order[n // 128], n % 128
            sl, here = gather(u_tab, l, t_, k)
            c = 128 * t_ + k
            s = V(lambda e: e.tensor_tensor_reduce(out=sl.ap, in0=sl.ap, in1=row_y[t_], scale=1.0, scalar=0.0, op0=ALU.mult,
                                                   op1=ALU.add, accum_out=hid[:, c:c + 1]), here, xn_done[(l, t_)])
            sl.free = [s]
            if k == 127:
                left[("xn", t_)] = s
            if k % G == G - 1:
                c = 128 * t_ + k + 1 - G
                w_ = wexp[:, c:c + G]
                s = A(lambda e: e.activation(w_, hid[:, c:c + G], ACT.Gelu_apprx_tanh), s, [read.get((t_, j)) for j in range(k + 1 - G, k + 1)])
                weighted[(l, t_, k // G)] = V(lambda e: e.tensor_tensor(w_, w_, gate[t_][:, k + 1 - G:k + 1], ALU.mult),
                                              s, gated[(l, t_, k // 32)])

        def on_vector(n):
            return n < 128 and n % 128 not in (0, 127) and n % SHARE[1] < SHARE[0]

        def weigh(n):
            (l, t_), k = order[n // 128], n % 128
            if on_vector(n):
                return
            dg, c = diags[n % 4], 128 * t_ + k
            dg.made = A(lambda e: e.activation(dg.ap, ident, ACT.Copy, scale=wexp[:, c:c + 1]), weighted[(l, t_, k // G)], dg.free)
            read[(t_, k)] = dg.made

        def down(n):
            (l, t_), k = order[n // 128], n % 128
            sl, here = gather(v_tab, l, t_, k)
            if k == 127:
                left[("idx", t_)] = here
            if on_vector(n):
                c = 128 * t_ + k
                s = V(lambda e: e.scalar_tensor_tensor(x3[:, t_, :], sl.ap, wexp[:, c:c + 1], x3[:, t_, :], ALU.mult, ALU.add),
                      here, weighted[(l, t_, k // G)], left["x"][t_])
                left["x"][t_] = [s]
                read[(t_, k)] = s
                sl.free = [s]
                return
            dg = diags[n % 4]
            s_dg = dg.made
            for half in range(2):
                b = bank[ADD[half]]
                s = E(lambda e: e.matmul(b.ap[:, :], dg.ap, sl.ap[:, 512 * half:512 * half + 512], start=(k == 0), stop=(k == 127)),
                      here, s_dg, b.free if k == 0 else None)
            dg.free = [s]
            sl.free = [s]
            if k == 127:
                done = []
                for half in range(2):
                    b = bank[ADD[half]]
                    q = add_to_x(t_, half, b, [s, left["x"][t_]])
                    b.free = [q]
                    done.append(q)
                left["x"][t_] = done

        stores = []
        l_out = landing("l_out")
        o3 = out.rearrange("(t p) d -> p t d", p=P)

        def finish(t_):
            if t_ == 0:
                landed_l["row"] = load(S, l_row, rowg[:, :], T["rows"][:, B_FIN:B_FIN + 1024], left["row"])
            y = row_y[t_]
            r, s = yield from rms_tile(t_, y, left["x"][t_], left[("xn", t_)])
            q = V(lambda e: e.scalar_tensor_tensor(y, x3[:, t_, :], r, rowg[:, :], ALU.mult, ALU.mult), s, landed_l["row"])
            stores.append(load(S, l_out, o3[:, t_, :], y, q))

        for _ in block1(0, Room(bank, range(8), (0, 6), (2,), (4,), scr, hT, tmp)):
            pass
        routing = mixer(0, 0, Room(bank, (0, 1, 2, 3, 0, 1, 2, 3), (0,), (2,), (3,), arena[:, 0:2816], arena[:, 3072:5120],
                                   arena[:, 5120:8192]))
        ahead = block1(1, Room(bank, (4, 5, 6, 7, 4, 5, 6, 7), (4,), (6,), (7,), scr, hT, tmp))
        credit = 0.0
        while (0, 0, 0) not in gated:
            if next(routing) is None:
                credit += RATIO[1] if "mixed" in left else RATIO[0]
            while credit > 0:
                credit -= next(ahead) or SIDE
        for b in slots[:6]:
            b.free = [left["mixed"]]
        later = Room(bank, (4, 5, 1, 3, 4, 5, 6, 7), (4, 6), (1,), (3,), scr, hT, tmp)

        def first_then_second():
            yield from routing
            yield from ahead
            yield from mixer(0, 1, later)

        pace = FIRST / (118.0 - LAG)
        todo = None
        credit = 0.0
        for n in range(512 + LAG):
            if n < 512:
                while (*order[n // 128], min(n % 128 + 4, 127) // 32) not in gated:
                    next(todo)
                up(n)
            if 0 <= n + AHEAD - LAG < 512:
                weigh(n + AHEAD - LAG)
            if n >= LAG:
                down(n - LAG)
            if n == 0:
                todo = first_then_second()
            if n in (128 + LAG, 256 + LAG, 384 + LAG):
                todo = chain(todo or (), mixer(*order[n // 128 + 1], later) if n < 384 else finish(0))
                pace = SECOND / (118.0 - LAG)
            credit += pace
            while todo and credit >= 1:
                cost = next(todo, "end")
                if cost == "end":
                    todo = None
                else:
                    credit -= cost or WAITS
            credit = min(credit, 1.0)
        for _ in todo or ():
            pass
        for _ in finish(1):
            pass
        S(lambda e: e.nop(), stores)

        for q in (S, A, V, E, M):
            q.number()
        block = ctx.enter_context(nc.Block())

        @block.sync
        def _(eng):
            S.emit(eng)

        @block.scalar
        def _(eng):
            A.emit(eng)

        @block.vector
        def _(eng):
            V.emit(eng)

        @block.tensor
        def _(eng):
            E.emit(eng)

        @block.gpsimd
        def _(eng):
            M.emit(eng)


def constants():
    c = np.zeros((P, K_END), np.float32)
    c[:, K_ID:K_ID + 128] = np.eye(P)
    i = np.arange(256)[:, None]
    j = np.arange(256)[None, :]
    causal = j <= i
    d = i - j
    counts = causal * ((d <= 128).astype(int) + (d % 4 == 0) + (d % 16 == 0))
    for at, m in ((K_MC, np.where(causal, 0.0, NEG)), (K_MD, np.where(counts > 0, 0.0, NEG)), (K_CD, counts)):
        c[:, at:at + 512] = m.reshape(2, P, 256).transpose(1, 0, 2).reshape(P, 512)
    c[:, K_ONE:K_ONE + 128] = 1.0
    c[:, K_IO:K_IO + 16] = np.arange(16)
    c[:, K_IF:K_IF + 32] = np.float32(10000.0) ** (-np.arange(32, dtype=np.float32) / np.float32(32))
    for h in range(8):
        at = 64 * (h % 2) + h
        c[at + 32, K_SEL + h // 2] = 8.0
        c[at, K_SEL + 5 + h // 2] = 1.0
    for at in (0, 64):
        c[at:at + 8, K_SEL + 4] = -8.0
        c[at + 32:at + 40, K_SEL + 9] = 1.0
    return c


def kernel(**inputs):
    import concourse.bacc as _bacc
    from concourse.bass_utils import run_bass_kernel_spmd as _run

    a = {k: np.asarray(v) for k, v in inputs.items()}

    def col(v):
        return v.reshape(-1, P).T

    def pad(v, n):
        out = np.zeros((P, n), v.dtype)
        out[:v.shape[0]] = v.reshape(v.shape[0], -1)
        return out

    def forget(v):
        out = np.zeros(v.shape[:-1] + (104,), v.dtype)
        for at in (0, 32, 64, 96):
            out[..., at:at + 8] = v
        return out

    parts = [col(a["mix_norm_g"][0]), col(a["mem_norm_g"][0]), col(a["ffn_norm_g"][0]),
             col(a["norm1_g_2"][0]), col(a["norm1_g_2"][1]),
             a["ffn_conv_w"][0].reshape(3, 44, P).transpose(2, 1, 0).reshape(P, 132), col(a["ffn_conv_b"][0])]
    for l in range(2):
        parts += [a["conv_dw_w_2"][l].reshape(31, 2, P).transpose(2, 1, 0).reshape(P, 62), col(a["conv_dw_b_2"][l]),
                  col(a["conv_ln_g_2"][l]), col(a["conv_ln_b_2"][l]),
                  a["rg_conv_w_2"][l].reshape(4, 2, P).transpose(2, 1, 0).reshape(P, 8), col(a["rg_conv_b_2"][l]),
                  col(a["rg_b_r_2"][l]), col(a["rg_b_i_2"][l]), col(a["rg_lambda_2"][l]),
                  pad(forget(a["b_forget_2"][l]), 1)]
    vecs = np.concatenate(parts, axis=1)
    row = np.concatenate([a[n][0] for n in ("moba_q_norm_g", "moba_k_norm_g", "dil_q_norm_g", "dil_k_norm_g",
                                            "mem_q_norm_g", "mem_k_norm_g")]
                         + [a["norm2_g_2"][0], a["norm2_g_2"][1], a["final_g_2"]])
    keys = np.stack([a["peer_k1_2"], a["peer_k2_2"]], axis=1).transpose(0, 4, 1, 2, 3).reshape(2, P, 2048)
    rg = np.zeros((2, 2, 2, P, P), np.float32)
    for g, n in enumerate(("rg_w_r_2", "rg_w_i_2")):
        for h in range(4):
            o = 64 * (h % 2)
            rg[:, g, h // 2, o:o + 64, o:o + 64] = a[n][:, h]
    rgw = rg.transpose(0, 3, 1, 2, 4).reshape(2, P, 512)
    wf = forget(a["w_in_2"][:, :, 1536:1544]).reshape(2, 8, P, 104).transpose(0, 2, 1, 3).reshape(2, P, 832)
    arrays = {
        "x": a["x"][0], "mem": a["mem"][0], "pos": a["positions"][0].reshape(2, P).T,
        "const": constants(), "vecs": vecs, "rows": np.broadcast_to(row, (P, row.size)),
        "keys": keys, "rgw": rgw, "wf": wf,
        "w_in": a["w_in"][0], "w_mem_kv": a["w_mem_kv"][0], "w_branch_moba": a["w_branch_moba"][0],
        "w_branch_dil": a["w_branch_dil"][0], "w_branch_mem": a["w_branch_mem"][0], "w_out": a["w_out"][0],
        "w_ffn_up": a["w_ffn_up"][0], "w_ffn_down": a["w_ffn_down"][0],
        "w_in_2": a["w_in_2"], "w_out_2": a["w_out_2"], "peer_wq": a["peer_wq_2"],
        "peer_u": a["peer_u_2"], "peer_v": a["peer_v_2"],
    }
    nc = _bacc.Bacc("TRN2", target_bir_lowering=False, num_devices=1)
    feeds, T = {}, {}
    for name, v in arrays.items():
        v = np.ascontiguousarray(v)
        feeds[f"in_{name}_dram"] = v
        T[name] = nc.dram_tensor(f"in_{name}_dram", v.shape, mybir.dt.from_np(v.dtype), kind="ExternalInput").ap()
    out = nc.dram_tensor("out_0_dram", (256, 1024), F32, kind="ExternalOutput").ap()
    program(nc, T, out)
    r = _run(nc, [feeds], core_ids=[0])
    return r.results[0]["out_0_dram"].reshape(1, 256, 1024)
```
